# Optimizing a Trainium2 kernel written in Bass

```python
import jax, jax.numpy as jnp
from jax import lax
import numpy as np

D_MODEL = 1024
BATCH = 1
SEQ = 2048
DEPTH = 1
DEC_BATCH = 8
DEC_SEQ = 1
PAST_LEN = 4096
PAGE_SIZE = 128

GLA_HEADS = 4
GLA_DV = D_MODEL // 2 // GLA_HEADS
GLA_DK = GLA_DV // 2
GLA_WIDTH = GLA_HEADS * GLA_DV
GLA_KWIDTH = GLA_HEADS * GLA_DK
GLA_RANK = 16
GLA_TAU = 16.0
GLA_CHUNK = 64
SWA_HEADS = 8
SWA_HD = 64
SWA_KV_HEADS = 2
SWA_GROUP = SWA_HEADS // SWA_KV_HEADS
SWA_WIDTH = SWA_HEADS * SWA_HD
SWA_KVWIDTH = SWA_KV_HEADS * SWA_HD
WINDOW = 128
MIX_WIDTH = GLA_WIDTH + SWA_WIDTH
EPS = 1e-6
NEG_INF = -1e30
SPLITS = (GLA_KWIDTH, GLA_KWIDTH, GLA_WIDTH, GLA_WIDTH, GLA_RANK,
          SWA_WIDTH, SWA_KVWIDTH, SWA_KVWIDTH, SWA_WIDTH)
IN_WIDTH = sum(SPLITS)
SPLIT_POINTS = [int(o) for o in np.cumsum(SPLITS)[:-1]]

kernel_name = "hymba_gla_swa_sink_step"

def _rmsnorm(x, g):
    xf = x.astype(jnp.float32)
    y = xf * lax.rsqrt(jnp.mean(xf * xf, axis=-1, keepdims=True) + EPS) * g.astype(jnp.float32)
    return y.astype(x.dtype)

def _project(h, w_in, w_gate_up, b_gate):
    B, L, _ = h.shape
    proj = jnp.einsum('bld,de->ble', h, w_in)
    gq, gk, gv, g_gate, g_low, sq, sk, sv, s_gate = jnp.split(proj, SPLIT_POINTS, axis=-1)
    z = jnp.einsum('blr,rk->blk', g_low, w_gate_up) + b_gate
    log_a = jax.nn.log_sigmoid(z.astype(jnp.float32)) / GLA_TAU
    heads = lambda t, d: t.reshape(B, L, GLA_HEADS, d)
    gla = (heads(gq, GLA_DK), heads(gk, GLA_DK), heads(gv, GLA_DV), heads(log_a, GLA_DK))
    return gla, g_gate, (sq, sk, sv), s_gate

def _gla_scan(q, k, v, log_a, s0):
    B, L = q.shape[:2]
    c = min(GLA_CHUNK, L)
    n = -(-L // c)
    pad = n * c - L

    def prep(t):
        t = jnp.pad(t.astype(jnp.float32), ((0, 0), (0, pad), (0, 0), (0, 0)))
        return t.reshape(B, n, c, GLA_HEADS, t.shape[-1]).transpose(1, 0, 3, 2, 4)

    qs, ks, vs, gs = prep(q * (GLA_DK ** -0.5)), prep(k), prep(v), prep(log_a)
    tri = jnp.tril(jnp.ones((c, c), dtype=bool))[:, :, None]

    def step(S, inp):
        qc, kc, vc, gc = inp
        b = jnp.cumsum(gc, axis=-2)
        o_inter = jnp.einsum('bhid,bhde->bhie', qc * jnp.exp(b), S)
        diff = b[..., :, None, :] - b[..., None, :, :]
        decay = jnp.where(tri, jnp.exp(jnp.where(tri, diff, 0.0)), 0.0)
        attn = jnp.einsum('bhid,bhjd,bhijd->bhij', qc, kc, decay)
        o = o_inter + jnp.einsum('bhij,bhje->bhie', attn, vc)
        b_last = b[..., -1:, :]
        S = jnp.exp(b_last[..., 0, :])[..., None] * S + \
            jnp.einsum('bhjd,bhje->bhde', kc * jnp.exp(b_last - b), vc)
        return S, o

    S, o = lax.scan(step, s0.astype(jnp.float32), (qs, ks, vs, gs))
    o = o.transpose(1, 0, 3, 2, 4).reshape(B, n * c, GLA_HEADS, GLA_DV)[:, :L]
    return o, S

def _gla_branch(q, k, v, log_a, s0, gla_norm):
    B, L = q.shape[:2]
    o, S = _gla_scan(q, k, v, log_a, s0)
    o = _rmsnorm(o, gla_norm)
    return o.reshape(B, L, GLA_WIDTH), S

def _sink_attn(q, k, v, valid, sinks):
    s = jnp.einsum('...qkgd,...skd->...kgqs', q, k).astype(jnp.float32) * (SWA_HD ** -0.5)
    s = jnp.where(valid, s, NEG_INF)
    sink = jnp.broadcast_to(sinks.astype(jnp.float32).reshape(SWA_KV_HEADS, SWA_GROUP, 1, 1),
                            s.shape[:-1] + (1,))
    p = jax.nn.softmax(jnp.concatenate([s, sink], axis=-1), axis=-1)[..., :-1]
    return jnp.einsum('...kgqs,...skd->...qkgd', p.astype(v.dtype), v)

def _swa_prompt(sq, sk, sv, sinks):
    B, L, _ = sq.shape
    nb = L // WINDOW
    q = sq.reshape(B, nb, WINDOW, SWA_KV_HEADS, SWA_GROUP, SWA_HD)
    k = sk.reshape(B, nb, WINDOW, SWA_KV_HEADS, SWA_HD)
    v = sv.reshape(B, nb, WINDOW, SWA_KV_HEADS, SWA_HD)
    shift = lambda t: jnp.pad(t, ((0, 0), (1, 0), (0, 0), (0, 0), (0, 0)))[:, :-1]
    kk = jnp.concatenate([shift(k), k], axis=2)
    vv = jnp.concatenate([shift(v), v], axis=2)
    qi = jnp.arange(WINDOW)[:, None]
    sj = jnp.arange(2 * WINDOW)[None, :]
    d = qi + WINDOW - sj
    band = (d >= 0) & (d < WINDOW)
    has_prev = (jnp.arange(nb) > 0)[:, None, None] | (sj >= WINDOW)[None]
    valid = (band[None] & has_prev)[:, None, None]
    o = _sink_attn(q, kk, vv, valid, sinks)
    new_k = sk.reshape(B, L, SWA_KV_HEADS, SWA_HD)[:, L - WINDOW:]
    new_v = sv.reshape(B, L, SWA_KV_HEADS, SWA_HD)[:, L - WINDOW:]
    return o.reshape(B, L, SWA_WIDTH), new_k, new_v

def _swa_sample(sq, sk, sv, k_buf, v_buf, sinks):
    DB, L, _ = sq.shape
    wb = k_buf.shape[1]
    q = sq.reshape(DB, L, SWA_KV_HEADS, SWA_GROUP, SWA_HD)
    kk = jnp.concatenate([k_buf.astype(sk.dtype), sk.reshape(DB, L, SWA_KV_HEADS, SWA_HD)], axis=1)
    vv = jnp.concatenate([v_buf.astype(sv.dtype), sv.reshape(DB, L, SWA_KV_HEADS, SWA_HD)], axis=1)
    rel_k = jnp.concatenate([jnp.arange(wb) - wb, jnp.arange(L)])
    d = jnp.arange(L)[:, None] - rel_k[None, :]
    valid = (d >= 0) & (d < WINDOW)
    o = _sink_attn(q, kk, vv, valid, sinks)
    return o.reshape(DB, L, SWA_WIDTH), kk[:, -wb:], vv[:, -wb:]

def _merge(o_gla, g_gate, o_swa, s_gate, w_out):
    dt = g_gate.dtype
    u = jnp.concatenate([o_gla.astype(dt) * jax.nn.silu(g_gate),
                         o_swa.astype(dt) * jax.nn.silu(s_gate)], axis=-1)
    return jnp.einsum('ble,ed->bld', u, w_out)

def _layer(h, s0, swa_fn, norm_g, w_in, w_gate_up, b_gate, gla_norm, w_out):
    u = _rmsnorm(h, norm_g)
    gla, g_gate, (sq, sk, sv), s_gate = _project(u, w_in, w_gate_up, b_gate)
    o_gla, S = _gla_branch(*gla, s0, gla_norm)
    o_swa, k_new, v_new = swa_fn(sq, sk, sv)
    h = h + _merge(o_gla, g_gate, o_swa, s_gate, w_out)
    return h, S, k_new, v_new

def setup_inputs(seed: int = 0) -> dict:
    key = jax.random.key(seed)
    ks = jax.random.split(key, 16)
    w_buf = min(WINDOW, PAST_LEN)
    f32 = jnp.float32
    return {
        "x_prompt": jax.random.normal(ks[0], (BATCH, SEQ, D_MODEL), f32),
        "x_sample": jax.random.normal(ks[1], (DEC_BATCH, DEC_SEQ, D_MODEL), f32),
        "state_gla": 0.5 * jax.random.normal(ks[2], (DEPTH, DEC_BATCH, GLA_HEADS, GLA_DK, GLA_DV), f32),
        "cache_win_k": jax.random.normal(ks[3], (DEPTH, DEC_BATCH, w_buf, SWA_KV_HEADS, SWA_HD), f32),
        "cache_win_v": jax.random.normal(ks[4], (DEPTH, DEC_BATCH, w_buf, SWA_KV_HEADS, SWA_HD), f32),
        "norm_in": 1.0 + 0.01 * jax.random.normal(ks[5], (DEPTH, D_MODEL), f32),
        "w_in": jax.random.normal(ks[6], (DEPTH, D_MODEL, IN_WIDTH), f32) * D_MODEL ** -0.5,
        "w_gate_up": jax.random.normal(ks[7], (DEPTH, GLA_RANK, GLA_KWIDTH), f32) * GLA_RANK ** -0.5,
        "b_gate": 0.1 * jax.random.normal(ks[8], (DEPTH, GLA_KWIDTH), f32),
        "gla_norm": 1.0 + 0.01 * jax.random.normal(ks[9], (DEPTH, GLA_DV), f32),
        "attn_sinks": 0.5 * jax.random.normal(ks[10], (DEPTH, SWA_HEADS), f32),
        "w_out": jax.random.normal(ks[11], (DEPTH, MIX_WIDTH, D_MODEL), f32) * MIX_WIDTH ** -0.5,
        "norm_f": 1.0 + 0.01 * jax.random.normal(ks[12], (D_MODEL,), f32),
    }

def reference(x_prompt, x_sample, state_gla, cache_win_k, cache_win_v, norm_in, w_in,
              w_gate_up, b_gate, gla_norm, attn_sinks, w_out, norm_f):
    hp, hs = x_prompt, x_sample
    sp_l, kp_l, vp_l, ss_l, ks_l, vs_l = [], [], [], [], [], []
    for l in range(DEPTH):
        params = (norm_in[l], w_in[l], w_gate_up[l], b_gate[l], gla_norm[l], w_out[l])
        sinks = attn_sinks[l]
        s0 = jnp.zeros((hp.shape[0], GLA_HEADS, GLA_DK, GLA_DV), jnp.float32)
        hp, S_p, k_p, v_p = _layer(hp, s0, lambda q, k, v: _swa_prompt(q, k, v, sinks), *params)
        kb, vb = cache_win_k[l], cache_win_v[l]
        hs, S_s, k_s, v_s = _layer(hs, state_gla[l],
                                   lambda q, k, v: _swa_sample(q, k, v, kb, vb, sinks), *params)
        sp_l.append(S_p.astype(state_gla.dtype)); kp_l.append(k_p); vp_l.append(v_p)
        ss_l.append(S_s.astype(state_gla.dtype)); ks_l.append(k_s); vs_l.append(v_s)
    y_prompt = _rmsnorm(hp, norm_f)
    y_sample = _rmsnorm(hs, norm_f)
    return (y_prompt, y_sample,
            jnp.stack(sp_l), jnp.stack(kp_l), jnp.stack(vp_l),
            jnp.stack(ss_l), jnp.stack(ks_l), jnp.stack(vs_l))


_drawn_inputs = setup_inputs


def setup_inputs(seed=0):
    import zlib

    import numpy as np

    out = dict(_drawn_inputs(seed))
    spreads = {}
    factors = {'norm_in': 3.645, 'gla_norm': 40.334, 'attn_sinks': 64.0, 'norm_f': 33.31}
    for name, (base, spread) in spreads.items():
        noise = np.random.default_rng([zlib.crc32(name.encode()), seed]).standard_normal(out[name].shape)
        drawn = base * np.exp(spread * noise) if base else spread * noise
        out[name] = __import__('jax').numpy.asarray(drawn.astype(out[name].dtype))
    for name, factor in factors.items():
        out[name] = (out[name] * factor).astype(out[name].dtype)
    return out
```

```python
from contextlib import ExitStack

import concourse.bass as bass
from concourse import mybir

F32 = mybir.dt.float32
F16 = mybir.dt.float16
BF16 = mybir.dt.bfloat16
I32 = mybir.dt.int32
ALU = mybir.AluOpType
ACT = mybir.ActivationFunctionType
AX = mybir.AxisListType

P = 128
D = 1024
DT = D // P
SEQ = 2048
NT = SEQ // P
NS = 8
EPS = 1e-6
TAU = 16.0
HG, DK, DV = 4, 64, 128
FT = HG * DK // P
KVH, GRP, HD = 2, 4, 64
RANK = 16
GROUPS = [("gqk", 512), ("sq", 512), ("sklow", 272), ("gv", 512), ("gg", 512), ("sg", 512)]
COL = {}
_c = 0
for _name, _n in GROUPS:
    COL[_name] = _c
    _c += _n
IN_W = _c
OUT_GROUPS = 2
NG = len(GROUPS) + OUT_GROUPS
LEVELS = (64, 32, 16, 8)
LEAF = 8
LEAF_FLOOR = -20.0
U_SCALE = float(2 ** 10)
W_TOP = float(2 ** 14)
O_TOP = float(2 ** 14)
S_LEVEL, S_STATE, S_LEAFK, S_INTER, S_LEAFQ = 0, 4, 5, 6, 7


class Tile:

    def __init__(self, off, j=None):
        self.off, self.j = off, j
        self.p = off % 2

    @property
    def n(self):
        return self.off if self.j is None else self.j * 2 + self.off

    def __add__(self, d):
        return Tile(self.off + d, self.j)

    @property
    def static(self):
        return self.j is None

    @property
    def tokens(self):
        return NS if self.static and self.off == NT else P

    @property
    def sample(self):
        return self.static and self.off == NT


class Events:

    def __init__(self, sem, names):
        self.sem, self.names = sem, names

    def at(self, name, t):
        return t.n * len(self.names) + (self.names.index(name) + 1)

    def wait(self, eng, name, t):
        if not (t.static and t.off < 0):
            eng.wait_ge(self.sem, self.at(name, t))


class Ring:

    def __init__(self, banks, full, freed, order, tail=None):
        self.banks, self.full, self.freed, self.order = banks, full, freed, order
        self.tail = order if tail is None else tail

    def _list(self, t):
        return self.tail if t.sample else self.order

    def _index(self, name, t):
        return [u for u, _ in self._list(t)].index(name)

    def bank(self, name, t):
        return self.banks[(len(self.order) * t.p + self._index(name, t)) % 2]

    def wait_full(self, eng, name, t):
        eng.wait_ge(self.full, t.n * len(self.order) + (self._index(name, t) + 1))

    def wait_freed(self, eng, name, t):
        who = dict(self._list(t))[name]
        total = sum(1 for _, w in self.order if w == who)
        rank = [u for u, w in self._list(t) if w == who].index(name) + 1
        eng.wait_ge(self.freed[who], t.n * total + rank)

    def wait_free(self, eng, name, t):
        i = self._index(name, t)
        if i >= 2:
            self.wait_freed(eng, self._list(t)[i - 2][0], t)
        elif not (t.static and t.off == 0):
            self.wait_freed(eng, self.order[len(self.order) + i - 2][0], t + -1)


def bcast(ap, axis, n):
    ap = ap.unsqueeze(axis)
    shape = list(ap.shape)
    shape[axis] = n
    return ap.broadcast_to(shape)


def hymba_step_kernel(nc, xT_d, xq_d, xsT_d, xs_d, w_d, gin_d, gout_d, wgu_d, bg_d, sink_d, normf_d,
                      state_d, kcT_d, vc_d, sinks_s_d, ident_d, tri_d, lvl_d, leafscan_d, band_d,
                      y_d, ys_d, Sp_d, kp_d, vp_d, Ss_d, ksT_d, vs_d):
    with ExitStack() as ctx:
        def sb(name, shape, dt=F32):
            return ctx.enter_context(nc.sbuf_tensor(name, shape, dt))

        def sem(name):
            return ctx.enter_context(nc.semaphore(name))

        w_region = sb("w_in_hi_lo", [P, DT * IN_W])
        w_half = w_region[:, :].bitcast(F16).rearrange("p (s d c) -> p s d c", s=2, d=DT)
        w_hi, w_lo = w_half[:, 0], w_half[:, 1]
        wo_hi = sb("w_out_hi", [P, DT, D], F16)
        wo_lo = sb("w_out_lo", [P, DT, D], F16)
        xT = sb("xT", [P, DT, P])
        u_hi = sb("u_hi", [P, 2, DT, P], F16)
        u_lo = sb("u_lo", [P, 2, DT, P], F16)
        xq = sb("x_rows", [P, D])
        gq = sb("gla_q", [P, 2, FT, P])
        gk = sb("gla_k", [P, 2, FT, P])
        gv = sb("gla_v", [P, 2, HG * DV])
        sq = sb("win_q", [P, 2, GRP, P])
        kwin = sb("win_k", [P, 2, KVH, 2 * P])
        vwin = sb("win_v", [P, 2, 2, P])
        glow = sb("g_low", [P, 2, RANK])
        S_bd = sb("gla_state", [P, FT, 2, DV])
        normf = sb("norm_f", [P, D])
        flex = sb("flex", [P, 8192])
        stage = [flex[:, 4096 * s:4096 * s + 4096] for s in range(2)]
        at = [0]

        def part(n):
            at[0] += n
            return flex[:, at[0] - n:at[0]]

        gates = part(D)
        xres = part(D)
        EX = part(8 * FT * P).rearrange("p (s f c) -> p s f c", s=8, f=FT)
        QE = part(4 * FT * P).rearrange("p (l f h c) -> p l f h c", l=4, f=FT, h=2)
        QL = part(2 * FT * P).rearrange("p (f h c) -> p f h c", f=FT, h=2)
        AT = part(HG * P).rearrange("p (h c) -> p h c", h=HG)
        PR = part(2 * 2 * 2 * P).rearrange("p (s h c) -> p s h c", s=2, h=2)
        PT = part(2 * 2 * P).rearrange("p (h k c) -> p h k c", h=2, k=2)
        KST = part(HG * DK)
        bsum = part(FT * P).rearrange("p (f c) -> p f c", f=FT)
        assert at[0] <= 8192
        lsum = sb("decay_sum_leaf", [P, FT, P])
        ogT_hi = sb("ogT_hi", [P, DT, P], F16)
        ogT_lo = sb("ogT_lo", [P, DT, P], F16)
        junk = sb("junk", [P, D], BF16)
        glT = sb("g_lowT", [RANK, P])
        ident = sb("ident", [P, P])
        ident_b = sb("ident_bf16", [P, P], BF16)
        band = sb("band_bf16", [P, 2, 2 * P], BF16)
        leafmask = sb("leaf_mask", [P, P])
        lvlmask = sb("level_mask", [P, 4, DK])
        leafscan = sb("leaf_scan", [P, 2, P])
        diag = sb("rstd_diag", [P, P])
        gin = sb("norm_in", [P, DT])
        gout = sb("gla_norm", [P, DT])
        wgu = sb("w_gate_up", [RANK, HG * DK])
        bg = sb("b_gate", [P, FT])
        sink = sb("sinks", [P, 8])
        nsink = sb("neg_sinks", [P, 8])
        wabs = sb("w_abs", [P, 2, DT])
        wcol = sb("w_col", [P, 4])
        gs = sb("w_scale", [P, 2, DT])
        inv = sb("inv_scale", [P, NG])
        invq = sb("inv_scale_q", [P, 2])
        ones = sb("ones", [P, 1])
        xst = sb("x_stat", [P, 2, 8])
        ost = sb("o_stat", [P, 8, HG])
        hst = sb("h_stat", [P, 8])
        wst = sb("win_stat", [P, 6, 8])
        amax = sb("row_max", [P, 4])
        isc = sb("row_unscale", [P, 2])
        dec = sb("chunk_decay", [P, FT])

        banks = [ctx.enter_context(nc.psum_tensor(f"bank{i}", [P, 512], F32)) for i in range(8)]
        accS, accG = banks[6], banks[7]

        const_in = sem("const_in")
        w_in_sem = [sem("w_staged_0"), sem("w_staged_1")]
        xT_in = sem("xT_in")
        xq_in = sem("xq_in")
        xres_in = sem("xres_in")
        y_out = sem("y_out")
        tail_out = sem("tail_out")
        tail_in = sem("tail_in")
        w_row = sem("w_rowmax_done")
        w_max = sem("w_max_done")
        w_scaled = sem("w_scale_done")
        w_dve = sem("w_dve_steps")
        w_hi_done = sem("w_hi_done")
        w_lo_done = sem("w_lo_done")
        init = sem("init_done")
        pj = Ring(banks[0:2], sem("proj_full"), {"act": sem("proj_freed_act"), "dve": sem("proj_freed_dve")},
                  [("bc", "dve"), ("gqk", "act"), ("sq", "act"), ("sklow", "dve"), ("gv", "dve"),
                   ("gg", "act"), ("sg", "act")])
        at_ring = Ring(banks[2:4], sem("attn_full"), {"act": sem("attn_freed_act"), "dve": sem("attn_freed_dve")},
                       [("s0", "act"), ("s1", "act"), ("s2", "act"), ("s3", "act"),
                        ("L3", "dve"), ("L1", "dve"), ("L2", "dve"), ("y0", "dve"), ("y1", "dve")],
                       [("y0", "dve"), ("y1", "dve")])
        tr = Ring(banks[4:6], sem("turn_full"), {"act": sem("turn_freed_act"), "dve": sem("turn_freed_dve")},
                  [("glT", "act"), ("z", "dve"), ("pt0", "dve"), ("pt1", "act"), ("pt2", "dve"), ("pt3", "act"),
                   ("KST", "act"), ("SU", "dve"), ("og0", "dve"), ("og1", "dve")],
                  [("og0", "dve"), ("og1", "dve")])
        act_u = Events(sem("act_norm"), ["ssq", "ln", "exp", "hi"])
        dve_u = Events(sem("dve_norm"), ["ms", "n0", "n1", "rstd", "diag", "lo"])
        act_g = Events(sem("act_gla"), ["az", "ez", "l1", "E"])
        dve_g = Events(sem("dve_gla"), ["mz", "la", "lc", "scan", "Q", "QF", "L16"])
        pool_g = Events(sem("pool_gla"), ["D"])
        pool_w = Events(sem("pool_win"), ["gs"])
        win_kept = Events(sem("window_kept"), ["win"])
        dve_w = Events(sem("dve_win"), ["mx0", "nm0", "mx1", "nm1", "mx2", "nm2", "mx3", "nm3", "esi", "den", "rden"])
        act_w = Events(sem("act_win"), ["es"])
        pe_pv = Events(sem("pe_pv"), ["pv0", "pv1", "pv2", "pv3"])
        pe_o = Events(sem("pe_gla_out"), ["o"])
        dve_o = Events(sem("dve_out"), ["sg", "oms", "on0", "on1", "orstd", "gg", "am", "amc", "rsc", "gsc", "isc",
                                        "hms", "hn0", "hn1", "hr", "y"])
        act_o = Events(sem("act_out"), ["oss", "oln", "oexp", "hi0", "hi1", "hss", "hln", "hexp"])
        smp = {e: sem(f"sample_{e}") for e in ("act", "dve", "pe", "pool")}

        w_at = [0]

        def wpart(n):
            w_at[0] += n
            return w_region[:, w_at[0] - n:w_at[0]]

        s_state = wpart(NS * FT * DV).rearrange("p (b f c) -> p b f c", b=NS, f=FT)
        s_kT = wpart(NS * P).rearrange("p (b c) -> p b c", b=NS)
        s_v = wpart(NS * P).rearrange("p (b c) -> p b c", b=NS)
        s_km = wpart(NS * HG * DK).rearrange("p (b c) -> p b c", b=NS)[0:NS]
        s_kt = wpart(HG * DK)[0:NS]
        s_qm = wpart(HG * NS * NS).rearrange("p (f h b c) -> p f h b c", f=FT, h=2, b=NS)
        s_z = wpart(6 * FT * NS).rearrange("p (s f b) -> p s f b", s=6, f=FT)
        s_qs = wpart(NS * 8).rearrange("p (b h) -> p b h", b=NS)
        s_p = wpart(NS * P).rearrange("p (b c) -> p b c", b=NS)[0:8]
        s_st = wpart(8 * NS).rearrange("p (s b) -> p s b", s=8)[0:8]
        s_pT = wpart(NS * 8).rearrange("p (b h) -> p b h", b=NS)
        s_oT = wpart(GRP * NS).rearrange("p (f b) -> p f b", f=GRP)
        s_sink = sb("sample_sinks", [8, 2])
        s_knew = sb("sample_k_new", [P, NS])
        s_vnew_t = sb("sample_v_new", [NS, P])
        s_vnew = s_vnew_t[:, :]
        SV = {}
        for eng, names in (("act", ["glT", "az", "ez", "l1", "a", "exp"]),
                           ("dve", ["zb", "mz", "la", "kt", "km", "qz", "qm", "kT", "qsz", "qs", "st0", "st1", "st2",
                                    "state", "mx", "nm", "sub", "esi", "sum", "den", "rden", "pn", "pT", "oT"]),
                           ("pe", ["glT", "z", "kt", "kv0", "kv1", "kv2", "kv3", "o", "sc", "pT", "pv", "oT"])):
            for i, name in enumerate(names):
                SV[f"{eng}_{name}"] = i + 1

        def after(eng, step):
            eng.wait_ge(smp[step.split("_")[0]], SV[step])

        def w_slice(g, w_in, w_out):
            if g < len(GROUPS):
                return w_in[:, :, COL[GROUPS[g][0]]:COL[GROUPS[g][0]] + GROUPS[g][1]]
            c = (g - len(GROUPS)) * D // OUT_GROUPS
            return w_out[:, :, c:c + D // OUT_GROUPS]

        block = ctx.enter_context(nc.Block())

        def iterations(eng, body):
            body(Tile(0))
            with eng.Fori(0, (NT - 4) // 2) as j:
                body(Tile(1, j))
                body(Tile(2, j))
            for n in range(NT - 3, NT):
                body(Tile(n))

        @block.sync
        def _(sp):
            def load_x(t):
                n = t.tokens
                if not (t.static and t.off < 1):
                    dve_u.wait(sp, "lo", t + -1)
                if t.sample:
                    sp.dma_start(xT[:, :, 0:n], xsT_d).then_inc(xT_in, 16)
                else:
                    sp.dma_start(xT[:, :, :], xT_d[bass.ds(t.n, 1)].rearrange("a p d c -> (a p) d c")
                                 ).then_inc(xT_in, 16)
                if not (t.static and t.off < 1):
                    act_u.wait(sp, "ssq", t + -1)
                src = xs_d if t.sample else xq_d[bass.ds(t.n, 1)].rearrange("a p c -> (a p) c")
                sp.dma_start(xq[0:n, :], src).then_inc(xq_in, 16)

            def load_w(g):
                n = GROUPS[g][1] if g < len(GROUPS) else D // OUT_GROUPS
                off = DT * (COL[GROUPS[g][0]] if g < len(GROUPS) else IN_W + (g - len(GROUPS)) * D // OUT_GROUPS)
                if g >= 2:
                    sp.wait_ge(w_lo_done, g - 1)
                sp.dma_start(stage[g % 2][:, 0:DT * n], w_d[:, off:off + DT * n]).then_inc(w_in_sem[g % 2], 16)

            load_w(0)
            for dst, src in ((gin[:, :], gin_d), (gout[:, :], gout_d), (ident[:, :], ident_d)):
                sp.dma_start(dst, src).then_inc(const_in, 16)
            load_w(1)
            load_x(Tile(0))
            for dst, src in ((wgu[:, :], wgu_d), (bg[:, :], bg_d), (sink[:, :], sink_d), (normf[:, :], normf_d),
                             (leafmask[:, :], tri_d), (lvlmask[:, :, :], lvl_d), (leafscan[:, :, :], leafscan_d),
                             (band[:, :, :], band_d), (s_sink[:, 0:1], sinks_s_d)):
                sp.dma_start(dst, src).then_inc(const_in, 16)
            load_x(Tile(1))
            for g in range(2, NG):
                load_w(g)
            sp.wait_ge(w_lo_done, NG)
            sp.wait_ge(w_hi_done, NG)

            def body(t):
                n = t.tokens
                if not (t.static and t.off == 0):
                    sp.wait_ge(y_out, t.n * 16)
                sp.dma_start(xres, xq_d[bass.ds(t.n, 1)].rearrange("a p c -> (a p) c")).then_inc(xres_in, 16)
                if not (t.static and t.off + 2 > NT):
                    load_x(t + 2)
                dve_o.wait(sp, "y", t)
                sp.dma_start(y_d[bass.ds(t.n, 1)].rearrange("a p c -> (a p) c"), xres).then_inc(y_out, 16)

            iterations(sp, body)
            last = Tile(NT)
            sp.wait_ge(y_out, NT * 16)
            sp.dma_start(xres[0:NS, :], xs_d).then_inc(xres_in, 16)
            pj.wait_full(sp, "sg", last)
            sp.dma_start(s_state, state_d).then_inc(tail_in, 16)
            sp.dma_start(s_kT, kcT_d).then_inc(tail_in, 16)
            sp.dma_start(s_v[0:P - 1], vc_d).then_inc(tail_in, 16)
            pj.wait_freed(sp, "sklow", last)
            sp.dma_start(s_v[P - 1:P], s_vnew).then_inc(tail_in, 16)
            tr.wait_freed(sp, "SU", Tile(NT - 1))
            for h in range(HG):
                r, f = DK * (h % 2), h // 2
                sp.dma_start(Sp_d[h], S_bd[r:r + DK, f, h % 2, :]).then_inc(tail_out, 16)
            for kv in range(KVH):
                sp.dma_start(kp_d[kv], kwin[HD * kv:HD * kv + HD, (NT - 1) % 2, kv, P:2 * P]).then_inc(tail_out, 16)
            sp.dma_start(vp_d, vwin[:, (NT - 1) % 2, 1, :]).then_inc(tail_out, 16)
            sp.wait_ge(tail_in, 64)
            sp.dma_start(vs_d, s_v).then_inc(tail_out, 16)
            sp.wait_ge(smp["dve"], SV["dve_kT"])
            sp.dma_start(ksT_d, s_kT).then_inc(tail_out, 16)
            sp.wait_ge(smp["dve"], SV["dve_state"])
            sp.dma_start(Ss_d, s_state).then_inc(tail_out, 16)
            dve_o.wait(sp, "y", last)
            sp.dma_start(ys_d, xres[0:NS, :]).then_inc(y_out, 16)
            sp.wait_ge(y_out, 16 * (NT + 1))
            sp.wait_ge(tail_out, 16 * (HG + KVH + 1 + 3))

        @block.tensor
        def _(pe):
            def split_product(out, terms, start=True, stop=True):
                last = len(terms) - 1
                for i, (a_hi, a_lo, b_hi, b_lo) in enumerate(terms):
                    nc.tensor.matmul(out, a_hi, b_hi, start=start and i == 0, stop=False)
                    nc.tensor.matmul(out, a_hi, b_lo, start=False, stop=False)
                    mm = nc.tensor.matmul(out, a_lo, b_hi, start=False, stop=stop and i == last)
                return mm

            def bc(t):
                n = t.tokens
                pj.wait_free(pe, "bc", t)
                dve_u.wait(pe, "diag", t)
                nc.tensor.matmul(pj.bank("bc", t)[:, 0:n], ones[0:n, :].broadcast_to([n, P]), diag[0:n, 0:n],
                                 start=True, stop=True).then_inc(pj.full, 1)

            def features(t, bank, at_, c0, ntile):
                n = t.tokens
                for f in range(ntile):
                    c = c0 + f * P
                    mm = split_product(bank[:, at_ + f * P:at_ + f * P + n],
                                       [(w_hi[:, d, c:c + P], w_lo[:, d, c:c + P],
                                         u_hi[:, t.p, d, 0:n], u_lo[:, t.p, d, 0:n]) for d in range(DT)])
                return mm

            def rows(t, bank, at_, c0, width):
                n = t.tokens
                return split_product(bank[0:n, at_:at_ + width],
                                     [(u_hi[:, t.p, d, 0:n], u_lo[:, t.p, d, 0:n],
                                       w_hi[:, d, c0:c0 + width], w_lo[:, d, c0:c0 + width]) for d in range(DT)])

            def proj(t, name):
                if t.static and t.off == 0:
                    pe.wait_ge(w_lo_done, 1 + [g for g, _ in GROUPS].index(name))
                pj.wait_free(pe, name, t)
                dve_u.wait(pe, "lo", t)
                bank = pj.bank(name, t)
                if name == "gqk":
                    mm = features(t, bank, 0, COL[name], 4)
                elif name == "sq":
                    mm = features(t, bank, 0, COL[name], 4)
                elif name == "sklow":
                    features(t, bank, 0, COL[name], 1)
                    mm = rows(t, bank, P, COL[name] + P, P + RANK)
                else:
                    mm = rows(t, bank, 0, COL[name], 512)
                mm.then_inc(pj.full, 1)

            def scores(t, f):
                name = f"s{f}"
                at_ring.wait_free(pe, name, t)
                bank = at_ring.bank(name, t)
                if f == 0:
                    pj.wait_freed(pe, "sq", t)
                    pj.wait_freed(pe, "sklow", t)
                    if not (t.static and t.off == 0):
                        win_kept.wait(pe, "win", t + -1)
                nc.tensor.matmul(bank[:, :], sq[:, t.p, f, :], kwin[:, t.p].rearrange("p h c -> p (h c)"),
                                 start=True, stop=False)
                first = 1 if t.static and t.off == 0 else 0
                nc.tensor.matmul(bank[:, :].rearrange("p (h c) -> p h c", h=2), ident_b[:, :], bcast(band[:, first], 1, 2),
                                 start=False, stop=True).then_inc(at_ring.full, 1)

            def turn_probs(t, f):
                name = f"pt{f}"
                tr.wait_free(pe, name, t)
                at_ring.wait_freed(pe, f"s{f}", t)
                bank = tr.bank(name, t)
                for h in range(2):
                    for kb in range(2):
                        c = (2 * h + kb) * P
                        tp = nc.tensor.transpose(bank[:, c:c + P], PR[:, f % 2, h, kb * P:kb * P + P], ident[:, :])
                tp.then_inc(tr.full, 1)

            def values(t, f):
                if f == 0 and not (t.static and t.off == 0):
                    dve_o.wait(pe, "sg", t + -1)
                tr.wait_freed(pe, f"pt{f}", t)
                for h in range(2):
                    c = f * P + h * HD
                    for kb in range(2):
                        mm = nc.tensor.matmul(accS[:, c:c + HD], PT[:, h, kb, :],
                                              vwin[:, t.p, kb, h * HD:h * HD + HD], start=kb == 0, stop=kb == 1)
                mm.then_inc(pe_pv.sem, 1)

            def turn_low(t):
                tr.wait_free(pe, "glT", t)
                pj.wait_freed(pe, "sklow", t)
                nc.tensor.transpose(tr.bank("glT", t)[0:RANK, 0:P], glow[:, t.p, :], ident[:, :]).then_inc(tr.full, 1)

            def gate_up(t):
                tr.wait_free(pe, "z", t)
                tr.wait_freed(pe, "glT", t)
                bank = tr.bank("z", t)
                for f in range(FT):
                    mm = nc.tensor.matmul(bank[:, f * P:f * P + P], wgu[:, f * P:f * P + P], glT[:, :],
                                          start=True, stop=True)
                mm.then_inc(tr.full, 1)

            def leaf_scores(t):
                at_ring.wait_free(pe, "L3", t)
                dve_g.wait(pe, "QF", t)
                bank = at_ring.bank("L3", t)
                for f in range(FT):
                    mm = nc.tensor.matmul(bank[:, f * 2 * P:f * 2 * P + 2 * P], EX[:, S_LEAFK, f, :],
                                          QL[:, f].rearrange("p h c -> p (h c)"), start=True, stop=True)
                mm.then_inc(at_ring.full, 1)

            def level_scores(t, name, l0):
                at_ring.wait_free(pe, name, t)
                bank = at_ring.bank(name, t)
                for l in range(2):
                    for f in range(FT):
                        c = (l * FT + f) * P
                        mm = nc.tensor.matmul(bank[:, c:c + P], EX[:, l0 + l, f, :],
                                              QE[:, l0 + l, f].rearrange("p h c -> p (h c)"), start=True, stop=True)
                mm.then_inc(at_ring.full, 1)

            def turn_keys(t):
                tr.wait_free(pe, "KST", t)
                dve_g.wait(pe, "QF", t)
                for f in range(FT):
                    tp = nc.tensor.transpose(tr.bank("KST", t)[:, f * P:f * P + P], EX[:, S_STATE, f, :], ident[:, :])
                tp.then_inc(tr.full, 1)

            def gla_out(t):
                if not (t.static and t.off == 0):
                    dve_o.wait(pe, "gg", t + -1)
                    tr.wait_freed(pe, "SU", t + -1)
                at_ring.wait_freed(pe, "L2", t)
                pj.wait_freed(pe, "gv", t)
                for f in range(FT):
                    nc.tensor.matmul(accG[:, f * 2 * DV:(f + 1) * 2 * DV], EX[:, S_INTER, f, :],
                                     S_bd[:, f].rearrange("p h c -> p (h c)"), start=f == 0, stop=False,
                                     skip_group_check=True)
                for h in range(HG):
                    mm = nc.tensor.matmul(accG[:, h * DV:h * DV + DV], AT[:, h, :],
                                          gv[:, t.p, h * DV:h * DV + DV], start=False, stop=h == HG - 1,
                                          skip_group_check=True)
                mm.then_inc(pe_o.sem, 1)

            def state_update(t):
                tr.wait_free(pe, "SU", t)
                tr.wait_freed(pe, "KST", t)
                bank = tr.bank("SU", t)
                for h in range(HG):
                    r, f = DK * (h % 2), h // 2
                    mm = nc.tensor.matmul(bank[r:r + DK, f * DV:f * DV + DV], KST[:, h * DK:h * DK + DK],
                                          gv[:, t.p, h * DV:h * DV + DV], start=True, stop=True)
                mm.then_inc(tr.full, 1)

            def turn_out(t, g):
                n = t.tokens
                name = f"og{g}"
                tr.wait_free(pe, name, t)
                dve_o.wait(pe, "gsc", t)
                bank = tr.bank(name, t)
                for k in range(4):
                    c = (4 * g + k) * P
                    tp = nc.tensor.transpose(bank[:, k * P:k * P + n], gates[0:n, c:c + P], ident[0:n, 0:n])
                tp.then_inc(tr.full, 1)

            def out_proj(t, g):
                n = t.tokens
                name = f"y{g}"
                at_ring.wait_free(pe, name, t)
                if g == 0:
                    tr.wait_freed(pe, "og1", t)
                c = g * D // OUT_GROUPS
                split_product(at_ring.bank(name, t)[0:n, :],
                              [(ogT_hi[:, f, 0:n], ogT_lo[:, f, 0:n], wo_hi[:, f, c:c + 512], wo_lo[:, f, c:c + 512])
                               for f in range(DT)]).then_inc(at_ring.full, 1)

            def sample():
                t = Tile(NT)
                p = t.p
                pj.wait_freed(pe, "sg", t)
                pj.wait_freed(pe, "gv", t)
                nc.tensor.transpose(banks[0][0:RANK, 0:NS], glow[0:NS, p, :], ident[0:NS, 0:NS]
                                    ).then_inc(smp["pe"], 1)
                after(pe, "act_glT")
                for f in range(FT):
                    mm = nc.tensor.matmul(banks[1][:, f * NS:f * NS + NS], wgu[:, f * P:f * P + P], glT[:, 0:NS],
                                          start=True, stop=True)
                mm.then_inc(smp["pe"], 1)
                for f in range(FT):
                    tp = nc.tensor.transpose(banks[0][0:NS, f * P:f * P + P], gk[:, p, f, 0:NS], ident[:, :])
                tp.then_inc(smp["pe"], 1)
                after(pe, "dve_km")
                for r in range(4):
                    if r >= 2:
                        after(pe, f"dve_st{r - 2}")
                    for b in range(2):
                        for h in range(HG):
                            c = (2 * b + h // 2) * DV
                            o = DK * (h % 2)
                            mm = nc.tensor.matmul(banks[r % 2][o:o + DK, c:c + DV],
                                                  s_km[:, 2 * r + b, h * DK:h * DK + DK],
                                                  gv[0:NS, p, h * DV:h * DV + DV], start=True, stop=True)
                    mm.then_inc(smp["pe"], 1)
                after(pe, "dve_state")
                dve_o.wait(pe, "gg", Tile(NT - 1))
                for h in range(HG):
                    for b in range(NS):
                        mm = nc.tensor.matmul(accG[0:NS, h * DV:h * DV + DV], s_qm[:, h // 2, h % 2, b, :],
                                              s_state[:, b, h // 2, :], start=b == 0, stop=b == NS - 1)
                mm.then_inc(smp["pe"], 1)
                for b in range(NS):
                    c = (b % 4) * P
                    mm = nc.tensor.matmul(banks[b // 4][0:8, c:c + P], s_qs[:, b, :], s_kT[:, b, :],
                                          start=True, stop=True)
                mm.then_inc(smp["pe"], 1)
                after(pe, "dve_pn")
                for b in range(NS):
                    tp = nc.tensor.transpose(banks[0][:, 8 * b:8 * b + 8], s_p[:, b, :], ident[0:8, 0:8])
                tp.then_inc(smp["pe"], 1)
                after(pe, "dve_pT")
                for b in range(NS):
                    mm = nc.tensor.matmul(banks[1][:, 8 * b:8 * b + 8], s_v[:, b, :], s_pT[:, b, :],
                                          start=True, stop=True)
                mm.then_inc(smp["pe"], 1)
                after(pe, "dve_oT")
                dve_o.wait(pe, "sg", Tile(NT - 1))
                for f in range(GRP):
                    tp = nc.tensor.transpose(accS[0:NS, f * P:f * P + P], s_oT[:, f, :], ident[:, :])
                tp.then_inc(smp["pe"], 1)

            pe.wait_ge(init, 1)
            bc(Tile(0))
            for name, _ in GROUPS:
                proj(Tile(0), name)
            bc(Tile(1))
            pe.wait_ge(w_lo_done, NG)

            def body(t):
                nxt = t + 1
                turn_low(t)
                proj(nxt, "gqk")
                gate_up(t)
                scores(t, 0)
                scores(t, 1)
                proj(nxt, "sq")
                turn_probs(t, 0)
                scores(t, 2)
                turn_probs(t, 1)
                scores(t, 3)
                values(t, 0)
                proj(nxt, "sklow")
                turn_probs(t, 2)
                values(t, 1)
                turn_probs(t, 3)
                values(t, 2)
                leaf_scores(t)
                level_scores(t, "L1", 0)
                values(t, 3)
                level_scores(t, "L2", 2)
                turn_keys(t)
                proj(nxt, "gv")
                gla_out(t)
                state_update(t)
                proj(nxt, "gg")
                turn_out(t, 0)
                turn_out(t, 1)
                proj(nxt, "sg")
                if not (t.static and t.off + 2 > NT):
                    bc(t + 2)
                out_proj(t, 0)
                out_proj(t, 1)

            iterations(pe, body)
            sample()
            turn_out(Tile(NT), 0)
            turn_out(Tile(NT), 1)
            out_proj(Tile(NT), 0)
            out_proj(Tile(NT), 1)

        @block.scalar
        def _(act):
            def norm_rows(t):
                n, s = t.tokens, xst[0:t.tokens, t.p]
                act.wait_ge(xq_in, (t.n + 1) * 16)
                nc.scalar.activation(xq[0:n, :], xq[0:n, :], ACT.Square, accum_out=s[:, 0:1]).then_inc(act_u.sem, 1)
                dve_u.wait(act, "ms", t)
                nc.scalar.activation(s[:, 2:3], s[:, 1:2], ACT.Ln).then_inc(act_u.sem, 1)
                act_u.wait(act, "ln", t)
                nc.scalar.activation(s[:, 3:4], s[:, 2:3], ACT.Exp, scale=-0.5).then_inc(act_u.sem, 1)

            def split_u(t):
                n = t.tokens
                pj.wait_freed(act, "bc", t)
                if not (t.static and t.off < 2):
                    pj.wait_full(act, "sg", t + -2)
                nc.scalar.copy(u_hi[:, t.p, :, 0:n], xT[:, :, 0:n]).then_inc(act_u.sem, 1)

            def take_qk(t):
                n = t.tokens
                pj.wait_full(act, "gqk", t)
                bank = pj.bank("gqk", t)[:, :].rearrange("p (f c) -> p f c", f=4)
                nc.scalar.activation(gq[:, t.p, :, 0:n], bank[:, 0:2, 0:n], ACT.Identity, scale=invq[:, 0:1])
                nc.scalar.activation(gk[:, t.p, :, 0:n], bank[:, 2:4, 0:n], ACT.Identity,
                                     scale=inv[:, 0:1]).then_inc(pj.freed["act"], 1)

            def take_sq(t):
                n = t.tokens
                pj.wait_full(act, "sq", t)
                bank = pj.bank("sq", t)[:, :].rearrange("p (f c) -> p f c", f=4)
                nc.scalar.activation(sq[:, t.p, :, 0:n], bank[:, :, 0:n], ACT.Identity,
                                     scale=invq[:, 1:2]).then_inc(pj.freed["act"], 1)

            def take_gate(t, g):
                n, name = t.tokens, ("gg", "sg")[g]
                pj.wait_full(act, name, t)
                if g == 0 and not (t.static and t.off == 0):
                    tr.wait_full(act, "og1", t + -1)
                nc.scalar.activation(gates[0:n, g * 512:g * 512 + 512], pj.bank(name, t)[0:n, :], ACT.Silu,
                                     scale=inv[0:n, 4 + g:5 + g]).then_inc(pj.freed["act"], 1)

            def take_low(t):
                tr.wait_full(act, "glT", t)
                nc.scalar.copy(glT[:, :], tr.bank("glT", t)[0:RANK, 0:P]).then_inc(tr.freed["act"], 1)

            def log_gate(t):
                tr.wait_freed(act, "z", t)
                nc.scalar.activation(EX[:, 1], EX[:, 0], ACT.Abs).then_inc(act_g.sem, 1)
                act_g.wait(act, "az", t)
                nc.scalar.activation(EX[:, 1], EX[:, 1], ACT.Exp, scale=-1.0).then_inc(act_g.sem, 1)
                act_g.wait(act, "ez", t)
                nc.scalar.activation(EX[:, 1], EX[:, 1], ACT.Ln, bias=1.0).then_inc(act_g.sem, 1)

            def decays(t):
                dve_g.wait(act, "scan", t)
                nc.scalar.activation(EX[:, S_INTER], bsum[:, :, :], ACT.Exp, scale=1 / TAU)
                nc.scalar.activation(dec[:, :].unsqueeze(2), bsum[:, :, P - 1:P], ACT.Exp, scale=1 / TAU)
                pool_g.wait(act, "D", t)
                nc.scalar.activation(EX[:, S_LEAFK], EX[:, S_LEAFQ], ACT.Exp, scale=-1 / TAU)
                nc.scalar.activation(EX[:, 0:5], EX[:, 0:5], ACT.Exp, scale=1 / TAU)
                nc.scalar.activation(EX[:, S_LEAFQ], EX[:, S_LEAFQ], ACT.Exp, scale=1 / TAU).then_inc(act_g.sem, 1)

            def probs(t, f):
                name = f"s{f}"
                bank = at_ring.bank(name, t)
                dve_w.wait(act, f"nm{f}", t)
                if f >= 2:
                    tr.wait_full(act, f"pt{f - 2}", t)
                elif not (t.static and t.off == 0):
                    tr.wait_full(act, f"pt{f + 2}", t + -1)
                for h in range(2):
                    e = nc.scalar.activation(PR[:, f % 2, h, :], bank[:, h * 2 * P:(h + 1) * 2 * P], ACT.Exp,
                                             bias=wst[:, 0, 2 * f + h:2 * f + h + 1],
                                             accum_out=wst[:, 1, 2 * f + h:2 * f + h + 1])
                e.then_inc(at_ring.freed["act"], 1)

            def take_pt(t, f):
                tr.wait_full(act, f"pt{f}", t)
                pe_pv.wait(act, f"pv{f - 1}", t)
                nc.scalar.copy(PT[:, :, :, :].rearrange("p a b c -> p (a b c)"),
                               tr.bank(f"pt{f}", t)[:, :]).then_inc(tr.freed["act"], 1)

            def sink_term(t):
                dve_w.wait(act, "esi", t)
                nc.scalar.activation(wst[:, 2, :], wst[:, 2, :], ACT.Exp).then_inc(act_w.sem, 1)

            def take_kst(t):
                tr.wait_full(act, "KST", t)
                nc.scalar.copy(KST[:, :], tr.bank("KST", t)[:, 0:2 * P]).then_inc(tr.freed["act"], 1)

            def head_norm(t):
                n = t.tokens
                if t.sample:
                    act.wait_ge(smp["pe"], SV["pe_o"])
                else:
                    pe_o.wait(act, "o", t)
                for h in range(HG):
                    sq_ = nc.scalar.activation(junk[0:n, h * DV:h * DV + DV], accG[0:n, h * DV:h * DV + DV], ACT.Square,
                                               accum_out=ost[0:n, 0, h:h + 1])
                sq_.then_inc(act_o.sem, 1)
                dve_o.wait(act, "oms", t)
                nc.scalar.activation(ost[0:n, 2, :], ost[0:n, 1, :], ACT.Ln).then_inc(act_o.sem, 1)
                act_o.wait(act, "oln", t)
                nc.scalar.activation(ost[0:n, 3, :], ost[0:n, 2, :], ACT.Exp, scale=-0.5).then_inc(act_o.sem, 1)

            def take_out(t, g):
                n = t.tokens
                tr.wait_full(act, f"og{g}", t)
                bank = tr.bank(f"og{g}", t)[:, :].rearrange("p (f c) -> p f c", f=4)
                nc.scalar.copy(ogT_hi[:, 4 * g:4 * g + 4, 0:n], bank[:, :, 0:n]).then_inc(act_o.sem, 1)

            def final_norm(t):
                n = t.tokens
                at_ring.wait_freed(act, "y1", t)
                nc.scalar.activation(junk[0:n, :], xres[0:n, :], ACT.Square, accum_out=hst[0:n, 0:1]
                                     ).then_inc(act_o.sem, 1)
                dve_o.wait(act, "hms", t)
                nc.scalar.activation(hst[0:n, 2:3], hst[0:n, 1:2], ACT.Ln).then_inc(act_o.sem, 1)
                act_o.wait(act, "hln", t)
                nc.scalar.activation(hst[0:n, 3:4], hst[0:n, 2:3], ACT.Exp, scale=-0.5).then_inc(act_o.sem, 1)

            def split_w(g):
                n = GROUPS[g][1] if g < len(GROUPS) else D // OUT_GROUPS
                act.wait_ge(w_scaled, g + 1)
                src = stage[g % 2][:, 0:DT * n].rearrange("p (d c) -> p d c", d=DT)
                for d in range(DT):
                    h = nc.scalar.activation(w_slice(g, w_hi, wo_hi)[:, d], src[:, d], ACT.Identity,
                                             scale=gs[:, g % 2, d:d + 1])
                h.then_inc(w_hi_done, 1)

            def sample():
                t = Tile(NT)
                after(act, "pe_glT")
                nc.scalar.copy(glT[:, 0:NS], banks[0][0:RANK, 0:NS]).then_inc(smp["act"], 1)
                after(act, "dve_zb")
                nc.scalar.activation(s_z[:, 1], s_z[:, 0], ACT.Abs).then_inc(smp["act"], 1)
                after(act, "act_az")
                nc.scalar.activation(s_z[:, 1], s_z[:, 1], ACT.Exp, scale=-1.0).then_inc(smp["act"], 1)
                after(act, "act_ez")
                nc.scalar.activation(s_z[:, 1], s_z[:, 1], ACT.Ln, bias=1.0).then_inc(smp["act"], 1)
                after(act, "dve_la")
                nc.scalar.activation(s_z[:, 4], s_z[:, 3], ACT.Exp, scale=1 / TAU).then_inc(smp["act"], 1)
                after(act, "dve_esi")
                nc.scalar.activation(s_p, s_p, ACT.Exp)
                nc.scalar.activation(s_st[:, 3, :], s_st[:, 2, :], ACT.Exp).then_inc(smp["act"], 1)

            norm_rows(Tile(0))
            split_u(Tile(0))
            for g in range(NG):
                split_w(g)
                if g == 0:
                    norm_rows(Tile(1))
                if g == 1:
                    take_qk(Tile(0))
                if g == 2:
                    take_sq(Tile(0))
            act.wait_ge(w_lo_done, NG)
            take_gate(Tile(0), 0)
            take_gate(Tile(0), 1)
            split_u(Tile(1))

            def body(t):
                nxt = t + 1
                take_low(t)
                take_qk(nxt)
                log_gate(t)
                probs(t, 0)
                probs(t, 1)
                take_sq(nxt)
                decays(t)
                probs(t, 2)
                take_pt(t, 1)
                probs(t, 3)
                take_pt(t, 3)
                sink_term(t)
                take_kst(t)
                if not (t.static and t.off + 2 > NT):
                    norm_rows(t + 2)
                head_norm(t)
                take_out(t, 0)
                take_out(t, 1)
                take_gate(nxt, 0)
                take_gate(nxt, 1)
                if not (t.static and t.off + 2 > NT):
                    split_u(t + 2)
                final_norm(t)

            iterations(act, body)
            sample()
            head_norm(Tile(NT))
            take_out(Tile(NT), 0)
            take_out(Tile(NT), 1)
            final_norm(Tile(NT))

        @block.vector
        def _(dve):
            V = nc.vector

            def rsqrt_step(ev, names, a, y0, tmp, y, t, gain=1.0):
                V.tensor_tensor(tmp, y0, y0, ALU.mult).then_inc(ev.sem, 1)
                ev.wait(dve, names[0], t)
                V.scalar_tensor_tensor(out=tmp, in0=tmp, scalar=-0.5 * gain, in1=a, op0=ALU.mult,
                                       op1=ALU.mult).then_inc(ev.sem, 1)
                ev.wait(dve, names[1], t)
                V.scalar_tensor_tensor(out=y, in0=tmp, scalar=1.5 * gain, in1=y0, op0=ALU.add,
                                       op1=ALU.mult).then_inc(ev.sem, 1)
                ev.wait(dve, names[2], t)

            def norm_x(t):
                n, s = t.tokens, xst[0:t.tokens, t.p]
                act_u.wait(dve, "ssq", t)
                V.tensor_scalar(s[:, 1:2], s[:, 0:1], 1.0 / D, EPS, ALU.mult, ALU.add).then_inc(dve_u.sem, 1)
                act_u.wait(dve, "exp", t)
                rsqrt_step(dve_u, ["n0", "n1", "rstd"], s[:, 1:2], s[:, 3:4], s[:, 4:5], s[:, 5:6], t, U_SCALE)
                if not (t.static and t.off == 0):
                    pj.wait_full(dve, "bc", t + -1)
                V.tensor_scalar(diag[0:n, 0:n], ident[0:n, 0:n], s[:, 5:6], None, ALU.mult).then_inc(dve_u.sem, 1)

            def scale_u(t):
                n = t.tokens
                dve.wait_ge(xT_in, (t.n + 1) * 16)
                pj.wait_full(dve, "bc", t)
                V.tensor_tensor(xT[:, :, 0:n], xT[:, :, 0:n], bcast(pj.bank("bc", t)[:, 0:n], 1, DT),
                                ALU.mult).then_inc(pj.freed["dve"], 1)

            def split_u(t):
                n = t.tokens
                act_u.wait(dve, "hi", t)
                V.tensor_tensor(u_lo[:, t.p, :, 0:n], xT[:, :, 0:n], u_hi[:, t.p, :, 0:n],
                                ALU.subtract).then_inc(dve_u.sem, 1)

            def take_kv(t):
                n = t.tokens
                pj.wait_full(dve, "sklow", t)
                bank = pj.bank("sklow", t)
                if t.sample:
                    V.tensor_scalar(s_knew[:, :], bank[:, 0:n], inv[:, 2:3], None, ALU.mult)
                    V.tensor_scalar(s_vnew, bank[0:n, P:2 * P], inv[0:n, 2:3], None, ALU.mult)
                else:
                    for h in range(KVH):
                        r = h * HD
                        V.tensor_scalar(kwin[r:r + HD, t.p, h, P:2 * P], bank[r:r + HD, 0:P], inv[r:r + HD, 2:3],
                                        None, ALU.mult)
                    V.tensor_scalar(vwin[:, t.p, 1, :], bank[:, P:2 * P], inv[:, 2:3], None, ALU.mult)
                V.tensor_scalar(glow[0:n, t.p, :], bank[0:n, 2 * P:2 * P + RANK], inv[0:n, 2:3], None,
                                ALU.mult).then_inc(pj.freed["dve"], 1)

            def take_gv(t):
                n = t.tokens
                pj.wait_full(dve, "gv", t)
                V.tensor_scalar(gv[0:n, t.p, :], pj.bank("gv", t)[0:n, :], inv[0:n, 3:4], None,
                                ALU.mult).then_inc(pj.freed["dve"], 1)

            def take_z(t):
                tr.wait_full(dve, "z", t)
                bank = tr.bank("z", t)
                for f in range(FT):
                    z = V.tensor_scalar(EX[:, 0, f, :], bank[:, f * P:f * P + P], bg[:, f:f + 1], None, ALU.add)
                z.then_inc(tr.freed["dve"], 1)
                tr.wait_freed(dve, "z", t)
                V.tensor_scalar(EX[:, 2], EX[:, 0], 0.0, None, ALU.min).then_inc(dve_g.sem, 1)

            def sums(t):
                act_g.wait(dve, "l1", t)
                dve_g.wait(dve, "mz", t)
                V.tensor_tensor(EX[:, 2], EX[:, 2], EX[:, 1], ALU.subtract).then_inc(dve_g.sem, 1)
                dve_g.wait(dve, "la", t)
                V.tensor_scalar(EX[:, 3], EX[:, 2], LEAF_FLOOR * TAU, None, ALU.max).then_inc(dve_g.sem, 1)
                dve_g.wait(dve, "lc", t)
                for f in range(FT):
                    V.tensor_tensor_scan(bsum[:, f, :], leafscan[:, 0, :], EX[:, 2, f, :], 0.0, ALU.mult, ALU.add)
                    sc = V.tensor_tensor_scan(lsum[:, f, :], leafscan[:, 1, :], EX[:, 3, f, :], 0.0, ALU.mult, ALU.add)
                sc.then_inc(dve_g.sem, 1)

            def factors(t):
                act_g.wait(dve, "E", t)
                for l, s in enumerate(LEVELS):
                    for h in range(2):
                        r = h * DK
                        late = lambda ap: ap.rearrange("p f (b c) -> p f b c", c=2 * s)[:, :, :, s:2 * s]
                        V.tensor_tensor(QE[r:r + DK, l, :, h, :].rearrange("p f (b c) -> p f b c", c=s),
                                        late(gq[r:r + DK, t.p]), late(EX[r:r + DK, l]), ALU.mult)
                for h in range(2):
                    r = h * DK
                    V.tensor_tensor(QL[r:r + DK, :, h, :], gq[r:r + DK, t.p], EX[r:r + DK, S_LEAFQ], ALU.mult)
                V.tensor_tensor(EX[:, S_INTER], EX[:, S_INTER], gq[:, t.p], ALU.mult).then_inc(dve_g.sem, 1)
                dve_g.wait(dve, "Q", t)
                V.tensor_tensor(EX[:, 0:6], EX[:, 0:6], bcast(gk[:, t.p], 1, 6), ALU.mult).then_inc(dve_g.sem, 1)

            def assemble(t):
                at_ring.wait_full(dve, "L3", t)
                V.tensor_tensor(AT, at_ring.bank("L3", t)[:, :].rearrange("p (h c) -> p h c", h=HG),
                                bcast(leafmask[:, :], 1, HG), ALU.mult).then_inc(at_ring.freed["dve"], 1)
                at_ring.wait_full(dve, "L1", t)
                at_ring.wait_freed(dve, "L3", t)
                lv = at_ring.bank("L1", t)[:, :].rearrange("p (l h c) -> p l h c", l=2, h=HG)
                V.tensor_copy(AT[0:64, :, 64:128], lv[0:64, 0])
                V.tensor_copy(AT[0:32, :, 32:64], lv[0:32, 1, :, 0:32])
                V.tensor_copy(AT[64:96, :, 96:128], lv[64:96, 1, :, 32:64]).then_inc(at_ring.freed["dve"], 1)
                at_ring.wait_freed(dve, "L1", t)
                at_ring.wait_full(dve, "L2", t)
                if not (t.static and t.off == 0):
                    pe_pv.wait(dve, "pv3", t + -1)
                V.tensor_copy(kwin[:, 1 - t.p, :, 0:P], kwin[:, t.p, :, P:2 * P])
                masked_copy(t, 2).then_inc(dve_g.sem, 1)
                dve_g.wait(dve, "L16", t)
                V.tensor_copy(vwin[:, 1 - t.p, 0, :], vwin[:, t.p, 1, :]).then_inc(win_kept.sem, 1)
                masked_copy(t, 3).then_inc(at_ring.freed["dve"], 1)

            def masked_copy(t, l):
                s = LEVELS[l]
                return V.copy_predicated(
                    AT.rearrange("p h (b c) -> p h b c", c=2 * s)[:, :, :, s:2 * s],
                    bcast(lvlmask[:, l, :].bitcast(I32).rearrange("p (b c) -> p b c", c=s), 1, HG),
                    at_ring.bank("L2", t)[:, (l - 2) * 256:(l - 1) * 256].rearrange(
                        "p (h b c) -> p h b c", h=HG, c=s))

            def update_state(t):
                tr.wait_full(dve, "SU", t)
                bank = tr.bank("SU", t)
                for h in range(HG):
                    r, f = DK * (h % 2), h // 2
                    s = S_bd[r:r + DK, f, h % 2, :]
                    up = V.scalar_tensor_tensor(out=s, in0=s, scalar=dec[r:r + DK, f:f + 1],
                                                in1=bank[r:r + DK, f * DV:f * DV + DV], op0=ALU.mult, op1=ALU.add)
                up.then_inc(tr.freed["dve"], 1)

            def row_max(t, f):
                at_ring.wait_full(dve, f"s{f}", t)
                V.tensor_reduce(wst[:, 3, 2 * f:2 * f + 2],
                                at_ring.bank(f"s{f}", t)[:, :].rearrange("p (h c) -> p h c", h=2),
                                AX.X, ALU.max, negate=True).then_inc(dve_w.sem, 1)
                dve_w.wait(dve, f"mx{f}", t)
                V.tensor_tensor(wst[:, 0, 2 * f:2 * f + 2], wst[:, 3, 2 * f:2 * f + 2], nsink[:, 2 * f:2 * f + 2],
                                ALU.min).then_inc(dve_w.sem, 1)

            def take_pt(t, f):
                tr.wait_full(dve, f"pt{f}", t)
                if f > 0:
                    pe_pv.wait(dve, f"pv{f - 1}", t)
                elif not (t.static and t.off == 0):
                    pe_pv.wait(dve, "pv3", t + -1)
                V.tensor_copy(PT[:, :, :, :].rearrange("p a b c -> p (a b c)"),
                              tr.bank(f"pt{f}", t)[:, :]).then_inc(tr.freed["dve"], 1)

            def denominators(t):
                dve_w.wait(dve, "nm3", t)
                V.tensor_tensor(wst[:, 2, :], wst[:, 0, :], sink[:, :], ALU.add).then_inc(dve_w.sem, 1)
                act_w.wait(dve, "es", t)
                V.tensor_tensor(wst[:, 4, :], wst[:, 1, :], wst[:, 2, :], ALU.add).then_inc(dve_w.sem, 1)
                dve_w.wait(dve, "den", t)
                V.reciprocal(wst[:, 5, :], wst[:, 4, :]).then_inc(dve_w.sem, 1)

            def gate_window(t):
                n = t.tokens
                if t.sample:
                    dve.wait_ge(smp["pe"], SV["pe_oT"])
                    pj.wait_freed(dve, "sg", t)
                else:
                    pool_w.wait(dve, "gs", t)
                    pe_pv.wait(dve, "pv3", t)
                V.tensor_tensor(gates[0:n, 512:1024], gates[0:n, 512:1024], accS[0:n, :], ALU.mult
                                ).then_inc(dve_o.sem, 1)

            def gate_gla(t):
                n = t.tokens
                o = ost[0:n]
                act_o.wait(dve, "oss", t)
                V.tensor_scalar(o[:, 1, :], o[:, 0, :], 1.0 / DV, EPS, ALU.mult, ALU.add).then_inc(dve_o.sem, 1)
                act_o.wait(dve, "oexp", t)
                rsqrt_step(dve_o, ["on0", "on1", "orstd"], o[:, 1, :], o[:, 3, :], o[:, 4, :], o[:, 5, :], t)
                pj.wait_freed(dve, "gg", t)
                for h in range(HG):
                    g = gates[0:n, h * DV:h * DV + DV]
                    gg = V.scalar_tensor_tensor(out=g, in0=accG[0:n, h * DV:h * DV + DV], scalar=o[:, 5, h:h + 1],
                                                in1=g, op0=ALU.mult, op1=ALU.mult)
                gg.then_inc(dve_o.sem, 1)

            def scale_rows(t):
                n = t.tokens
                a = amax[0:n]
                dve_o.wait(dve, "gg", t)
                V.tensor_reduce(a[:, 0:1], gates[0:n, :], AX.X, ALU.max, apply_absolute_value=True
                                ).then_inc(dve_o.sem, 1)
                dve_o.wait(dve, "am", t)
                V.tensor_scalar(a[:, 1:2], a[:, 0:1], 1e-30, None, ALU.max).then_inc(dve_o.sem, 1)
                dve_o.wait(dve, "amc", t)
                V.reciprocal(a[:, 2:3], a[:, 1:2]).then_inc(dve_o.sem, 1)
                dve_o.wait(dve, "rsc", t)
                V.tensor_scalar(gates[0:n, :], gates[0:n, :], a[:, 2:3], O_TOP, ALU.mult, ALU.mult
                                ).then_inc(dve_o.sem, 1)
                V.tensor_scalar(isc[0:n, :], inv[0:n, NG - 2:NG], a[:, 1:2], 1.0 / O_TOP, ALU.mult, ALU.mult
                                ).then_inc(dve_o.sem, 1)

            def take_out(t, g):
                n = t.tokens
                act_o.wait(dve, f"hi{g}", t)
                bank = tr.bank(f"og{g}", t)[:, :].rearrange("p (f c) -> p f c", f=4)
                V.tensor_tensor(ogT_lo[:, 4 * g:4 * g + 4, 0:n], bank[:, :, 0:n], ogT_hi[:, 4 * g:4 * g + 4, 0:n],
                                ALU.subtract).then_inc(tr.freed["dve"], 1)

            def residual(t):
                n = t.tokens
                dve.wait_ge(xres_in, (t.n + 1) * 16)
                dve_o.wait(dve, "isc", t)
                for g in range(OUT_GROUPS):
                    at_ring.wait_full(dve, f"y{g}", t)
                    x = xres[0:n, g * 512:g * 512 + 512]
                    V.scalar_tensor_tensor(out=x, in0=at_ring.bank(f"y{g}", t)[0:n, :], scalar=isc[0:n, g:g + 1],
                                           in1=x, op0=ALU.mult, op1=ALU.add).then_inc(at_ring.freed["dve"], 1)

            def final_norm(t):
                n = t.tokens
                h = hst[0:n]
                act_o.wait(dve, "hss", t)
                V.tensor_scalar(h[:, 1:2], h[:, 0:1], 1.0 / D, EPS, ALU.mult, ALU.add).then_inc(dve_o.sem, 1)
                act_o.wait(dve, "hexp", t)
                rsqrt_step(dve_o, ["hn0", "hn1", "hr"], h[:, 1:2], h[:, 3:4], h[:, 4:5], h[:, 5:6], t)
                V.scalar_tensor_tensor(out=xres[0:n, :], in0=xres[0:n, :], scalar=h[:, 5:6], in1=normf[0:n, :],
                                       op0=ALU.mult, op1=ALU.mult).then_inc(dve_o.sem, 1)

            def split_w(g):
                n = GROUPS[g][1] if g < len(GROUPS) else D // OUT_GROUPS
                gain = (gin if g < len(GROUPS) else gout)[:, :]
                s = g % 2
                src = stage[s][:, 0:DT * n].rearrange("p (d c) -> p d c", d=DT)
                step = 4 * g
                dve.wait_ge(w_in_sem[s], 16 * (g // 2 + 1))
                V.tensor_reduce(wabs[:, s, :], src, AX.X, ALU.max, apply_absolute_value=True).then_inc(w_dve, 1)
                dve.wait_ge(w_dve, step + 1)
                V.tensor_tensor(wabs[:, s, :], wabs[:, s, :], gain, ALU.mult).then_inc(w_dve, 1)
                dve.wait_ge(w_dve, step + 2)
                V.tensor_reduce(wcol[:, 0:1], wabs[:, s, :], AX.X, ALU.max, apply_absolute_value=True
                                ).then_inc(w_row, 1)
                dve.wait_ge(w_max, g + 1)
                V.tensor_scalar(wcol[:, 2:3], wcol[:, 1:2], 1.0 / W_TOP, 1e-30, ALU.mult, ALU.max).then_inc(w_dve, 1)
                dve.wait_ge(w_dve, step + 3)
                V.reciprocal(wcol[:, 3:4], wcol[:, 2:3]).then_inc(w_dve, 1)
                c = 1.0 / U_SCALE if g < len(GROUPS) else 1.0
                V.tensor_scalar(inv[:, g:g + 1], wcol[:, 2:3], c, None, ALU.mult)
                if g < 2:
                    V.tensor_scalar(invq[:, g:g + 1], wcol[:, 2:3], c * DK ** -0.5, None, ALU.mult)
                dve.wait_ge(w_dve, step + 4)
                V.tensor_scalar(gs[:, s, :], gain, wcol[:, 3:4], None, ALU.mult).then_inc(w_scaled, 1)
                dve.wait_ge(w_hi_done, g + 1)
                for d in range(DT):
                    lo = V.scalar_tensor_tensor(out=w_slice(g, w_lo, wo_lo)[:, d], in0=src[:, d],
                                                scalar=gs[:, s, d:d + 1], in1=w_slice(g, w_hi, wo_hi)[:, d],
                                                op0=ALU.mult, op1=ALU.subtract)
                lo.then_inc(w_lo_done, 1)

            def sample():
                t = Tile(NT)
                p = t.p
                done = smp["dve"]
                after(dve, "pe_z")
                for f in range(FT):
                    z = V.tensor_scalar(s_z[:, 0, f, :], banks[1][:, f * NS:f * NS + NS], bg[:, f:f + 1], None,
                                        ALU.add)
                z.then_inc(done, 1)
                after(dve, "dve_zb")
                V.tensor_scalar(s_z[:, 2], s_z[:, 0], 0.0, None, ALU.min).then_inc(done, 1)
                after(dve, "act_l1")
                after(dve, "dve_mz")
                V.tensor_tensor(s_z[:, 3], s_z[:, 2], s_z[:, 1], ALU.subtract).then_inc(done, 1)
                after(dve, "pe_kt")
                V.tensor_copy(s_kt, banks[0][0:NS, 0:HG * DK]).then_inc(done, 1)
                after(dve, "dve_kt")
                V.tensor_tensor(s_km, bcast(s_kt, 1, NS), bcast(ident[0:NS, 0:NS], 2, HG * DK), ALU.mult
                                ).then_inc(done, 1)
                V.memset(s_qm, 0.0).then_inc(done, 1)
                after(dve, "dve_qz")
                for f in range(FT):
                    for h in range(2):
                        r = h * DK
                        q = V.tensor_copy(s_qm[r:r + DK, f, h].rearrange("p b c -> p (b c)")[:, 0:NS * NS:NS + 1],
                                          gq[r:r + DK, p, f, 0:NS])
                q.then_inc(done, 1)
                dve.wait_ge(tail_in, 64)
                V.tensor_copy(s_kT[:, :, P - 1:P], s_knew[:, :].unsqueeze(2)).then_inc(done, 1)
                V.memset(s_qs, 0.0).then_inc(done, 1)
                after(dve, "dve_qsz")
                for h in range(KVH):
                    r = h * HD
                    q = V.tensor_copy(s_qs[r:r + HD, :, GRP * h:GRP * h + GRP],
                                      sq[r:r + HD, p, :, 0:NS].rearrange("p f b -> p b f"))
                q.then_inc(done, 1)
                after(dve, "act_a")
                for r in range(4):
                    after(dve, f"pe_kv{r}")
                    for b in range(2):
                        for f in range(FT):
                            s = s_state[:, 2 * r + b, f, :]
                            c = (2 * b + f) * DV
                            up = V.scalar_tensor_tensor(out=s, in0=s, scalar=s_z[:, 4, f, 2 * r + b:2 * r + b + 1],
                                                        in1=banks[r % 2][:, c:c + DV], op0=ALU.mult, op1=ALU.add)
                    up.then_inc(done, 1)
                after(dve, "pe_sc")
                for i in range(2):
                    mx = V.tensor_reduce(s_st[:, 0, 4 * i:4 * i + 4],
                                         banks[i][0:8, :].rearrange("p (b c) -> p b c", b=4), AX.X, ALU.max,
                                         negate=True)
                mx.then_inc(done, 1)
                after(dve, "dve_mx")
                V.tensor_scalar(s_st[:, 1, :], s_st[:, 0, :], s_sink[:, 1:2], None, ALU.min).then_inc(done, 1)
                after(dve, "dve_nm")
                for i in range(2):
                    sub = V.tensor_tensor(s_p[:, 4 * i:4 * i + 4, :], banks[i][0:8, :].rearrange(
                        "p (b c) -> p b c", b=4), bcast(s_st[:, 1, 4 * i:4 * i + 4], 2, P), ALU.add)
                sub.then_inc(done, 1)
                V.tensor_scalar(s_st[:, 2, :], s_st[:, 1, :], s_sink[:, 0:1], None, ALU.add).then_inc(done, 1)
                after(dve, "act_exp")
                V.tensor_reduce(s_st[:, 4, :], s_p, AX.X, ALU.add).then_inc(done, 1)
                after(dve, "dve_sum")
                V.tensor_tensor(s_st[:, 5, :], s_st[:, 4, :], s_st[:, 3, :], ALU.add).then_inc(done, 1)
                after(dve, "dve_den")
                V.reciprocal(s_st[:, 6, :], s_st[:, 5, :]).then_inc(done, 1)
                after(dve, "dve_rden")
                V.tensor_tensor(s_p, s_p, bcast(s_st[:, 6, :], 2, P), ALU.mult).then_inc(done, 1)
                after(dve, "pe_pT")
                V.tensor_copy(s_pT, banks[0][:, 0:8 * NS].rearrange("p (b h) -> p b h", b=NS)).then_inc(done, 1)
                after(dve, "pe_pv")
                for h in range(KVH):
                    r = h * HD
                    o = V.tensor_copy(s_oT[r:r + HD, :, :], banks[1][r:r + HD, 0:8 * NS].rearrange(
                        "p (b h) -> p h b", b=NS)[:, GRP * h:GRP * h + GRP, :])
                o.then_inc(done, 1)

            dve.wait_ge(const_in, 16 * 12)
            V.tensor_copy(ident_b[:, :], ident[:, :])
            V.tensor_scalar(s_sink[:, 1:2], s_sink[:, 0:1], -1.0, None, ALU.mult)
            V.tensor_scalar(nsink[:, :], sink[:, :], -1.0, None, ALU.mult)
            V.memset(ones[:, :], 1.0)
            V.memset(kwin[:, :, :, :], 0.0)
            V.memset(vwin[:, :, :, :], 0.0)
            V.memset(S_bd[:, :, :, :], 0.0).then_inc(init, 1)
            norm_x(Tile(0))
            scale_u(Tile(0))
            split_u(Tile(0))
            for g in range(NG):
                split_w(g)
                if g == 0:
                    norm_x(Tile(1))
                if g == 3:
                    take_kv(Tile(0))
                if g == 4:
                    take_gv(Tile(0))
            scale_u(Tile(1))
            split_u(Tile(1))
            dve.wait_ge(w_hi_done, NG)
            V.memset(QE, 0.0)
            V.memset(QL, 0.0)

            def body(t):
                nxt = t + 1
                take_z(t)
                row_max(t, 0)
                row_max(t, 1)
                sums(t)
                take_pt(t, 0)
                row_max(t, 2)
                row_max(t, 3)
                factors(t)
                take_kv(nxt)
                take_pt(t, 2)
                denominators(t)
                assemble(t)
                take_gv(nxt)
                if not (t.static and t.off + 2 > NT):
                    norm_x(t + 2)
                gate_window(t)
                gate_gla(t)
                scale_rows(t)
                update_state(t)
                take_out(t, 0)
                take_out(t, 1)
                if not (t.static and t.off + 2 > NT):
                    scale_u(t + 2)
                    split_u(t + 2)
                residual(t)
                final_norm(t)

            iterations(dve, body)
            sample()
            gate_window(Tile(NT))
            gate_gla(Tile(NT))
            scale_rows(Tile(NT))
            take_out(Tile(NT), 0)
            take_out(Tile(NT), 1)
            residual(Tile(NT))
            final_norm(Tile(NT))

        @block.gpsimd
        def _(pool):
            G = nc.gpsimd
            for g in range(NG):
                pool.wait_ge(w_row, g + 1)
                G.partition_all_reduce(wcol[:, 1:2], wcol[:, 0:1], P, bass.bass_isa.ReduceOp.max
                                       ).then_inc(w_max, 1)

            def differences(t):
                dve_g.wait(pool, "scan", t)
                for l, s in enumerate(LEVELS):
                    b = bsum[:, :, :].rearrange("p f (b c) -> p (f b) c", c=2 * s)
                    o = EX[:, l].rearrange("p f (b c) -> p (f b) c", c=2 * s)
                    mid = b[:, :, s - 1:s].broadcast_to([P, FT * P // (2 * s), s])
                    G.tensor_tensor(o[:, :, 0:s], mid, b[:, :, 0:s], ALU.subtract)
                    G.tensor_tensor(o[:, :, s:2 * s], b[:, :, s:2 * s], mid, ALU.subtract)
                G.tensor_tensor(EX[:, S_STATE], bsum[:, :, P - 1:P].broadcast_to([P, FT, P]), bsum[:, :, :],
                                ALU.subtract)
                b = lsum[:, :, :].rearrange("p f (b c) -> p (f b) c", c=LEAF)
                G.tensor_tensor(EX[:, S_LEAFQ].rearrange("p f (b c) -> p (f b) c", c=LEAF), b,
                                b[:, :, LEAF // 2 - 1:LEAF // 2].broadcast_to([P, FT * P // LEAF, LEAF]),
                                ALU.subtract).then_inc(pool_g.sem, 1)

            def gates_over_sums(t):
                dve_w.wait(pool, "rden", t)
                pj.wait_freed(pool, "sg", t)
                g = gates[:, 512:1024].rearrange("p (h c) -> p h c", h=8)
                G.tensor_tensor(g, g, bcast(wst[:, 5, :], 2, HD), ALU.mult).then_inc(pool_w.sem, 1)

            def body(t):
                differences(t)
                gates_over_sums(t)

            iterations(pool, body)


def _columns():
    import numpy as np
    heads = np.concatenate([np.arange(HD) + HD * (GRP * kv + f) for f in range(GRP) for kv in range(KVH)])
    gq, gk, gv, gg, low, sq, sk, sv, sg = np.split(
        np.arange(IN_W), np.cumsum([256, 256, 512, 512, 16, 512, 128, 128]))
    return [np.concatenate([gq, gk]), sq[heads], np.concatenate([sk, sv, low]), gv, gg, sg[heads]], heads


def kernel(**inputs):
    import numpy as np
    import ml_dtypes
    import concourse.bacc as _bacc
    from concourse.bass_utils import run_bass_kernel_spmd as _run

    a = {k: np.asarray(v) for k, v in inputs.items()}
    cols, heads = _columns()
    x, xs = a["x_prompt"][0], a["x_sample"][:, 0]
    w_in, w_out = a["w_in"][0], a["w_out"][0]
    w_out = np.concatenate([w_out[:512], w_out[512 + heads]])
    rows = lambda w: w.reshape(DT, P, -1).transpose(1, 0, 2).reshape(P, -1)
    half = D // OUT_GROUPS
    w_all = np.concatenate([rows(w_in[:, c]) for c in cols]
                           + [rows(w_out[:, g * half:g * half + half]) for g in range(OUT_GROUPS)], axis=1)
    head_of = np.array([GRP * kv + f for f in range(GRP) for kv in range(KVH)])
    tok = np.arange(P)
    same = tok[:, None] // LEAF == tok[None, :] // LEAF
    leaf = (same & (tok[:, None] <= tok[None, :])).astype(np.float32)
    lvl = np.zeros((P, len(LEVELS), P // 2), np.float32)
    for i, s in enumerate(LEVELS):
        pair = np.arange(P // 2) // s
        lvl[:, i] = (tok[:, None] // (2 * s) == pair[None, :]) & (tok[:, None] % (2 * s) < s)
    scan = np.ones((P, 2, P), np.float32)
    scan[:, 1, ::LEAF] = 0.0
    key = np.arange(2 * P)[None, :]
    ok = (tok[:, None] + P - key >= 0) & (tok[:, None] + P - key < P)
    band = np.stack([np.where(ok, 0.0, -1e30), np.where(ok & (key >= P), 0.0, -1e30)], 1)
    arrays = {
        "xT": x.reshape(NT, P, DT, P).transpose(0, 3, 2, 1),
        "xq": x.reshape(NT, P, D),
        "xsT": xs.reshape(NS, DT, P).transpose(2, 1, 0),
        "xs": xs,
        "w": w_all,
        "gin": a["norm_in"][0].reshape(DT, P).T,
        "gout": np.concatenate([np.repeat(a["gla_norm"][0][:, None], HG, 1), np.ones((P, HG), np.float32)], 1),
        "wgu": a["w_gate_up"][0],
        "bg": a["b_gate"][0].reshape(FT, P).T,
        "sink": np.broadcast_to(a["attn_sinks"][0][head_of], (P, 8)),
        "normf": np.broadcast_to(a["norm_f"], (P, D)),
        "state": a["state_gla"][0].reshape(NS, FT, 2, DK, DV).transpose(2, 3, 0, 1, 4).reshape(P, NS, FT, DV),
        "kcT": np.roll(a["cache_win_k"][0], -1, axis=1).transpose(2, 3, 0, 1).reshape(P, NS, P),
        "vc": a["cache_win_v"][0].transpose(1, 0, 2, 3).reshape(P, NS, P)[1:],
        "sinks_s": a["attn_sinks"][0][:, None],
        "ident": np.eye(P, dtype=np.float32),
        "tri": leaf,
        "lvl": lvl,
        "leafscan": scan,
        "band": band.astype(ml_dtypes.bfloat16),
    }
    outs = [("y", (NT, P, D)), ("ys", (NS, D)), ("Sp", (HG, DK, DV)), ("kp", (KVH, HD, P)), ("vp", (P, P)),
            ("Ss", (P, NS, FT, DV)), ("ksT", (P, NS, P)), ("vs", (P, NS, P))]
    nc = _bacc.Bacc("TRN2", target_bir_lowering=False, num_devices=1)
    maps, args = {}, []
    for name, v in arrays.items():
        v = np.ascontiguousarray(v)
        maps[f"in_{name}"] = v
        args.append(nc.dram_tensor(f"in_{name}", v.shape, mybir.dt.from_np(v.dtype), kind="ExternalInput").ap())
    for name, shape in outs:
        args.append(nc.dram_tensor(f"out_{name}", shape, F32, kind="ExternalOutput").ap())
    hymba_step_kernel(nc, *args)
    res = _run(nc, [maps], core_ids=[0]).results[0]
    y, ys, Sp, kp, vp, Ss, ksT, vs = (np.asarray(res[f"out_{name}"]) for name, _ in outs)
    return (y.reshape(1, SEQ, D),
            ys.reshape(NS, 1, D),
            Sp.reshape(1, 1, HG, DK, DV),
            kp.transpose(2, 0, 1).reshape(1, 1, P, KVH, HD),
            vp.reshape(1, 1, P, KVH, HD),
            Ss.reshape(2, DK, NS, FT, DV).transpose(2, 3, 0, 1, 4).reshape(1, NS, HG, DK, DV),
            ksT.reshape(KVH, HD, NS, P).transpose(2, 3, 0, 1)[None],
            vs.reshape(P, NS, KVH, HD).transpose(1, 0, 2, 3)[None])
```

```python
from contextlib import ExitStack

import concourse.bass as bass
from concourse import mybir

F32 = mybir.dt.float32
F16 = mybir.dt.float16
BF16 = mybir.dt.bfloat16
I32 = mybir.dt.int32
ALU = mybir.AluOpType
ACT = mybir.ActivationFunctionType
AX = mybir.AxisListType

P = 128
D = 1024
DT = D // P
SEQ = 2048
NT = SEQ // P
NS = 8
EPS = 1e-6
TAU = 16.0
HG, DK, DV = 4, 64, 128
FT = HG * DK // P
KVH, GRP, HD = 2, 4, 64
RANK = 16
GROUPS = [("gqk", 512), ("sq", 512), ("sklow", 272), ("gv", 512), ("gg", 512), ("sg", 512)]
COL = {}
_c = 0
for _name, _n in GROUPS:
    COL[_name] = _c
    _c += _n
IN_W = _c
OUT_GROUPS = 2
NG = len(GROUPS) + OUT_GROUPS
LEVELS = (64, 32, 16, 8)
LEAF = 8
LEAF_FLOOR = -20.0
U_SCALE = float(2 ** 10)
W_TOP = float(2 ** 14)
O_TOP = float(2 ** 14)
LOG_EXP_SET = "natural_log_exp_and_others"
DVE_TILES = [4] * 7 + [6]
STAGE_OF = [0, 1, 2, 3, 0, 2, 1, 0]
LOAD_ORDER = [0, 1, 2, 3, 4, 6, 5, 7]
S_LEVEL, S_STATE, S_LEAFK, S_INTER, S_LEAFQ = 0, 4, 5, 6, 7


class Tile:

    def __init__(self, off, j=None):
        self.off, self.j = off, j
        self.p = off % 2

    @property
    def n(self):
        return self.off if self.j is None else self.j * 2 + self.off

    def __add__(self, d):
        return Tile(self.off + d, self.j)

    @property
    def static(self):
        return self.j is None

    @property
    def tokens(self):
        return NS if self.static and self.off == NT else P

    @property
    def sample(self):
        return self.static and self.off == NT


class Events:

    def __init__(self, sem, names):
        self.sem, self.names = sem, names

    def at(self, name, t):
        return t.n * len(self.names) + (self.names.index(name) + 1)

    def wait(self, eng, name, t):
        if not (t.static and t.off < 0):
            eng.wait_ge(self.sem, self.at(name, t))


class Ring:

    def __init__(self, banks, full, freed, order, tail=None):
        self.banks, self.full, self.freed, self.order = banks, full, freed, order
        self.tail = order if tail is None else tail

    def _list(self, t):
        return self.tail if t.sample else self.order

    def _index(self, name, t):
        return [u for u, _ in self._list(t)].index(name)

    def bank(self, name, t):
        return self.banks[(len(self.order) * t.p + self._index(name, t)) % 2]

    def wait_full(self, eng, name, t):
        eng.wait_ge(self.full, t.n * len(self.order) + (self._index(name, t) + 1))

    def wait_freed(self, eng, name, t):
        who = dict(self._list(t))[name]
        total = sum(1 for _, w in self.order if w == who)
        rank = [u for u, w in self._list(t) if w == who].index(name) + 1
        eng.wait_ge(self.freed[who], t.n * total + rank)

    def wait_free(self, eng, name, t):
        i = self._index(name, t)
        if i >= 2:
            self.wait_freed(eng, self._list(t)[i - 2][0], t)
        elif not (t.static and t.off == 0):
            self.wait_freed(eng, self.order[len(self.order) + i - 2][0], t + -1)


def bcast(ap, axis, n):
    ap = ap.unsqueeze(axis)
    shape = list(ap.shape)
    shape[axis] = n
    return ap.broadcast_to(shape)


def hymba_step_kernel(nc, xT_d, xq_d, xsT_d, xs_d, w_d, gin_d, gout_d, wgu_d, bg_d, sink_d, normf_d,
                      state_d, kcT_d, vc_d, sinks_s_d, ident_d, tri_d, lvl_d, leafscan_d, band_d,
                      y_d, ys_d, Sp_d, kp_d, vp_d, Ss_d, ksT_d, vs_d):
    with ExitStack() as ctx:
        def sb(name, shape, dt=F32):
            return ctx.enter_context(nc.sbuf_tensor(name, shape, dt))

        def sem(name):
            return ctx.enter_context(nc.semaphore(name))

        w_region = sb("w_in_hi_lo", [P, DT * IN_W])
        w_half = w_region[:, :].bitcast(F16).rearrange("p (s d c) -> p s d c", s=2, d=DT)
        w_hi, w_lo = w_half[:, 0], w_half[:, 1]
        wo_hi = sb("w_out_hi", [P, DT, D], F16)
        wo_lo = sb("w_out_lo", [P, DT, D], F16)
        xT = sb("xT", [P, DT, P])
        u_hi = sb("u_hi", [P, 2, DT, P], F16)
        u_lo = sb("u_lo", [P, 2, DT, P], F16)
        xq = sb("x_rows", [P, D])
        gq = sb("gla_q", [P, 2, FT, P])
        gk = sb("gla_k", [P, 2, FT, P])
        gv = sb("gla_v", [P, 2, HG * DV])
        sq = sb("win_q", [P, 2, GRP, P])
        kwin = sb("win_k", [P, 2, 2 * P])
        vwin = sb("win_v", [P, 2, 2, P])
        glow = sb("g_low", [P, 2, RANK])
        S_bd = sb("gla_state", [P, FT, 2, DV])
        normf = sb("norm_f", [P, D])
        flex = sb("flex", [P, 8192])
        stage = [flex[:, 4096 * s:4096 * s + 4096] for s in range(2)]
        stage += [w[:, :, :].rearrange("p d c -> p (d c)").bitcast(F32) for w in (wo_hi, wo_lo)]
        at = [0]

        def part(n):
            at[0] += n
            return flex[:, at[0] - n:at[0]]

        xres = part(D)
        EX = part(8 * FT * P).rearrange("p (s f c) -> p s f c", s=8, f=FT)
        QE = part(4 * FT * P).rearrange("p (l f h c) -> p l f h c", l=4, f=FT, h=2)
        assert at[0] == 4096
        gates = part(D)
        QL = part(FT * P).rearrange("p (f c) -> p f c", f=FT)
        AT = part(HG * P).rearrange("p (h c) -> p h c", h=HG)
        PR = part(2 * 2 * 2 * P).rearrange("p (s h c) -> p s h c", s=2, h=2)
        PT = part(2 * 2 * P).rearrange("p (h k c) -> p h k c", h=2, k=2)
        KST = part(HG * DK)
        bsum = part(FT * P).rearrange("p (f c) -> p f c", f=FT)
        assert at[0] <= 8192
        lsum = sb("decay_sum_leaf", [P, FT, P])
        ogT_hi = sb("ogT_hi", [P, DT, P], F16)
        ogT_lo = sb("ogT_lo", [P, DT, P], F16)
        junk = sb("junk", [P, D], BF16)
        glT = sb("g_lowT", [RANK, P])
        ident = sb("ident", [P, P])
        ident_b = sb("ident_bf16", [P, P], BF16)
        band = sb("band_bf16", [P, 2, 2 * P], BF16)
        leafmask = sb("leaf_mask", [P, P])
        lvlmask = sb("level_mask", [P, 4, DK])
        leafscan = sb("leaf_scan", [P, 2, P])
        diag = sb("rstd_diag", [P, P])
        gin = sb("norm_in", [P, DT])
        gout = sb("gla_norm", [P, DT])
        wgu = sb("w_gate_up", [RANK, HG * DK])
        bg = sb("b_gate", [P, FT])
        sink = sb("sinks", [P, 8])
        nsink = sb("neg_sinks", [P, 8])
        wabs = sb("w_abs", [P, 2, DT])
        wcol = sb("w_col", [P, 4])
        gs = sb("w_scale", [P, 2, DT])
        inv = sb("inv_scale", [P, NG])
        invq = sb("inv_scale_q", [P, 2])
        ones = sb("ones", [P, 1])
        xst = sb("x_stat", [P, 2, 8])
        ost = sb("o_stat", [P, 8, HG])
        hst = sb("h_stat", [P, 8])
        wst = sb("win_stat", [P, 6, 8])
        amax = sb("row_max", [P, 4])
        isc = sb("row_unscale", [P, 2])
        dec = sb("chunk_decay", [P, FT])

        banks = [ctx.enter_context(nc.psum_tensor(f"bank{i}", [P, 512], F32)) for i in range(8)]
        accS, accG = banks[6], banks[7]

        const_in = sem("const_in")
        w_in_sem = [sem(f"w_staged_{i}") for i in range(4)]
        xT_in = sem("xT_in")
        xq_in = sem("xq_in")
        xres_in = sem("xres_in")
        y_out = sem("y_out")
        tail_out = sem("tail_out")
        tail_in = sem("tail_in")
        w_row = sem("w_rowmax_done")
        w_max = sem("w_max_done")
        w_scaled = sem("w_scale_done")
        w_dve = sem("w_dve_steps")
        w_hi_done = sem("w_hi_done")
        w_lo_done = sem("w_lo_done")
        w_lo_pool = sem("w_lo_pool")
        w_in_place = sem("w_scaled_in_place")
        w_hi_pool = sem("w_hi_for_pool")
        first_in = sem("first_in")
        ones_set = sem("ones_set")
        init = sem("init_done")
        pj = Ring(banks[0:2], sem("proj_full"), {"act": sem("proj_freed_act"), "dve": sem("proj_freed_dve")},
                  [("bc", "dve"), ("gqk", "act"), ("sq", "act"), ("sklow", "dve"), ("gv", "dve"),
                   ("gg", "act"), ("sg", "act")])
        at_ring = Ring(banks[2:4], sem("attn_full"), {"act": sem("attn_freed_act"), "dve": sem("attn_freed_dve")},
                       [("s0", "act"), ("s1", "act"), ("s2", "act"), ("s3", "act"),
                        ("leaf0", "dve"), ("leaf1", "dve"), ("L1", "dve"), ("L2", "dve"),
                        ("y0", "dve"), ("y1", "dve")],
                       [("y0", "dve"), ("y1", "dve")])
        tr = Ring(banks[4:6], sem("turn_full"), {"act": sem("turn_freed_act"), "dve": sem("turn_freed_dve")},
                  [("glT", "act"), ("z", "dve"), ("pt0", "dve"), ("pt1", "act"), ("pt2", "act"), ("pt3", "act"),
                   ("KST", "act"), ("SU", "dve"), ("og0", "dve"), ("og1", "dve")],
                  [("og0", "dve"), ("og1", "dve")])
        act_u = Events(sem("act_norm"), ["ssq", "ln", "exp", "hi"])
        dve_u = Events(sem("dve_norm"), ["ms", "n0", "n1", "rstd", "diag", "lo"])
        act_g = Events(sem("act_gla"), ["az", "ez", "l1", "E"])
        dve_g = Events(sem("dve_gla"), ["mz", "la", "lc", "scan", "Q", "QF", "L16"])
        pool_g = Events(sem("pool_gla"), ["D"])
        pool_w = Events(sem("pool_win"), ["gs"])
        win_kept = Events(sem("window_kept"), ["win"])
        dve_w = Events(sem("dve_win"), ["mx0", "nm0", "mx1", "nm1", "mx2", "nm2", "mx3", "nm3", "esi", "den", "rden"])
        act_w = Events(sem("act_win"), ["es"])
        pe_pv = Events(sem("pe_pv"), ["pv0", "pv1", "pv2", "pv3"])
        pe_o = Events(sem("pe_gla_out"), ["o"])
        dve_o = Events(sem("dve_out"), ["sg", "amw", "oms", "on0", "on1", "orstd", "gg", "am", "amc", "rsc", "gsc0",
                                        "gsc1", "isc", "hms", "hn0", "hn1", "hr", "y"])
        act_o = Events(sem("act_out"), ["oss", "oln", "oexp", "hi0", "hi1", "hss", "hln", "hexp"])
        smp = {e: sem(f"sample_{e}") for e in ("act", "dve", "pe", "pool")}

        w_at = [0]

        def wpart(n):
            w_at[0] += n
            return w_region[:, w_at[0] - n:w_at[0]]

        s_state = wpart(NS * FT * DV).rearrange("p (b f c) -> p b f c", b=NS, f=FT)
        s_kT = wpart(NS * P).rearrange("p (b c) -> p b c", b=NS)
        s_v = wpart(NS * P).rearrange("p (b c) -> p b c", b=NS)
        s_km = wpart(NS * HG * DK).rearrange("p (b c) -> p b c", b=NS)[0:NS]
        s_kt = wpart(HG * DK)[0:NS]
        s_qm = wpart(HG * NS * NS).rearrange("p (f h b c) -> p f h b c", f=FT, h=2, b=NS)
        s_z = wpart(6 * FT * NS).rearrange("p (s f b) -> p s f b", s=6, f=FT)
        s_qs = wpart(NS * 8).rearrange("p (b h) -> p b h", b=NS)
        s_p = wpart(NS * P).rearrange("p (b c) -> p b c", b=NS)[0:8]
        s_st = wpart(8 * NS).rearrange("p (s b) -> p s b", s=8)[0:8]
        s_pT = wpart(NS * 8).rearrange("p (b h) -> p b h", b=NS)
        s_oT = wpart(GRP * NS).rearrange("p (f b) -> p f b", f=GRP)
        s_sink = sb("sample_sinks", [8, 2])
        s_knew = sb("sample_k_new", [P, NS])
        s_vnew_t = sb("sample_v_new", [NS, P])
        s_vnew = s_vnew_t[:, :]
        SV = {}
        for eng, names in (("act", ["glT", "az", "ez", "l1", "a", "exp"]),
                           ("dve", ["zb", "mz", "la", "kt", "km", "qz", "qm", "kT", "qsz", "qs", "st0", "st1", "st2",
                                    "state", "mx", "nm", "sub", "esi", "sum", "den", "rden", "pn", "pT", "oT"]),
                           ("pe", ["glT", "z", "kt", "kv0", "kv1", "kv2", "kv3", "o", "sc", "pT", "pv", "oT"])):
            for i, name in enumerate(names):
                SV[f"{eng}_{name}"] = i + 1

        def after(eng, step):
            eng.wait_ge(smp[step.split("_")[0]], SV[step])

        def head(u, i):
            return (u // 2 * 2 + i) * KVH + u % 2

        def w_slice(g, w_in, w_out):
            if g < len(GROUPS):
                return w_in[:, :, COL[GROUPS[g][0]]:COL[GROUPS[g][0]] + GROUPS[g][1]]
            c = (g - len(GROUPS)) * D // OUT_GROUPS
            return w_out[:, :, c:c + D // OUT_GROUPS]

        def group_width(g):
            return GROUPS[g][1] if g < len(GROUPS) else D // OUT_GROUPS

        def staged(g):
            return stage[STAGE_OF[g]][:, 0:DT * group_width(g)].rearrange("p (d c) -> p d c", d=DT)

        def wait_staged(eng, g):
            eng.wait_ge(w_in_sem[STAGE_OF[g]], 16 * (STAGE_OF[:g].count(STAGE_OF[g]) + 1))

        block = ctx.enter_context(nc.Block())

        def iterations(eng, body):
            body(Tile(0))
            with eng.Fori(0, (NT - 4) // 2) as j:
                body(Tile(1, j))
                body(Tile(2, j))
            for n in range(NT - 3, NT):
                body(Tile(n))

        @block.sync
        def _(sp):
            def load_x(t):
                n = t.tokens
                if not (t.static and t.off < 1):
                    dve_u.wait(sp, "lo", t + -1)
                if t.sample:
                    sp.dma_start(xT[:, :, 0:n], xsT_d).then_inc(xT_in, 16)
                else:
                    sp.dma_start(xT[:, :, :], xT_d[bass.ds(t.n, 1)].rearrange("a p d c -> (a p) d c")
                                 ).then_inc(xT_in, 16)
                if not (t.static and t.off < 1):
                    act_u.wait(sp, "ssq", t + -1)
                src = xs_d if t.sample else xq_d[bass.ds(t.n, 1)].rearrange("a p c -> (a p) c")
                sp.dma_start(xq[0:n, :], src).then_inc(xq_in, 16)

            def load_w(g):
                n = group_width(g)
                off = DT * (COL[GROUPS[g][0]] if g < len(GROUPS) else IN_W + (g - len(GROUPS)) * D // OUT_GROUPS)
                before = [b for b in range(g) if STAGE_OF[b] == STAGE_OF[g]]
                if before:
                    for split in (w_hi_done, w_lo_done, w_lo_pool):
                        sp.wait_ge(split, before[-1] + 1)
                sp.dma_start(staged(g).rearrange("p d c -> p (d c)"), w_d[:, off:off + DT * n]
                             ).then_inc(w_in_sem[STAGE_OF[g]], 16)

            load_x(Tile(0))
            load_w(0)
            for g in LOAD_ORDER[1:4]:
                load_w(g)
            for dst, src in ((gout[:, :], gout_d), (wgu[:, :], wgu_d), (bg[:, :], bg_d), (sink[:, :], sink_d), (normf[:, :], normf_d),
                             (leafmask[:, :], tri_d), (lvlmask[:, :, :], lvl_d), (leafscan[:, :, :], leafscan_d),
                             (band[:, :, :], band_d), (s_sink[:, 0:1], sinks_s_d)):
                sp.dma_start(dst, src).then_inc(const_in, 16)
            load_x(Tile(1))
            for g in LOAD_ORDER[4:]:
                load_w(g)
            sp.wait_ge(w_lo_done, NG)
            sp.wait_ge(w_lo_pool, NG)
            sp.wait_ge(w_hi_done, NG)

            def body(t):
                n = t.tokens
                if not (t.static and t.off == 0):
                    sp.wait_ge(y_out, t.n * 16)
                sp.dma_start(xres, xq_d[bass.ds(t.n, 1)].rearrange("a p c -> (a p) c")).then_inc(xres_in, 16)
                if not (t.static and t.off + 2 > NT):
                    load_x(t + 2)
                dve_o.wait(sp, "y", t)
                sp.dma_start(y_d[bass.ds(t.n, 1)].rearrange("a p c -> (a p) c"), xres).then_inc(y_out, 16)

            iterations(sp, body)
            last = Tile(NT)
            sp.wait_ge(y_out, NT * 16)
            sp.dma_start(xres[0:NS, :], xs_d).then_inc(xres_in, 16)
            pj.wait_full(sp, "sg", last)
            sp.dma_start(s_state, state_d).then_inc(tail_in, 16)
            sp.dma_start(s_kT, kcT_d).then_inc(tail_in, 16)
            sp.dma_start(s_v[0:P - 1], vc_d).then_inc(tail_in, 16)
            pj.wait_freed(sp, "sklow", last)
            sp.dma_start(s_v[P - 1:P], s_vnew).then_inc(tail_in, 16)
            tr.wait_freed(sp, "SU", Tile(NT - 1))
            for h in range(HG):
                r, f = DK * (h % 2), h // 2
                sp.dma_start(Sp_d[h], S_bd[r:r + DK, f, h % 2, :]).then_inc(tail_out, 16)
            for kv in range(KVH):
                sp.dma_start(kp_d[kv], kwin[HD * kv:HD * kv + HD, (NT - 1) % 2, P:2 * P]).then_inc(tail_out, 16)
            sp.dma_start(vp_d, vwin[:, (NT - 1) % 2, 1, :]).then_inc(tail_out, 16)
            sp.wait_ge(tail_in, 64)
            sp.dma_start(vs_d, s_v).then_inc(tail_out, 16)
            sp.wait_ge(smp["dve"], SV["dve_kT"])
            sp.dma_start(ksT_d, s_kT).then_inc(tail_out, 16)
            sp.wait_ge(smp["dve"], SV["dve_state"])
            sp.dma_start(Ss_d, s_state).then_inc(tail_out, 16)
            dve_o.wait(sp, "y", last)
            sp.dma_start(ys_d, xres[0:NS, :]).then_inc(y_out, 16)
            sp.wait_ge(y_out, 16 * (NT + 1))
            sp.wait_ge(tail_out, 16 * (HG + KVH + 1 + 3))

        @block.tensor
        def _(pe):
            def split_product(out, terms, start=True, stop=True):
                last = len(terms) - 1
                for i, (a_hi, a_lo, b_hi, b_lo) in enumerate(terms):
                    nc.tensor.matmul(out, a_hi, b_hi, start=start and i == 0, stop=False)
                    nc.tensor.matmul(out, a_hi, b_lo, start=False, stop=False)
                    mm = nc.tensor.matmul(out, a_lo, b_hi, start=False, stop=stop and i == last)
                return mm

            def bc(t):
                n = t.tokens
                pj.wait_free(pe, "bc", t)
                dve_u.wait(pe, "diag", t)
                nc.tensor.matmul(pj.bank("bc", t)[:, 0:n], ones[0:n, :].broadcast_to([n, P]), diag[0:n, 0:n],
                                 start=True, stop=True).then_inc(pj.full, 1)

            def features(t, bank, at_, c0, ntile):
                n = t.tokens
                for f in range(ntile):
                    c = c0 + f * P
                    mm = split_product(bank[:, at_ + f * P:at_ + f * P + n],
                                       [(w_hi[:, d, c:c + P], w_lo[:, d, c:c + P],
                                         u_hi[:, t.p, d, 0:n], u_lo[:, t.p, d, 0:n]) for d in range(DT)])
                return mm

            def rows(t, bank, at_, c0, width):
                n = t.tokens
                return split_product(bank[0:n, at_:at_ + width],
                                     [(u_hi[:, t.p, d, 0:n], u_lo[:, t.p, d, 0:n],
                                       w_hi[:, d, c0:c0 + width], w_lo[:, d, c0:c0 + width]) for d in range(DT)])

            def proj(t, name):
                if t.static and t.off == 0:
                    g = [g for g, _ in GROUPS].index(name)
                    pe.wait_ge(w_lo_done, g + 1)
                    pe.wait_ge(w_lo_pool, g + 1)
                pj.wait_free(pe, name, t)
                dve_u.wait(pe, "lo", t)
                bank = pj.bank(name, t)
                if name == "gqk":
                    mm = features(t, bank, 0, COL[name], 4)
                elif name == "sq":
                    mm = features(t, bank, 0, COL[name], 4)
                elif name == "sklow":
                    features(t, bank, 0, COL[name], 1)
                    mm = rows(t, bank, P, COL[name] + P, P + RANK)
                else:
                    mm = rows(t, bank, 0, COL[name], 512)
                mm.then_inc(pj.full, 1)

            def scores(t, pair):
                units = [f"s{2 * pair + h}" for h in range(KVH)]
                for name in units:
                    at_ring.wait_free(pe, name, t)
                if pair == 0:
                    pj.wait_freed(pe, "sq", t)
                    pj.wait_freed(pe, "sklow", t)
                    if not (t.static and t.off == 0):
                        win_kept.wait(pe, "win", t + -1)
                first = 1 if t.static and t.off == 0 else 0
                for name in units:
                    nc.tensor.matmul(at_ring.bank(name, t)[:, :].rearrange("p (h c) -> p h c", h=2), ident_b[:, :],
                                     bcast(band[:, first], 1, 2), start=True, stop=False, skip_group_check=True)
                for i in range(2):
                    for h, name in enumerate(units):
                        r = h * HD
                        mm = nc.tensor.matmul(at_ring.bank(name, t)[:, i * 2 * P:(i + 1) * 2 * P],
                                              sq[r:r + HD, t.p, 2 * pair + i, :], kwin[r:r + HD, t.p, :],
                                              start=False, stop=True, skip_group_check=True)
                        if i == 1:
                            mm.then_inc(at_ring.full, 1)

            def turn_probs(t, u):
                name = f"pt{u}"
                tr.wait_free(pe, name, t)
                at_ring.wait_freed(pe, f"s{u}", t)
                bank = tr.bank(name, t)
                for i in range(2):
                    for kb in range(2):
                        c = (2 * i + kb) * P
                        tp = nc.tensor.transpose(bank[:, c:c + P], PR[:, u % 2, i, kb * P:kb * P + P], ident[:, :])
                tp.then_inc(tr.full, 1)

            def values(t, u):
                if u == 0 and not (t.static and t.off == 0):
                    dve_o.wait(pe, "sg", t + -1)
                tr.wait_freed(pe, f"pt{u}", t)
                h = u % 2
                for i in range(2):
                    c = (u // 2 * 2 + i) * P + h * HD
                    for kb in range(2):
                        mm = nc.tensor.matmul(accS[:, c:c + HD], PT[:, i, kb, :],
                                              vwin[:, t.p, kb, h * HD:h * HD + HD], start=kb == 0, stop=kb == 1)
                mm.then_inc(pe_pv.sem, 1)

            def turn_low(t):
                tr.wait_free(pe, "glT", t)
                pj.wait_freed(pe, "sklow", t)
                nc.tensor.transpose(tr.bank("glT", t)[0:RANK, 0:P], glow[:, t.p, :], ident[:, :]).then_inc(tr.full, 1)

            def gate_up(t):
                tr.wait_free(pe, "z", t)
                tr.wait_freed(pe, "glT", t)
                bank = tr.bank("z", t)
                for f in range(FT):
                    mm = nc.tensor.matmul(bank[:, f * P:f * P + P], wgu[:, f * P:f * P + P], glT[:, :],
                                          start=True, stop=True)
                mm.then_inc(tr.full, 1)

            def leaf_scores(t):
                for h in range(2):
                    at_ring.wait_free(pe, f"leaf{h}", t)
                dve_g.wait(pe, "QF", t)
                for f in range(FT):
                    for h in range(2):
                        r = h * DK
                        mm = nc.tensor.matmul(at_ring.bank(f"leaf{h}", t)[:, f * P:f * P + P],
                                              EX[r:r + DK, S_LEAFK, f, :], QL[r:r + DK, f, :], start=True, stop=True)
                        if f == FT - 1:
                            mm.then_inc(at_ring.full, 1)

            def level_scores(t, name, l0):
                at_ring.wait_free(pe, name, t)
                bank = at_ring.bank(name, t)
                for l in range(2):
                    for f in range(FT):
                        c = (l * FT + f) * P
                        mm = nc.tensor.matmul(bank[:, c:c + P], EX[:, l0 + l, f, :],
                                              QE[:, l0 + l, f].rearrange("p h c -> p (h c)"), start=True, stop=True)
                mm.then_inc(at_ring.full, 1)

            def turn_keys(t):
                tr.wait_free(pe, "KST", t)
                dve_g.wait(pe, "QF", t)
                for f in range(FT):
                    tp = nc.tensor.transpose(tr.bank("KST", t)[:, f * P:f * P + P], EX[:, S_STATE, f, :], ident[:, :])
                tp.then_inc(tr.full, 1)

            def gla_out(t):
                if not (t.static and t.off == 0):
                    dve_o.wait(pe, "gg", t + -1)
                    tr.wait_freed(pe, "SU", t + -1)
                at_ring.wait_freed(pe, "L2", t)
                pj.wait_freed(pe, "gv", t)
                for f in range(FT):
                    nc.tensor.matmul(accG[:, f * 2 * DV:(f + 1) * 2 * DV], EX[:, S_INTER, f, :],
                                     S_bd[:, f].rearrange("p h c -> p (h c)"), start=f == 0, stop=False,
                                     skip_group_check=True)
                for h in range(HG):
                    mm = nc.tensor.matmul(accG[:, h * DV:h * DV + DV], AT[:, h, :],
                                          gv[:, t.p, h * DV:h * DV + DV], start=False, stop=h == HG - 1,
                                          skip_group_check=True)
                mm.then_inc(pe_o.sem, 1)

            def state_update(t):
                tr.wait_free(pe, "SU", t)
                tr.wait_freed(pe, "KST", t)
                bank = tr.bank("SU", t)
                for h in range(HG):
                    r, f = DK * (h % 2), h // 2
                    mm = nc.tensor.matmul(bank[r:r + DK, f * DV:f * DV + DV], KST[:, h * DK:h * DK + DK],
                                          gv[:, t.p, h * DV:h * DV + DV], start=True, stop=True)
                mm.then_inc(tr.full, 1)

            def turn_out(t, g):
                n = t.tokens
                name = f"og{g}"
                tr.wait_free(pe, name, t)
                dve_o.wait(pe, f"gsc{g}", t)
                bank = tr.bank(name, t)
                for k in range(4):
                    c = (4 * g + k) * P
                    tp = nc.tensor.transpose(bank[:, k * P:k * P + n], gates[0:n, c:c + P], ident[0:n, 0:n])
                tp.then_inc(tr.full, 1)

            def out_proj(t, g):
                n = t.tokens
                name = f"y{g}"
                at_ring.wait_free(pe, name, t)
                if g == 0:
                    tr.wait_freed(pe, "og1", t)
                    if t.static and t.off == 0:
                        pe.wait_ge(w_lo_done, NG)
                        pe.wait_ge(w_lo_pool, NG)
                c = g * D // OUT_GROUPS
                split_product(at_ring.bank(name, t)[0:n, :],
                              [(ogT_hi[:, f, 0:n], ogT_lo[:, f, 0:n], wo_hi[:, f, c:c + 512], wo_lo[:, f, c:c + 512])
                               for f in range(DT)]).then_inc(at_ring.full, 1)

            def sample():
                t = Tile(NT)
                p = t.p
                pj.wait_freed(pe, "sg", t)
                pj.wait_freed(pe, "gv", t)
                nc.tensor.transpose(banks[0][0:RANK, 0:NS], glow[0:NS, p, :], ident[0:NS, 0:NS]
                                    ).then_inc(smp["pe"], 1)
                after(pe, "act_glT")
                for f in range(FT):
                    mm = nc.tensor.matmul(banks[1][:, f * NS:f * NS + NS], wgu[:, f * P:f * P + P], glT[:, 0:NS],
                                          start=True, stop=True)
                mm.then_inc(smp["pe"], 1)
                for f in range(FT):
                    tp = nc.tensor.transpose(banks[0][0:NS, f * P:f * P + P], gk[:, p, f, 0:NS], ident[:, :])
                tp.then_inc(smp["pe"], 1)
                after(pe, "dve_km")
                for r in range(4):
                    if r >= 2:
                        after(pe, f"dve_st{r - 2}")
                    for b in range(2):
                        for h in range(HG):
                            c = (2 * b + h // 2) * DV
                            o = DK * (h % 2)
                            mm = nc.tensor.matmul(banks[r % 2][o:o + DK, c:c + DV],
                                                  s_km[:, 2 * r + b, h * DK:h * DK + DK],
                                                  gv[0:NS, p, h * DV:h * DV + DV], start=True, stop=True)
                    mm.then_inc(smp["pe"], 1)
                after(pe, "dve_state")
                dve_o.wait(pe, "gg", Tile(NT - 1))
                for h in range(HG):
                    for b in range(NS):
                        mm = nc.tensor.matmul(accG[0:NS, h * DV:h * DV + DV], s_qm[:, h // 2, h % 2, b, :],
                                              s_state[:, b, h // 2, :], start=b == 0, stop=b == NS - 1)
                mm.then_inc(smp["pe"], 1)
                for b in range(NS):
                    c = (b % 4) * P
                    mm = nc.tensor.matmul(banks[b // 4][0:8, c:c + P], s_qs[:, b, :], s_kT[:, b, :],
                                          start=True, stop=True)
                mm.then_inc(smp["pe"], 1)
                after(pe, "dve_pn")
                for b in range(NS):
                    tp = nc.tensor.transpose(banks[0][:, 8 * b:8 * b + 8], s_p[:, b, :], ident[0:8, 0:8])
                tp.then_inc(smp["pe"], 1)
                after(pe, "dve_pT")
                for b in range(NS):
                    mm = nc.tensor.matmul(banks[1][:, 8 * b:8 * b + 8], s_v[:, b, :], s_pT[:, b, :],
                                          start=True, stop=True)
                mm.then_inc(smp["pe"], 1)
                after(pe, "dve_oT")
                dve_o.wait(pe, "sg", Tile(NT - 1))
                for f in range(GRP):
                    tp = nc.tensor.transpose(accS[0:NS, f * P:f * P + P], s_oT[:, f, :], ident[:, :])
                tp.then_inc(smp["pe"], 1)

            pe.wait_ge(ones_set, 1)
            bc(Tile(0))
            for name, _ in GROUPS:
                proj(Tile(0), name)
            bc(Tile(1))
            pe.wait_ge(init, 1)

            def body(t):
                nxt = t + 1
                turn_low(t)
                proj(nxt, "gqk")
                gate_up(t)
                scores(t, 0)
                proj(nxt, "sq")
                turn_probs(t, 0)
                turn_probs(t, 1)
                scores(t, 1)
                values(t, 0)
                proj(nxt, "sklow")
                values(t, 1)
                turn_probs(t, 2)
                turn_probs(t, 3)
                leaf_scores(t)
                values(t, 2)
                level_scores(t, "L1", 0)
                values(t, 3)
                level_scores(t, "L2", 2)
                turn_keys(t)
                proj(nxt, "gv")
                gla_out(t)
                state_update(t)
                proj(nxt, "gg")
                turn_out(t, 0)
                turn_out(t, 1)
                proj(nxt, "sg")
                if not (t.static and t.off + 2 > NT):
                    bc(t + 2)
                out_proj(t, 0)
                out_proj(t, 1)

            iterations(pe, body)
            sample()
            turn_out(Tile(NT), 0)
            turn_out(Tile(NT), 1)
            out_proj(Tile(NT), 0)
            out_proj(Tile(NT), 1)

        @block.scalar
        def _(act):
            def square_rows(t):
                n, s = t.tokens, xst[0:t.tokens, t.p]
                act.wait_ge(xq_in, (t.n + 1) * 16)
                nc.scalar.activation(xq[0:n, :], xq[0:n, :], ACT.Square, accum_out=s[:, 0:1]).then_inc(act_u.sem, 1)

            def norm_rows(t):
                s = xst[0:t.tokens, t.p]
                dve_u.wait(act, "ms", t)
                nc.scalar.activation(s[:, 2:3], s[:, 1:2], ACT.Ln).then_inc(act_u.sem, 1)
                act_u.wait(act, "ln", t)
                nc.scalar.activation(s[:, 3:4], s[:, 2:3], ACT.Exp, scale=-0.5).then_inc(act_u.sem, 1)

            def split_u(t):
                n = t.tokens
                pj.wait_freed(act, "bc", t)
                if not (t.static and t.off < 2):
                    pj.wait_full(act, "sg", t + -2)
                nc.scalar.copy(u_hi[:, t.p, :, 0:n], xT[:, :, 0:n]).then_inc(act_u.sem, 1)

            def take_qk(t):
                n = t.tokens
                pj.wait_full(act, "gqk", t)
                bank = pj.bank("gqk", t)[:, :].rearrange("p (f c) -> p f c", f=4)
                nc.scalar.activation(gq[:, t.p, :, 0:n], bank[:, 0:2, 0:n], ACT.Identity, scale=invq[:, 0:1])
                nc.scalar.activation(gk[:, t.p, :, 0:n], bank[:, 2:4, 0:n], ACT.Identity,
                                     scale=inv[:, 0:1]).then_inc(pj.freed["act"], 1)

            def take_sq(t):
                n = t.tokens
                pj.wait_full(act, "sq", t)
                bank = pj.bank("sq", t)[:, :].rearrange("p (f c) -> p f c", f=4)
                nc.scalar.activation(sq[:, t.p, :, 0:n], bank[:, :, 0:n], ACT.Identity,
                                     scale=invq[:, 1:2]).then_inc(pj.freed["act"], 1)

            def take_gate(t, g):
                n, name = t.tokens, ("gg", "sg")[g]
                pj.wait_full(act, name, t)
                if g == 0 and not (t.static and t.off == 0):
                    tr.wait_full(act, "og1", t + -1)
                nc.scalar.activation(gates[0:n, g * 512:g * 512 + 512], pj.bank(name, t)[0:n, :], ACT.Silu,
                                     scale=inv[0:n, 4 + g:5 + g]).then_inc(pj.freed["act"], 1)

            def take_low(t):
                tr.wait_full(act, "glT", t)
                nc.scalar.copy(glT[:, :], tr.bank("glT", t)[0:RANK, 0:P]).then_inc(tr.freed["act"], 1)

            def log_gate(t):
                tr.wait_freed(act, "z", t)
                nc.scalar.activation(EX[:, 1], EX[:, 0], ACT.Abs).then_inc(act_g.sem, 1)
                act_g.wait(act, "az", t)
                nc.scalar.activation(EX[:, 1], EX[:, 1], ACT.Exp, scale=-1.0).then_inc(act_g.sem, 1)
                act_g.wait(act, "ez", t)
                nc.scalar.activation(EX[:, 1], EX[:, 1], ACT.Ln, bias=1.0).then_inc(act_g.sem, 1)

            def decays(t):
                dve_g.wait(act, "scan", t)
                nc.scalar.activation(EX[:, S_INTER], bsum[:, :, :], ACT.Exp, scale=1 / TAU)
                nc.scalar.activation(dec[:, :].unsqueeze(2), bsum[:, :, P - 1:P], ACT.Exp, scale=1 / TAU)
                pool_g.wait(act, "D", t)
                nc.scalar.activation(EX[:, S_LEAFK], EX[:, S_LEAFQ], ACT.Exp, scale=-1 / TAU)
                nc.scalar.activation(EX[:, 0:5], EX[:, 0:5], ACT.Exp, scale=1 / TAU)
                nc.scalar.activation(EX[:, S_LEAFQ], EX[:, S_LEAFQ], ACT.Exp, scale=1 / TAU).then_inc(act_g.sem, 1)

            def probs(t, f):
                name = f"s{f}"
                bank = at_ring.bank(name, t)
                dve_w.wait(act, f"nm{f}", t)
                if f >= 2:
                    tr.wait_full(act, f"pt{f - 2}", t)
                elif not (t.static and t.off == 0):
                    tr.wait_full(act, f"pt{f + 2}", t + -1)
                for i in range(2):
                    k = head(f, i)
                    e = nc.scalar.activation(PR[:, f % 2, i, :], bank[:, i * 2 * P:(i + 1) * 2 * P], ACT.Exp,
                                             bias=wst[:, 0, k:k + 1], accum_out=wst[:, 1, k:k + 1])
                e.then_inc(at_ring.freed["act"], 1)

            def take_pt(t, f):
                tr.wait_full(act, f"pt{f}", t)
                pe_pv.wait(act, f"pv{f - 1}", t)
                nc.scalar.copy(PT[:, :, :, :].rearrange("p a b c -> p (a b c)"),
                               tr.bank(f"pt{f}", t)[:, :]).then_inc(tr.freed["act"], 1)

            def sink_term(t):
                dve_w.wait(act, "esi", t)
                nc.scalar.activation(wst[:, 2, :], wst[:, 2, :], ACT.Exp).then_inc(act_w.sem, 1)

            def take_kst(t):
                tr.wait_full(act, "KST", t)
                nc.scalar.copy(KST[:, :], tr.bank("KST", t)[:, 0:2 * P]).then_inc(tr.freed["act"], 1)

            def head_norm(t):
                n = t.tokens
                if t.sample:
                    act.wait_ge(smp["pe"], SV["pe_o"])
                else:
                    pe_o.wait(act, "o", t)
                for h in range(HG):
                    sq_ = nc.scalar.activation(junk[0:n, h * DV:h * DV + DV], accG[0:n, h * DV:h * DV + DV], ACT.Square,
                                               accum_out=ost[0:n, 0, h:h + 1])
                sq_.then_inc(act_o.sem, 1)
                dve_o.wait(act, "oms", t)
                nc.scalar.activation(ost[0:n, 2, :], ost[0:n, 1, :], ACT.Ln).then_inc(act_o.sem, 1)
                act_o.wait(act, "oln", t)
                nc.scalar.activation(ost[0:n, 3, :], ost[0:n, 2, :], ACT.Exp, scale=-0.5).then_inc(act_o.sem, 1)

            def take_out(t, g):
                n = t.tokens
                tr.wait_full(act, f"og{g}", t)
                bank = tr.bank(f"og{g}", t)[:, :].rearrange("p (f c) -> p f c", f=4)
                nc.scalar.copy(ogT_hi[:, 4 * g:4 * g + 4, 0:n], bank[:, :, 0:n]).then_inc(act_o.sem, 1)

            def final_norm(t):
                n = t.tokens
                at_ring.wait_freed(act, "y1", t)
                nc.scalar.activation(junk[0:n, :], xres[0:n, :], ACT.Square, accum_out=hst[0:n, 0:1]
                                     ).then_inc(act_o.sem, 1)
                dve_o.wait(act, "hms", t)
                nc.scalar.activation(hst[0:n, 2:3], hst[0:n, 1:2], ACT.Ln).then_inc(act_o.sem, 1)
                act_o.wait(act, "hln", t)
                nc.scalar.activation(hst[0:n, 3:4], hst[0:n, 2:3], ACT.Exp, scale=-0.5).then_inc(act_o.sem, 1)

            def split_w(g):
                act.wait_ge(w_scaled, g + 1)
                if g == len(GROUPS):
                    act.wait_ge(w_lo_done, g)
                    act.wait_ge(w_lo_pool, g)
                src, hi = staged(g), w_slice(g, w_hi, wo_hi)
                for d in range(DVE_TILES[g]):
                    h = nc.scalar.activation(hi[:, d], src[:, d], ACT.Identity, scale=gs[:, g % 2, d:d + 1])
                h.then_inc(w_hi_done, 1)
                for d in range(DVE_TILES[g], DT):
                    h = nc.scalar.activation(src[:, d], src[:, d], ACT.Identity, scale=gs[:, g % 2, d:d + 1])
                h.then_inc(w_in_place, 1)
                act.wait_ge(w_in_place, g + 1)
                nc.scalar.copy(hi[:, DVE_TILES[g]:DT], src[:, DVE_TILES[g]:DT]).then_inc(w_hi_pool, 1)

            def sample():
                t = Tile(NT)
                after(act, "pe_glT")
                nc.scalar.copy(glT[:, 0:NS], banks[0][0:RANK, 0:NS]).then_inc(smp["act"], 1)
                after(act, "dve_zb")
                nc.scalar.activation(s_z[:, 1], s_z[:, 0], ACT.Abs).then_inc(smp["act"], 1)
                after(act, "act_az")
                nc.scalar.activation(s_z[:, 1], s_z[:, 1], ACT.Exp, scale=-1.0).then_inc(smp["act"], 1)
                after(act, "act_ez")
                nc.scalar.activation(s_z[:, 1], s_z[:, 1], ACT.Ln, bias=1.0).then_inc(smp["act"], 1)
                after(act, "dve_la")
                nc.scalar.activation(s_z[:, 4], s_z[:, 3], ACT.Exp, scale=1 / TAU).then_inc(smp["act"], 1)
                after(act, "dve_esi")
                nc.scalar.activation(s_p, s_p, ACT.Exp)
                nc.scalar.activation(s_st[:, 3, :], s_st[:, 2, :], ACT.Exp).then_inc(smp["act"], 1)

            for dst, src in ((ident[:, :], ident_d), (gin[:, :], gin_d)):
                act.dma_start(dst, src).then_inc(first_in, 16)
            nc.scalar.preload_act_table_set(LOG_EXP_SET)
            square_rows(Tile(0))
            norm_rows(Tile(0))
            split_u(Tile(0))
            for g in range(NG):
                split_w(g)
                if g == 1:
                    square_rows(Tile(1))
                    norm_rows(Tile(1))
                if g == 1:
                    take_qk(Tile(0))
                if g == 2:
                    take_sq(Tile(0))
            act.wait_ge(w_lo_done, NG - 1)
            act.wait_ge(w_lo_pool, NG - 1)
            take_gate(Tile(0), 0)
            take_gate(Tile(0), 1)
            nc.scalar.preload_act_table_set(LOG_EXP_SET)
            split_u(Tile(1))

            def body(t):
                nxt = t + 1
                take_low(t)
                take_qk(nxt)
                log_gate(t)
                probs(t, 0)
                probs(t, 1)
                take_sq(nxt)
                decays(t)
                probs(t, 2)
                take_pt(t, 1)
                probs(t, 3)
                take_pt(t, 2)
                take_pt(t, 3)
                sink_term(t)
                take_kst(t)
                if not (t.static and t.off + 2 > NT):
                    square_rows(t + 2)
                head_norm(t)
                take_out(t, 0)
                take_out(t, 1)
                if not (t.static and t.off + 2 > NT):
                    norm_rows(t + 2)
                take_gate(nxt, 0)
                take_gate(nxt, 1)
                nc.scalar.preload_act_table_set(LOG_EXP_SET)
                if not (t.static and t.off + 2 > NT):
                    split_u(t + 2)
                final_norm(t)

            iterations(act, body)
            sample()
            head_norm(Tile(NT))
            take_out(Tile(NT), 0)
            take_out(Tile(NT), 1)
            final_norm(Tile(NT))

        @block.vector
        def _(dve):
            V = nc.vector

            def rsqrt_step(ev, names, a, y0, tmp, y, t, gain=1.0):
                V.tensor_tensor(tmp, y0, y0, ALU.mult).then_inc(ev.sem, 1)
                ev.wait(dve, names[0], t)
                V.scalar_tensor_tensor(out=tmp, in0=tmp, scalar=-0.5 * gain, in1=a, op0=ALU.mult,
                                       op1=ALU.mult).then_inc(ev.sem, 1)
                ev.wait(dve, names[1], t)
                V.scalar_tensor_tensor(out=y, in0=tmp, scalar=1.5 * gain, in1=y0, op0=ALU.add,
                                       op1=ALU.mult).then_inc(ev.sem, 1)
                ev.wait(dve, names[2], t)

            def mean_square(t):
                s = xst[0:t.tokens, t.p]
                act_u.wait(dve, "ssq", t)
                V.tensor_scalar(s[:, 1:2], s[:, 0:1], 1.0 / D, EPS, ALU.mult, ALU.add).then_inc(dve_u.sem, 1)

            def norm_x(t):
                n, s = t.tokens, xst[0:t.tokens, t.p]
                act_u.wait(dve, "exp", t)
                rsqrt_step(dve_u, ["n0", "n1", "rstd"], s[:, 1:2], s[:, 3:4], s[:, 4:5], s[:, 5:6], t, U_SCALE)
                if not (t.static and t.off == 0):
                    pj.wait_full(dve, "bc", t + -1)
                V.tensor_scalar(diag[0:n, 0:n], ident[0:n, 0:n], s[:, 5:6], None, ALU.mult).then_inc(dve_u.sem, 1)

            def scale_u(t):
                n = t.tokens
                dve.wait_ge(xT_in, (t.n + 1) * 16)
                pj.wait_full(dve, "bc", t)
                V.tensor_tensor(xT[:, :, 0:n], xT[:, :, 0:n], bcast(pj.bank("bc", t)[:, 0:n], 1, DT),
                                ALU.mult).then_inc(pj.freed["dve"], 1)

            def split_u(t):
                n = t.tokens
                act_u.wait(dve, "hi", t)
                V.tensor_tensor(u_lo[:, t.p, :, 0:n], xT[:, :, 0:n], u_hi[:, t.p, :, 0:n],
                                ALU.subtract).then_inc(dve_u.sem, 1)

            def take_kv(t):
                n = t.tokens
                pj.wait_full(dve, "sklow", t)
                bank = pj.bank("sklow", t)
                if t.sample:
                    V.tensor_scalar(s_knew[:, :], bank[:, 0:n], inv[:, 2:3], None, ALU.mult)
                    V.tensor_scalar(s_vnew, bank[0:n, P:2 * P], inv[0:n, 2:3], None, ALU.mult)
                else:
                    V.tensor_scalar(kwin[:, t.p, P:2 * P], bank[:, 0:P], inv[:, 2:3], None, ALU.mult)
                    V.tensor_scalar(vwin[:, t.p, 1, :], bank[:, P:2 * P], inv[:, 2:3], None, ALU.mult)
                V.tensor_scalar(glow[0:n, t.p, :], bank[0:n, 2 * P:2 * P + RANK], inv[0:n, 2:3], None,
                                ALU.mult).then_inc(pj.freed["dve"], 1)

            def take_gv(t):
                n = t.tokens
                pj.wait_full(dve, "gv", t)
                V.tensor_scalar(gv[0:n, t.p, :], pj.bank("gv", t)[0:n, :], inv[0:n, 3:4], None,
                                ALU.mult).then_inc(pj.freed["dve"], 1)

            def take_z(t):
                tr.wait_full(dve, "z", t)
                bank = tr.bank("z", t)
                for f in range(FT):
                    z = V.tensor_scalar(EX[:, 0, f, :], bank[:, f * P:f * P + P], bg[:, f:f + 1], None, ALU.add)
                z.then_inc(tr.freed["dve"], 1)
                tr.wait_freed(dve, "z", t)
                V.tensor_scalar(EX[:, 2], EX[:, 0], 0.0, None, ALU.min).then_inc(dve_g.sem, 1)

            def sums(t):
                act_g.wait(dve, "l1", t)
                dve_g.wait(dve, "mz", t)
                V.tensor_tensor(EX[:, 2], EX[:, 2], EX[:, 1], ALU.subtract).then_inc(dve_g.sem, 1)
                dve_g.wait(dve, "la", t)
                V.tensor_scalar(EX[:, 3], EX[:, 2], LEAF_FLOOR * TAU, None, ALU.max).then_inc(dve_g.sem, 1)
                dve_g.wait(dve, "lc", t)
                for f in range(FT):
                    V.tensor_tensor_scan(bsum[:, f, :], leafscan[:, 0, :], EX[:, 2, f, :], 0.0, ALU.mult, ALU.add)
                    sc = V.tensor_tensor_scan(lsum[:, f, :], leafscan[:, 1, :], EX[:, 3, f, :], 0.0, ALU.mult, ALU.add)
                sc.then_inc(dve_g.sem, 1)

            def factors(t):
                act_g.wait(dve, "E", t)
                for l, s in enumerate(LEVELS):
                    for h in range(2):
                        r = h * DK
                        late = lambda ap: ap.rearrange("p f (b c) -> p f b c", c=2 * s)[:, :, :, s:2 * s]
                        V.tensor_tensor(QE[r:r + DK, l, :, h, :].rearrange("p f (b c) -> p f b c", c=s),
                                        late(gq[r:r + DK, t.p]), late(EX[r:r + DK, l]), ALU.mult)
                V.tensor_tensor(QL, gq[:, t.p], EX[:, S_LEAFQ], ALU.mult)
                V.tensor_tensor(EX[:, S_INTER], EX[:, S_INTER], gq[:, t.p], ALU.mult).then_inc(dve_g.sem, 1)
                dve_g.wait(dve, "Q", t)
                V.tensor_tensor(EX[:, 0:6], EX[:, 0:6], bcast(gk[:, t.p], 1, 6), ALU.mult).then_inc(dve_g.sem, 1)

            def assemble_leaves(t):
                for h in range(2):
                    at_ring.wait_full(dve, f"leaf{h}", t)
                    V.tensor_tensor(heads_of(h), at_ring.bank(f"leaf{h}", t)[:, 0:FT * P].rearrange(
                        "p (f c) -> p f c", f=FT), bcast(leafmask[:, :], 1, FT), ALU.mult
                                    ).then_inc(at_ring.freed["dve"], 1)

            def assemble_levels(t):
                at_ring.wait_freed(dve, "leaf1", t)
                at_ring.wait_full(dve, "L1", t)
                lv = at_ring.bank("L1", t)[:, :].rearrange("p (l h c) -> p l h c", l=2, h=HG)
                V.tensor_copy(AT[0:64, :, 64:128], lv[0:64, 0])
                V.tensor_copy(AT[0:32, :, 32:64], lv[0:32, 1, :, 0:32])
                V.tensor_copy(AT[64:96, :, 96:128], lv[64:96, 1, :, 32:64]).then_inc(at_ring.freed["dve"], 1)
                at_ring.wait_freed(dve, "L1", t)
                at_ring.wait_full(dve, "L2", t)
                if not (t.static and t.off == 0):
                    pe_pv.wait(dve, "pv3", t + -1)
                V.tensor_copy(kwin[:, 1 - t.p, 0:P], kwin[:, t.p, P:2 * P])
                masked_copy(t, 2).then_inc(dve_g.sem, 1)
                dve_g.wait(dve, "L16", t)
                V.tensor_copy(vwin[:, 1 - t.p, 0, :], vwin[:, t.p, 1, :]).then_inc(win_kept.sem, 1)
                masked_copy(t, 3).then_inc(at_ring.freed["dve"], 1)

            def heads_of(h):
                return AT.rearrange("p (f h) c -> p f h c", h=2)[:, :, h, :]

            def masked_copy(t, l):
                s = LEVELS[l]
                return V.copy_predicated(
                    AT.rearrange("p h (b c) -> p h b c", c=2 * s)[:, :, :, s:2 * s],
                    bcast(lvlmask[:, l, :].bitcast(I32).rearrange("p (b c) -> p b c", c=s), 1, HG),
                    at_ring.bank("L2", t)[:, (l - 2) * 256:(l - 1) * 256].rearrange(
                        "p (h b c) -> p h b c", h=HG, c=s))

            def update_state(t):
                tr.wait_full(dve, "SU", t)
                bank = tr.bank("SU", t)
                for h in range(HG):
                    r, f = DK * (h % 2), h // 2
                    s = S_bd[r:r + DK, f, h % 2, :]
                    up = V.scalar_tensor_tensor(out=s, in0=s, scalar=dec[r:r + DK, f:f + 1],
                                                in1=bank[r:r + DK, f * DV:f * DV + DV], op0=ALU.mult, op1=ALU.add)
                up.then_inc(tr.freed["dve"], 1)

            def row_max(t, f):
                at_ring.wait_full(dve, f"s{f}", t)
                k = head(f, 0)
                V.tensor_reduce(wst[:, 3, k:k + 3:2],
                                at_ring.bank(f"s{f}", t)[:, :].rearrange("p (h c) -> p h c", h=2),
                                AX.X, ALU.max, negate=True).then_inc(dve_w.sem, 1)
                dve_w.wait(dve, f"mx{f}", t)
                V.tensor_tensor(wst[:, 0, k:k + 3:2], wst[:, 3, k:k + 3:2], nsink[:, k:k + 3:2],
                                ALU.min).then_inc(dve_w.sem, 1)

            def take_pt(t, f):
                tr.wait_full(dve, f"pt{f}", t)
                if f > 0:
                    pe_pv.wait(dve, f"pv{f - 1}", t)
                elif not (t.static and t.off == 0):
                    pe_pv.wait(dve, "pv3", t + -1)
                V.tensor_copy(PT[:, :, :, :].rearrange("p a b c -> p (a b c)"),
                              tr.bank(f"pt{f}", t)[:, :]).then_inc(tr.freed["dve"], 1)

            def denominators(t):
                dve_w.wait(dve, "nm3", t)
                V.tensor_tensor(wst[:, 2, :], wst[:, 0, :], sink[:, :], ALU.add).then_inc(dve_w.sem, 1)
                act_w.wait(dve, "es", t)
                V.tensor_tensor(wst[:, 4, :], wst[:, 1, :], wst[:, 2, :], ALU.add).then_inc(dve_w.sem, 1)
                dve_w.wait(dve, "den", t)
                V.reciprocal(wst[:, 5, :], wst[:, 4, :]).then_inc(dve_w.sem, 1)

            def gate_window(t):
                n = t.tokens
                if t.sample:
                    dve.wait_ge(smp["pe"], SV["pe_oT"])
                    pj.wait_freed(dve, "sg", t)
                else:
                    pool_w.wait(dve, "gs", t)
                    pe_pv.wait(dve, "pv3", t)
                V.tensor_tensor(gates[0:n, 512:1024], gates[0:n, 512:1024], accS[0:n, :], ALU.mult
                                ).then_inc(dve_o.sem, 1)
                dve_o.wait(dve, "sg", t)
                V.tensor_reduce(amax[0:n, 0:1], gates[0:n, 512:1024], AX.X, ALU.max, apply_absolute_value=True
                                ).then_inc(dve_o.sem, 1)

            def mean_heads(t):
                o = ost[0:t.tokens]
                act_o.wait(dve, "oss", t)
                V.tensor_scalar(o[:, 1, :], o[:, 0, :], 1.0 / DV, EPS, ALU.mult, ALU.add).then_inc(dve_o.sem, 1)

            def gate_gla(t):
                n = t.tokens
                o = ost[0:n]
                act_o.wait(dve, "oexp", t)
                rsqrt_step(dve_o, ["on0", "on1", "orstd"], o[:, 1, :], o[:, 3, :], o[:, 4, :], o[:, 5, :], t)
                pj.wait_freed(dve, "gg", t)
                for h in range(HG):
                    g = gates[0:n, h * DV:h * DV + DV]
                    gg = V.scalar_tensor_tensor(out=g, in0=accG[0:n, h * DV:h * DV + DV], scalar=o[:, 5, h:h + 1],
                                                in1=g, op0=ALU.mult, op1=ALU.mult)
                gg.then_inc(dve_o.sem, 1)

            def scale_rows(t):
                n = t.tokens
                a = amax[0:n]
                dve_o.wait(dve, "gg", t)
                V.tensor_reduce(a[:, 1:2], gates[0:n, 0:512], AX.X, ALU.max, apply_absolute_value=True
                                ).then_inc(dve_o.sem, 1)
                dve_o.wait(dve, "am", t)
                V.tensor_scalar(a[:, 2:3], a[:, 0:1], a[:, 1:2], 1e-30, ALU.max, ALU.max).then_inc(dve_o.sem, 1)
                dve_o.wait(dve, "amc", t)
                V.reciprocal(a[:, 3:4], a[:, 2:3]).then_inc(dve_o.sem, 1)
                dve_o.wait(dve, "rsc", t)
                for g in range(2):
                    c = g * 512
                    V.tensor_scalar(gates[0:n, c:c + 512], gates[0:n, c:c + 512], a[:, 3:4], O_TOP, ALU.mult,
                                    ALU.mult).then_inc(dve_o.sem, 1)
                V.tensor_scalar(isc[0:n, :], inv[0:n, NG - 2:NG], a[:, 2:3], 1.0 / O_TOP, ALU.mult, ALU.mult
                                ).then_inc(dve_o.sem, 1)

            def take_out(t, g):
                n = t.tokens
                act_o.wait(dve, f"hi{g}", t)
                bank = tr.bank(f"og{g}", t)[:, :].rearrange("p (f c) -> p f c", f=4)
                V.tensor_tensor(ogT_lo[:, 4 * g:4 * g + 4, 0:n], bank[:, :, 0:n], ogT_hi[:, 4 * g:4 * g + 4, 0:n],
                                ALU.subtract).then_inc(tr.freed["dve"], 1)

            def residual(t):
                n = t.tokens
                dve.wait_ge(xres_in, (t.n + 1) * 16)
                dve_o.wait(dve, "isc", t)
                for g in range(OUT_GROUPS):
                    at_ring.wait_full(dve, f"y{g}", t)
                    x = xres[0:n, g * 512:g * 512 + 512]
                    V.scalar_tensor_tensor(out=x, in0=at_ring.bank(f"y{g}", t)[0:n, :], scalar=isc[0:n, g:g + 1],
                                           in1=x, op0=ALU.mult, op1=ALU.add).then_inc(at_ring.freed["dve"], 1)

            def final_norm(t):
                n = t.tokens
                h = hst[0:n]
                act_o.wait(dve, "hss", t)
                V.tensor_scalar(h[:, 1:2], h[:, 0:1], 1.0 / D, EPS, ALU.mult, ALU.add).then_inc(dve_o.sem, 1)
                act_o.wait(dve, "hexp", t)
                rsqrt_step(dve_o, ["hn0", "hn1", "hr"], h[:, 1:2], h[:, 3:4], h[:, 4:5], h[:, 5:6], t)
                V.scalar_tensor_tensor(out=xres[0:n, :], in0=xres[0:n, :], scalar=h[:, 5:6], in1=normf[0:n, :],
                                       op0=ALU.mult, op1=ALU.mult).then_inc(dve_o.sem, 1)

            def w_gain(g):
                return (gin if g < len(GROUPS) else gout)[:, :]

            def max_w(g):
                s = g % 2
                if g >= 1:
                    dve.wait_ge(w_scaled, g)
                wait_staged(dve, g)
                V.tensor_reduce(wabs[:, s, :], staged(g), AX.X, ALU.max, apply_absolute_value=True).then_inc(w_dve, 1)
                dve.wait_ge(w_dve, 4 * g + 1)
                V.tensor_tensor(wabs[:, s, :], wabs[:, s, :], w_gain(g), ALU.mult).then_inc(w_dve, 1)
                dve.wait_ge(w_dve, 4 * g + 2)
                V.tensor_reduce(wcol[:, 0:1], wabs[:, s, :], AX.X, ALU.max, apply_absolute_value=True
                                ).then_inc(w_row, 1)

            def scale_w(g):
                dve.wait_ge(w_max, g + 1)
                V.tensor_scalar(wcol[:, 2:3], wcol[:, 1:2], 1.0 / W_TOP, 1e-30, ALU.mult, ALU.max).then_inc(w_dve, 1)
                dve.wait_ge(w_dve, 4 * g + 3)
                V.reciprocal(wcol[:, 3:4], wcol[:, 2:3]).then_inc(w_dve, 1)
                c = 1.0 / U_SCALE if g < len(GROUPS) else 1.0
                V.tensor_scalar(inv[:, g:g + 1], wcol[:, 2:3], c, None, ALU.mult)
                if g < 2:
                    V.tensor_scalar(invq[:, g:g + 1], wcol[:, 2:3], c * DK ** -0.5, None, ALU.mult)
                dve.wait_ge(w_dve, 4 * g + 4)
                V.tensor_scalar(gs[:, g % 2, :], w_gain(g), wcol[:, 3:4], None, ALU.mult).then_inc(w_scaled, 1)

            def lo_w(g, d0, d1):
                dve.wait_ge(w_hi_done, g + 1)
                for d in range(d0, d1):
                    lo = V.scalar_tensor_tensor(out=w_slice(g, w_lo, wo_lo)[:, d], in0=staged(g)[:, d],
                                                scalar=gs[:, g % 2, d:d + 1], in1=w_slice(g, w_hi, wo_hi)[:, d],
                                                op0=ALU.mult, op1=ALU.subtract)
                if d1 == DVE_TILES[g]:
                    lo.then_inc(w_lo_done, 1)

            def sample():
                t = Tile(NT)
                p = t.p
                done = smp["dve"]
                after(dve, "pe_z")
                for f in range(FT):
                    z = V.tensor_scalar(s_z[:, 0, f, :], banks[1][:, f * NS:f * NS + NS], bg[:, f:f + 1], None,
                                        ALU.add)
                z.then_inc(done, 1)
                after(dve, "dve_zb")
                V.tensor_scalar(s_z[:, 2], s_z[:, 0], 0.0, None, ALU.min).then_inc(done, 1)
                after(dve, "act_l1")
                after(dve, "dve_mz")
                V.tensor_tensor(s_z[:, 3], s_z[:, 2], s_z[:, 1], ALU.subtract).then_inc(done, 1)
                after(dve, "pe_kt")
                V.tensor_copy(s_kt, banks[0][0:NS, 0:HG * DK]).then_inc(done, 1)
                after(dve, "dve_kt")
                V.tensor_tensor(s_km, bcast(s_kt, 1, NS), bcast(ident[0:NS, 0:NS], 2, HG * DK), ALU.mult
                                ).then_inc(done, 1)
                V.memset(s_qm, 0.0).then_inc(done, 1)
                after(dve, "dve_qz")
                for f in range(FT):
                    for h in range(2):
                        r = h * DK
                        q = V.tensor_copy(s_qm[r:r + DK, f, h].rearrange("p b c -> p (b c)")[:, 0:NS * NS:NS + 1],
                                          gq[r:r + DK, p, f, 0:NS])
                q.then_inc(done, 1)
                dve.wait_ge(tail_in, 64)
                V.tensor_copy(s_kT[:, :, P - 1:P], s_knew[:, :].unsqueeze(2)).then_inc(done, 1)
                V.memset(s_qs, 0.0).then_inc(done, 1)
                after(dve, "dve_qsz")
                for h in range(KVH):
                    r = h * HD
                    q = V.tensor_copy(s_qs[r:r + HD, :, GRP * h:GRP * h + GRP],
                                      sq[r:r + HD, p, :, 0:NS].rearrange("p f b -> p b f"))
                q.then_inc(done, 1)
                after(dve, "act_a")
                for r in range(4):
                    after(dve, f"pe_kv{r}")
                    for b in range(2):
                        for f in range(FT):
                            s = s_state[:, 2 * r + b, f, :]
                            c = (2 * b + f) * DV
                            up = V.scalar_tensor_tensor(out=s, in0=s, scalar=s_z[:, 4, f, 2 * r + b:2 * r + b + 1],
                                                        in1=banks[r % 2][:, c:c + DV], op0=ALU.mult, op1=ALU.add)
                    up.then_inc(done, 1)
                after(dve, "pe_sc")
                for i in range(2):
                    mx = V.tensor_reduce(s_st[:, 0, 4 * i:4 * i + 4],
                                         banks[i][0:8, :].rearrange("p (b c) -> p b c", b=4), AX.X, ALU.max,
                                         negate=True)
                mx.then_inc(done, 1)
                after(dve, "dve_mx")
                V.tensor_scalar(s_st[:, 1, :], s_st[:, 0, :], s_sink[:, 1:2], None, ALU.min).then_inc(done, 1)
                after(dve, "dve_nm")
                for i in range(2):
                    sub = V.tensor_tensor(s_p[:, 4 * i:4 * i + 4, :], banks[i][0:8, :].rearrange(
                        "p (b c) -> p b c", b=4), bcast(s_st[:, 1, 4 * i:4 * i + 4], 2, P), ALU.add)
                sub.then_inc(done, 1)
                V.tensor_scalar(s_st[:, 2, :], s_st[:, 1, :], s_sink[:, 0:1], None, ALU.add).then_inc(done, 1)
                after(dve, "act_exp")
                V.tensor_reduce(s_st[:, 4, :], s_p, AX.X, ALU.add).then_inc(done, 1)
                after(dve, "dve_sum")
                V.tensor_tensor(s_st[:, 5, :], s_st[:, 4, :], s_st[:, 3, :], ALU.add).then_inc(done, 1)
                after(dve, "dve_den")
                V.reciprocal(s_st[:, 6, :], s_st[:, 5, :]).then_inc(done, 1)
                after(dve, "dve_rden")
                V.tensor_tensor(s_p, s_p, bcast(s_st[:, 6, :], 2, P), ALU.mult).then_inc(done, 1)
                after(dve, "pe_pT")
                V.tensor_copy(s_pT, banks[0][:, 0:8 * NS].rearrange("p (b h) -> p b h", b=NS)).then_inc(done, 1)
                after(dve, "pe_pv")
                for h in range(KVH):
                    r = h * HD
                    o = V.tensor_copy(s_oT[r:r + HD, :, :], banks[1][r:r + HD, 0:8 * NS].rearrange(
                        "p (b h) -> p h b", b=NS)[:, GRP * h:GRP * h + GRP, :])
                o.then_inc(done, 1)

            V.memset(ones[:, :], 1.0).then_inc(ones_set, 1)
            dve.wait_ge(first_in, 16 * 2)
            mean_square(Tile(0))
            norm_x(Tile(0))
            scale_u(Tile(0))
            max_w(0)
            scale_w(0)
            split_u(Tile(0))
            max_w(1)
            for g in range(NG):
                lo_w(g, 0, 2)
                if g + 1 < NG:
                    scale_w(g + 1)
                lo_w(g, 2, DVE_TILES[g])
                if g + 2 < NG:
                    max_w(g + 2)
                if g == 1:
                    dve.wait_ge(const_in, 16 * 10)
                    V.tensor_copy(ident_b[:, :], ident[:, :])
                    V.tensor_scalar(s_sink[:, 1:2], s_sink[:, 0:1], -1.0, None, ALU.mult)
                    V.tensor_scalar(nsink[:, :], sink[:, :], -1.0, None, ALU.mult)
                    V.memset(kwin[:, 0, 0:P], 0.0)
                    V.memset(vwin[:, 0, 0, :], 0.0)
                    V.memset(S_bd[:, :, :, :], 0.0).then_inc(init, 1)
                    mean_square(Tile(1))
                    norm_x(Tile(1))
                if g == 3:
                    take_kv(Tile(0))
                if g == 4:
                    take_gv(Tile(0))
            scale_u(Tile(1))
            split_u(Tile(1))
            dve.wait_ge(w_lo_pool, NG)
            V.memset(QE, 0.0)

            def body(t):
                nxt = t + 1
                take_z(t)
                row_max(t, 0)
                row_max(t, 1)
                sums(t)
                take_pt(t, 0)
                row_max(t, 2)
                row_max(t, 3)
                factors(t)
                take_kv(nxt)
                assemble_leaves(t)
                denominators(t)
                assemble_levels(t)
                take_gv(nxt)
                if not (t.static and t.off + 2 > NT):
                    mean_square(t + 2)
                gate_window(t)
                mean_heads(t)
                update_state(t)
                gate_gla(t)
                scale_rows(t)
                take_out(t, 0)
                take_out(t, 1)
                if not (t.static and t.off + 2 > NT):
                    norm_x(t + 2)
                if not (t.static and t.off + 2 > NT):
                    scale_u(t + 2)
                    split_u(t + 2)
                residual(t)
                final_norm(t)

            iterations(dve, body)
            sample()
            gate_window(Tile(NT))
            mean_heads(Tile(NT))
            gate_gla(Tile(NT))
            scale_rows(Tile(NT))
            take_out(Tile(NT), 0)
            take_out(Tile(NT), 1)
            residual(Tile(NT))
            final_norm(Tile(NT))

        @block.gpsimd
        def _(pool):
            G = nc.gpsimd

            def lo_w(g):
                d = DVE_TILES[g]
                pool.wait_ge(w_hi_pool, g + 1)
                G.tensor_tensor(w_slice(g, w_lo, wo_lo)[:, d:DT], staged(g)[:, d:DT],
                                w_slice(g, w_hi, wo_hi)[:, d:DT], ALU.subtract).then_inc(w_lo_pool, 1)

            for g in range(NG):
                pool.wait_ge(w_row, g + 1)
                G.partition_all_reduce(wcol[:, 1:2], wcol[:, 0:1], P, bass.bass_isa.ReduceOp.max
                                       ).then_inc(w_max, 1)
                if g >= 1:
                    lo_w(g - 1)
            lo_w(NG - 1)

            def differences(t):
                dve_g.wait(pool, "scan", t)
                for l, s in enumerate(LEVELS):
                    b = bsum[:, :, :].rearrange("p f (b c) -> p (f b) c", c=2 * s)
                    o = EX[:, l].rearrange("p f (b c) -> p (f b) c", c=2 * s)
                    mid = b[:, :, s - 1:s].broadcast_to([P, FT * P // (2 * s), s])
                    G.tensor_tensor(o[:, :, 0:s], mid, b[:, :, 0:s], ALU.subtract)
                    G.tensor_tensor(o[:, :, s:2 * s], b[:, :, s:2 * s], mid, ALU.subtract)
                G.tensor_tensor(EX[:, S_STATE], bsum[:, :, P - 1:P].broadcast_to([P, FT, P]), bsum[:, :, :],
                                ALU.subtract)
                b = lsum[:, :, :].rearrange("p f (b c) -> p (f b) c", c=LEAF)
                G.tensor_tensor(EX[:, S_LEAFQ].rearrange("p f (b c) -> p (f b) c", c=LEAF), b,
                                b[:, :, LEAF // 2 - 1:LEAF // 2].broadcast_to([P, FT * P // LEAF, LEAF]),
                                ALU.subtract).then_inc(pool_g.sem, 1)

            def gates_over_sums(t):
                dve_w.wait(pool, "rden", t)
                pj.wait_freed(pool, "sg", t)
                g = gates[:, 512:1024].rearrange("p (h c) -> p h c", h=8)
                G.tensor_tensor(g, g, bcast(wst[:, 5, :], 2, HD), ALU.mult).then_inc(pool_w.sem, 1)

            def body(t):
                differences(t)
                gates_over_sums(t)

            iterations(pool, body)


def _columns():
    import numpy as np
    heads = np.concatenate([np.arange(HD) + HD * (GRP * kv + f) for f in range(GRP) for kv in range(KVH)])
    gq, gk, gv, gg, low, sq, sk, sv, sg = np.split(
        np.arange(IN_W), np.cumsum([256, 256, 512, 512, 16, 512, 128, 128]))
    return [np.concatenate([gq, gk]), sq[heads], np.concatenate([sk, sv, low]), gv, gg, sg[heads]], heads


def kernel(**inputs):
    import numpy as np
    import ml_dtypes
    import concourse.bacc as _bacc
    from concourse.bass_utils import run_bass_kernel_spmd as _run

    a = {k: np.asarray(v) for k, v in inputs.items()}
    cols, heads = _columns()
    x, xs = a["x_prompt"][0], a["x_sample"][:, 0]
    w_in, w_out = a["w_in"][0], a["w_out"][0]
    w_out = np.concatenate([w_out[:512], w_out[512 + heads]])
    rows = lambda w: w.reshape(DT, P, -1).transpose(1, 0, 2).reshape(P, -1)
    half = D // OUT_GROUPS
    w_all = np.concatenate([rows(w_in[:, c]) for c in cols]
                           + [rows(w_out[:, g * half:g * half + half]) for g in range(OUT_GROUPS)], axis=1)
    head_of = np.array([GRP * kv + f for f in range(GRP) for kv in range(KVH)])
    tok = np.arange(P)
    same = tok[:, None] // LEAF == tok[None, :] // LEAF
    leaf = (same & (tok[:, None] <= tok[None, :])).astype(np.float32)
    lvl = np.zeros((P, len(LEVELS), P // 2), np.float32)
    for i, s in enumerate(LEVELS):
        pair = np.arange(P // 2) // s
        lvl[:, i] = (tok[:, None] // (2 * s) == pair[None, :]) & (tok[:, None] % (2 * s) < s)
    scan = np.ones((P, 2, P), np.float32)
    scan[:, 1, ::LEAF] = 0.0
    key = np.arange(2 * P)[None, :]
    ok = (tok[:, None] + P - key >= 0) & (tok[:, None] + P - key < P)
    band = np.stack([np.where(ok, 0.0, -1e30), np.where(ok & (key >= P), 0.0, -1e30)], 1)
    arrays = {
        "xT": x.reshape(NT, P, DT, P).transpose(0, 3, 2, 1),
        "xq": x.reshape(NT, P, D),
        "xsT": xs.reshape(NS, DT, P).transpose(2, 1, 0),
        "xs": xs,
        "w": w_all,
        "gin": a["norm_in"][0].reshape(DT, P).T,
        "gout": np.concatenate([np.repeat(a["gla_norm"][0][:, None], HG, 1), np.ones((P, HG), np.float32)], 1),
        "wgu": a["w_gate_up"][0],
        "bg": a["b_gate"][0].reshape(FT, P).T,
        "sink": np.broadcast_to(a["attn_sinks"][0][head_of], (P, 8)),
        "normf": np.broadcast_to(a["norm_f"], (P, D)),
        "state": a["state_gla"][0].reshape(NS, FT, 2, DK, DV).transpose(2, 3, 0, 1, 4).reshape(P, NS, FT, DV),
        "kcT": np.roll(a["cache_win_k"][0], -1, axis=1).transpose(2, 3, 0, 1).reshape(P, NS, P),
        "vc": a["cache_win_v"][0].transpose(1, 0, 2, 3).reshape(P, NS, P)[1:],
        "sinks_s": a["attn_sinks"][0][:, None],
        "ident": np.eye(P, dtype=np.float32),
        "tri": leaf,
        "lvl": lvl,
        "leafscan": scan,
        "band": band.astype(ml_dtypes.bfloat16),
    }
    outs = [("y", (NT, P, D)), ("ys", (NS, D)), ("Sp", (HG, DK, DV)), ("kp", (KVH, HD, P)), ("vp", (P, P)),
            ("Ss", (P, NS, FT, DV)), ("ksT", (P, NS, P)), ("vs", (P, NS, P))]
    nc = _bacc.Bacc("TRN2", target_bir_lowering=False, num_devices=1)
    maps, args = {}, []
    for name, v in arrays.items():
        v = np.ascontiguousarray(v)
        maps[f"in_{name}"] = v
        args.append(nc.dram_tensor(f"in_{name}", v.shape, mybir.dt.from_np(v.dtype), kind="ExternalInput").ap())
    for name, shape in outs:
        args.append(nc.dram_tensor(f"out_{name}", shape, F32, kind="ExternalOutput").ap())
    hymba_step_kernel(nc, *args)
    res = _run(nc, [maps], core_ids=[0]).results[0]
    y, ys, Sp, kp, vp, Ss, ksT, vs = (np.asarray(res[f"out_{name}"]) for name, _ in outs)
    return (y.reshape(1, SEQ, D),
            ys.reshape(NS, 1, D),
            Sp.reshape(1, 1, HG, DK, DV),
            kp.transpose(2, 0, 1).reshape(1, 1, P, KVH, HD),
            vp.reshape(1, 1, P, KVH, HD),
            Ss.reshape(2, DK, NS, FT, DV).transpose(2, 3, 0, 1, 4).reshape(1, NS, HG, DK, DV),
            ksT.reshape(KVH, HD, NS, P).transpose(2, 3, 0, 1)[None],
            vs.reshape(P, NS, KVH, HD).transpose(1, 0, 2, 3)[None])
```

```python
from contextlib import ExitStack

import concourse.bass as bass
from concourse import mybir

F32 = mybir.dt.float32
F16 = mybir.dt.float16
BF16 = mybir.dt.bfloat16
I32 = mybir.dt.int32
ALU = mybir.AluOpType
ACT = mybir.ActivationFunctionType
AX = mybir.AxisListType

P = 128
D = 1024
DT = D // P
SEQ = 2048
NT = SEQ // P
NS = 8
EPS = 1e-6
TAU = 16.0
HG, DK, DV = 4, 64, 128
FT = HG * DK // P
KVH, GRP, HD = 2, 4, 64
RANK = 16
GROUPS = [("gqk", 512), ("sq", 512), ("sklow", 272), ("gv", 512), ("gg", 512), ("sg", 512)]
COL = {}
_c = 0
for _name, _n in GROUPS:
    COL[_name] = _c
    _c += _n
IN_W = _c
OUT_GROUPS = 2
NG = len(GROUPS) + OUT_GROUPS
LEVELS = (64, 32, 16, 8)
LEAF = 8
LEAF_FLOOR = -20.0
U_SCALE = float(2 ** 10)
W_TOP = float(2 ** 14)
O_TOP = float(2 ** 14)
LOG_EXP_SET = "natural_log_exp_and_others"
DVE_TILES = [4] * 7 + [6]
STAGE_OF = [0, 1, 2, 3, 0, 2, 1, 0]
LOAD_ORDER = [0, 1, 2, 3, 4, 6, 5, 7]
DVE_LEVELS = 2
S_LEVEL, S_STATE, S_LEAFK, S_INTER, S_LEAFQ = 0, 4, 5, 6, 7


class Tile:

    def __init__(self, off, j=None):
        self.off, self.j = off, j
        self.p = off % 2

    @property
    def n(self):
        return self.off if self.j is None else self.j * 2 + self.off

    def __add__(self, d):
        return Tile(self.off + d, self.j)

    @property
    def static(self):
        return self.j is None

    @property
    def tokens(self):
        return NS if self.static and self.off == NT else P

    @property
    def sample(self):
        return self.static and self.off == NT


class Events:

    def __init__(self, sem, names):
        self.sem, self.names = sem, names

    def at(self, name, t):
        return t.n * len(self.names) + (self.names.index(name) + 1)

    def wait(self, eng, name, t):
        if not (t.static and t.off < 0):
            eng.wait_ge(self.sem, self.at(name, t))


class Ring:

    def __init__(self, banks, full, freed, order, tail=None, head=None):
        self.banks, self.full, self.freed, self.order = banks, full, freed, order
        self.tail = order if tail is None else tail
        self.head = [(u, n) for n in range(2) for u, _ in order] if head is None else head

    def _list(self, t):
        return self.tail if t.sample else self.order

    def _index(self, name, t):
        return [u for u, _ in self._list(t)].index(name)

    def _in_head(self, t):
        return t.static and t.off < 2

    def bank(self, name, t):
        if self._in_head(t):
            return self.banks[self.head.index((name, t.off)) % 2]
        return self.banks[(len(self.order) * t.p + self._index(name, t)) % 2]

    def wait_full(self, eng, name, t):
        if self._in_head(t):
            eng.wait_ge(self.full, self.head.index((name, t.off)) + 1)
        else:
            eng.wait_ge(self.full, t.n * len(self.order) + (self._index(name, t) + 1))

    def wait_freed(self, eng, name, t):
        who = dict(self._list(t))[name]
        if self._in_head(t):
            before = self.head[:self.head.index((name, t.off)) + 1]
            eng.wait_ge(self.freed[who], sum(1 for u, _ in before if dict(self.order)[u] == who))
            return
        total = sum(1 for _, w in self.order if w == who)
        rank = [u for u, w in self._list(t) if w == who].index(name) + 1
        eng.wait_ge(self.freed[who], t.n * total + rank)

    def wait_free(self, eng, name, t):
        if self._in_head(t):
            i = self.head.index((name, t.off))
            if i >= 2:
                before, n = self.head[i - 2]
                self.wait_freed(eng, before, Tile(n))
            return
        i = self._index(name, t)
        if i >= 2:
            self.wait_freed(eng, self._list(t)[i - 2][0], t)
        else:
            self.wait_freed(eng, self.order[len(self.order) + i - 2][0], t + -1)


def bcast(ap, axis, n):
    ap = ap.unsqueeze(axis)
    shape = list(ap.shape)
    shape[axis] = n
    return ap.broadcast_to(shape)


def hymba_step_kernel(nc, xT_d, xq_d, xsT_d, xs_d, w_d, gin_d, gout_d, wgu_d, bg_d, sink_d, normf_d, normfT_d,
                      state_d, kcT_d, vc_d, sinks_s_d, ident_d, tri_d, lvl_d, leafscan_d, band_d, older_d, window_d,
                      y_d, ys_d, Sp_d, kp_d, vp_d, Ss_d, ksT_d, vs_d):
    with ExitStack() as ctx:
        def sb(name, shape, dt=F32):
            return ctx.enter_context(nc.sbuf_tensor(name, shape, dt))

        def sem(name):
            return ctx.enter_context(nc.semaphore(name))

        w_region = sb("w_in_hi_lo", [P, DT * IN_W])
        w_half = w_region[:, :].bitcast(F16).rearrange("p (s d c) -> p s d c", s=2, d=DT)
        w_hi, w_lo = w_half[:, 0], w_half[:, 1]
        wo_hi = sb("w_out_hi", [P, DT, D], F16)
        wo_lo = sb("w_out_lo", [P, DT, D], F16)
        xT = sb("xT", [P, DT, P])
        u_hi = sb("u_hi", [P, 2, DT, P], F16)
        u_lo = sb("u_lo", [P, 2, DT, P], F16)
        xq = sb("x_rows", [P, D])
        gq = sb("gla_q", [P, 2, FT, P])
        gk = sb("gla_k", [P, 2, FT, P])
        gv = sb("gla_v", [P, 2, HG * DV])
        sq = sb("win_q", [P, 2, GRP, P])
        kwin = sb("win_k", [P, 2, 2 * P])
        vwin = sb("win_v", [P, 2, 2, P])
        glow = sb("g_low", [P, 2, RANK])
        S_bd = sb("gla_state", [P, FT, 2, DV])
        normf = sb("norm_f", [P, D])
        normfT = sb("norm_f_T", [P, DT])
        flex = sb("flex", [P, 8192])
        stage = [flex[:, 4096 * s:4096 * s + 4096] for s in range(2)]
        stage += [w[:, :, :].rearrange("p d c -> p (d c)").bitcast(F32) for w in (wo_hi, wo_lo)]
        at = [0]

        def part(n):
            at[0] += n
            return flex[:, at[0] - n:at[0]]

        xres = part(D)
        QE = part(4 * FT * P).rearrange("p (l f h c) -> p l f h c", l=4, f=FT, h=2)
        gates = part(D)
        PT = part(2 * 2 * 2 * P).rearrange("p (s h k c) -> p s h k c", s=2, h=2, k=2)
        KST = part(HG * DK)
        at[0] = 4096
        EX = part(8 * FT * P).rearrange("p (s f c) -> p s f c", s=8, f=FT)
        PR = part(2 * 2 * P).rearrange("p (s h c) -> p s h c", s=2, h=2)
        QL = part(FT * P).rearrange("p (f c) -> p f c", f=FT)
        AT = part(HG * P).rearrange("p (h c) -> p h c", h=HG)
        bsum = part(FT * P).rearrange("p (f c) -> p f c", f=FT)
        assert at[0] <= 8192
        lsum = sb("decay_sum_leaf", [P, FT, P])
        ogT_hi = sb("ogT_hi", [P, DT, P], F16)
        ogT_lo = sb("ogT_lo", [P, DT, P], F16)
        junk = sb("junk", [P, D], BF16)
        glT = sb("g_lowT", [RANK, P])
        ident = sb("ident", [P, P])
        band = sb("band_bf16", [P, 2, P], BF16)
        older = sb("older_key", [P, P])
        window = sb("window_mask", [P, 2, P])
        leafmask = sb("leaf_mask", [P, P])
        lvlmask = sb("level_mask", [P, 4, DK])
        leafscan = sb("leaf_scan", [P, 2, P])
        diag = sb("rstd_diag", [P, P])
        gin = sb("norm_in", [P, DT])
        gout = sb("gla_norm", [P, DT])
        wgu = sb("w_gate_up", [RANK, HG * DK])
        bg = sb("b_gate", [P, FT])
        sink = sb("sinks", [P, 8])
        nsink = sb("neg_sinks", [P, 8])
        wabs = sb("w_abs", [P, 2, DT])
        wcol = sb("w_col", [P, 4])
        gs = sb("w_scale", [P, 2, DT])
        inv = sb("inv_scale", [P, NG])
        invq = sb("inv_scale_q", [P, 2])
        ones = sb("ones", [P, 1])
        xst = sb("x_stat", [P, 2, 8])
        ost = sb("o_stat", [P, 8, HG])
        hst = sb("h_stat", [P, 8])
        wst = sb("win_stat", [P, 6, 8])
        amax = sb("row_max", [P, 4])
        isc = sb("row_unscale", [P, 2])
        dec = sb("chunk_decay", [P, FT])

        banks = [ctx.enter_context(nc.psum_tensor(f"bank{i}", [P, 512], F32)) for i in range(8)]
        accS, accG = banks[6], banks[7]

        const_in = sem("const_in")
        w_in_sem = [sem(f"w_staged_{i}") for i in range(4)]
        xT_in = sem("xT_in")
        xq_in = sem("xq_in")
        xres_in = sem("xres_in")
        y_out = sem("y_out")
        tail_out = sem("tail_out")
        w_row = sem("w_rowmax_done")
        w_max = sem("w_max_done")
        w_scaled = sem("w_scale_done")
        w_dve = sem("w_dve_steps")
        w_hi_done = sem("w_hi_done")
        w_lo_done = sem("w_lo_done")
        w_lo_pool = sem("w_lo_pool")
        w_in_place = sem("w_scaled_in_place")
        w_hi_pool = sem("w_hi_for_pool")
        first_in = sem("first_in")
        ones_set = sem("ones_set")
        init = sem("init_done")
        pj = Ring(banks[0:2], sem("proj_full"), {"act": sem("proj_freed_act"), "dve": sem("proj_freed_dve")},
                  [("bc", "dve"), ("gqk", "act"), ("sq", "act"), ("sklow", "dve"), ("gv", "dve"),
                   ("gg", "act"), ("sg", "act")],
                  [("bc", "dve"), ("gqk", "act"), ("sq", "act"), ("sklow", "dve"), ("gv", "dve"), ("low", "act"),
                   ("gates", "act"), ("z", "dve"), ("kt", "dve"), ("kv0", "dve"), ("kv1", "dve"), ("sc0", "dve"),
                   ("sc1", "dve"), ("kv2", "dve"), ("kv3", "dve"), ("pT", "dve"), ("pv", "dve"), ("o", "dve"),
                   ("ss", "dve"), ("y", "dve"), ("hs", "dve")],
                  [("bc", 0), ("gqk", 0), ("bc", 1), ("sq", 0), ("sklow", 0), ("gqk", 1), ("sq", 1), ("gv", 0),
                   ("sklow", 1), ("gv", 1), ("gg", 0), ("sg", 0), ("gg", 1), ("sg", 1)])
        at_ring = Ring(banks[2:4], sem("attn_full"), {"act": sem("attn_freed_act"), "dve": sem("attn_freed_dve")},
                       [("s0", "dve"), ("s1", "dve"), ("s2", "dve"), ("s3", "dve"),
                        ("leaf0", "dve"), ("leaf1", "dve"), ("L1", "dve"), ("L2", "dve"),
                        ("y0", "dve"), ("y1", "dve")])
        tr = Ring(banks[4:6], sem("turn_full"), {"act": sem("turn_freed_act"), "dve": sem("turn_freed_dve")},
                  [("glT", "act"), ("z", "dve"), ("pt0", "dve"), ("pt1", "dve"), ("pt2", "dve"), ("pt3", "dve"),
                   ("KST", "act"), ("SU", "dve"), ("og0", "dve"), ("og1", "dve")])
        act_u = Events(sem("act_norm"), ["ssq", "ln", "exp", "hi"])
        dve_u = Events(sem("dve_norm"), ["ms", "n0", "n1", "rstd", "diag", "lo"])
        act_g = Events(sem("act_gla"), ["az", "ez", "l1", "leaf", "E"])
        dve_g = Events(sem("dve_gla"), ["mz", "la", "lc", "scan", "D", "leaf", "Q", "QF", "L16"])
        pool_g = Events(sem("pool_gla"), ["leaf", "D"])
        pool_w = Events(sem("pool_win"), ["gs"])
        win_kept = Events(sem("window_kept"), ["win"])
        dve_w = Events(sem("dve_win"), ["m0", "m1", "m2", "m3", "esi", "den", "rden"])
        act_w = Events(sem("act_win"), ["p0", "p1", "p2", "p3", "es"])
        pe_pv = Events(sem("pe_pv"), ["pv0", "pv1", "pv2", "pv3"])
        pe_o = Events(sem("pe_gla_out"), ["o"])
        dve_o = Events(sem("dve_out"), ["sg", "amw", "oms", "on0", "on1", "orstd", "gg", "am", "amc", "rsc", "gsc0",
                                        "gsc1", "isc", "hms", "hn0", "hn1", "hr", "y"])
        act_o = Events(sem("act_out"), ["oss", "oln", "oexp", "hi0", "hi1", "hss", "hln", "hexp"])
        kT_in = sem("sample_keys_in")
        v_in = sem("sample_values_in")
        state_in = sem("sample_state_in")
        sx_in = sem("sample_x_in")
        smp = {"act": Events(sem("sample_act"), ["az", "ez", "l1", "a", "exp", "oln", "oexp", "hln", "hexp"]),
               "dve": Events(sem("sample_dve"), [
                   "mz", "km", "qz", "q2", "la", "kT", "qsz", "qs", "mx0", "mx", "nm", "esi", "sum", "den", "rden",
                   "pn", "sq", "n0", "n1", "rstd", "on", "gg", "am", "amc", "rsc", "rscs", "og", "hi", "lo",
                   "isc", "h0", "h1", "hsq", "hsum", "hn0", "hn1", "hr", "hn", "out"]),
               "pool": Events(sem("sample_pool"), ["am"])}

        w_at = [0]

        def wpart(n):
            w_at[0] += n
            return w_region[:, w_at[0] - n:w_at[0]]

        s_state = wpart(NS * FT * DV).rearrange("p (b f c) -> p b f c", b=NS, f=FT)
        s_kT = wpart(NS * P).rearrange("p (b c) -> p b c", b=NS)
        s_v = wpart(NS * P).rearrange("p (b c) -> p b c", b=NS)
        s_km = wpart(NS * HG * DK).rearrange("p (b c) -> p b c", b=NS)[0:NS]
        s_kt = wpart(HG * DK)[0:NS]
        s_q2 = wpart(HG * NS).rearrange("p (f b h) -> p f b h", f=FT, b=NS)
        s_z = wpart(6 * FT * NS).rearrange("p (s f b) -> p s f b", s=6, f=FT)
        s_qs = wpart(NS * 8).rearrange("p (b h) -> p b h", b=NS)
        s_p = wpart(NS * P).rearrange("p (b c) -> p b c", b=NS)[0:8]
        s_st = wpart(8 * NS).rearrange("p (s b) -> p s b", s=8)[0:8]
        s_pT = wpart(NS * 8).rearrange("p (b h) -> p b h", b=NS)
        s_gates = wpart(DT * NS).rearrange("p (d b) -> p d b", d=DT)
        s_og = wpart(DT * NS).rearrange("p (d b) -> p d b", d=DT)
        s_ogh = wpart(DT * NS // 2).bitcast(F16).rearrange("p (d b) -> p d b", d=DT)
        s_ogl = wpart(DT * NS // 2).bitcast(F16).rearrange("p (d b) -> p d b", d=DT)
        s_x = wpart(DT * NS).rearrange("p (d b) -> p d b", d=DT)
        s_y = wpart(DT * NS).rearrange("p (d b) -> p d b", d=DT)
        s_h2 = wpart(DT * NS).rearrange("p (d b) -> p d b", d=DT)
        s_on = wpart(7 * NS * HG).rearrange("p (s c) -> p s c", s=7)
        s_am = wpart(6 * NS).rearrange("p (s b) -> p s b", s=6)
        s_hn = wpart(6 * NS).rearrange("p (s b) -> p s b", s=6)
        s_sink = sb("sample_sinks", [8, 2])
        s_knew = sb("sample_k_new", [P, NS])
        s_vnew_t = sb("sample_v_new", [NS, P])
        s_vnew = s_vnew_t[:, :]

        def after(eng, step):
            who, name = step.split("_")
            smp[who].wait(eng, name, Tile(0))

        def head(u, i):
            return (u // 2 * 2 + i) * KVH + u % 2

        def w_slice(g, w_in, w_out):
            if g < len(GROUPS):
                return w_in[:, :, COL[GROUPS[g][0]]:COL[GROUPS[g][0]] + GROUPS[g][1]]
            c = (g - len(GROUPS)) * D // OUT_GROUPS
            return w_out[:, :, c:c + D // OUT_GROUPS]

        def group_width(g):
            return GROUPS[g][1] if g < len(GROUPS) else D // OUT_GROUPS

        def staged(g):
            return stage[STAGE_OF[g]][:, 0:DT * group_width(g)].rearrange("p (d c) -> p d c", d=DT)

        def wait_staged(eng, g):
            eng.wait_ge(w_in_sem[STAGE_OF[g]], 16 * (STAGE_OF[:g].count(STAGE_OF[g]) + 1))

        def level_differences(E, l):
            s = LEVELS[l]
            b = bsum[:, :, :].rearrange("p f (b c) -> p (f b) c", c=2 * s)
            o = EX[:, l].rearrange("p f (b c) -> p (f b) c", c=2 * s)
            mid = b[:, :, s - 1:s].broadcast_to([P, FT * P // (2 * s), s])
            E.tensor_tensor(o[:, :, 0:s], mid, b[:, :, 0:s], ALU.subtract)
            return E.tensor_tensor(o[:, :, s:2 * s], b[:, :, s:2 * s], mid, ALU.subtract)

        block = ctx.enter_context(nc.Block())

        def iterations(eng, body):
            body(Tile(0))
            with eng.Fori(0, (NT - 4) // 2) as j:
                body(Tile(1, j))
                body(Tile(2, j))
            for n in range(NT - 3, NT - 1):
                body(Tile(n))

        @block.sync
        def _(sp):
            def load_x(t):
                n = t.tokens
                if not (t.static and t.off < 1):
                    dve_u.wait(sp, "lo", t + -1)
                if t.sample:
                    sp.dma_start(xT[:, :, 0:n], xsT_d).then_inc(xT_in, 16)
                else:
                    sp.dma_start(xT[:, :, :], xT_d[bass.ds(t.n, 1)].rearrange("a p d c -> (a p) d c")
                                 ).then_inc(xT_in, 16)
                if not (t.static and t.off < 1):
                    act_u.wait(sp, "ssq", t + -1)
                src = xs_d if t.sample else xq_d[bass.ds(t.n, 1)].rearrange("a p c -> (a p) c")
                sp.dma_start(xq[0:n, :], src).then_inc(xq_in, 16)

            def load_w(g):
                n = group_width(g)
                off = DT * (COL[GROUPS[g][0]] if g < len(GROUPS) else IN_W + (g - len(GROUPS)) * D // OUT_GROUPS)
                before = [b for b in range(g) if STAGE_OF[b] == STAGE_OF[g]]
                if before:
                    for split in (w_hi_done, w_lo_done, w_lo_pool):
                        sp.wait_ge(split, before[-1] + 1)
                sp.dma_start(staged(g).rearrange("p d c -> p (d c)"), w_d[:, off:off + DT * n]
                             ).then_inc(w_in_sem[STAGE_OF[g]], 16)

            load_x(Tile(0))
            load_w(0)
            load_w(1)
            load_x(Tile(1))
            for g in LOAD_ORDER[2:4]:
                load_w(g)
            for dst, src in ((gout[:, :], gout_d), (wgu[:, :], wgu_d), (bg[:, :], bg_d), (sink[:, :], sink_d), (normf[:, :], normf_d),
                             (leafmask[:, :], tri_d), (lvlmask[:, :, :], lvl_d), (leafscan[:, :, :], leafscan_d),
                             (band[:, :, :], band_d), (older[:, :], older_d),
                             (window[:, :, :], window_d), (s_sink[:, 0:1], sinks_s_d),
                             (normfT[:, :], normfT_d)):
                sp.dma_start(dst, src).then_inc(const_in, 16)
            for g in LOAD_ORDER[4:]:
                load_w(g)
            sp.wait_ge(w_lo_done, NG)
            sp.wait_ge(w_lo_pool, NG)
            sp.wait_ge(w_hi_done, NG)

            def body(t):
                n = t.tokens
                if not (t.static and t.off == 0):
                    sp.wait_ge(y_out, t.n * 16)
                sp.dma_start(xres, xq_d[bass.ds(t.n, 1)].rearrange("a p c -> (a p) c")).then_inc(xres_in, 16)
                if not (t.static and t.off + 2 > NT):
                    load_x(t + 2)
                dve_o.wait(sp, "y", t)
                sp.dma_start(y_d[bass.ds(t.n, 1)].rearrange("a p c -> (a p) c"), xres).then_inc(y_out, 16)

            iterations(sp, body)
            t, s = Tile(NT - 1), Tile(NT)
            sp.wait_ge(y_out, t.n * 16)
            sp.dma_start(xres, xq_d[bass.ds(t.n, 1)].rearrange("a p c -> (a p) c")).then_inc(xres_in, 16)
            pj.wait_full(sp, "gates", s)
            sp.dma_start(s_kT, kcT_d).then_inc(kT_in, 16)
            sp.dma_start(s_state, state_d).then_inc(state_in, 16)
            sp.dma_start(s_v[0:P - 1], vc_d).then_inc(v_in, 16)
            pj.wait_freed(sp, "sklow", s)
            sp.dma_start(s_v[P - 1:P], s_vnew).then_inc(v_in, 16)
            sp.dma_start(s_x, xsT_d).then_inc(sx_in, 16)
            for kv in range(KVH):
                sp.dma_start(kp_d[kv], kwin[HD * kv:HD * kv + HD, t.p, P:2 * P]).then_inc(tail_out, 16)
            sp.dma_start(vp_d, vwin[:, t.p, 1, :]).then_inc(tail_out, 16)
            sp.wait_ge(v_in, 32)
            sp.dma_start(vs_d, s_v).then_inc(tail_out, 16)
            tr.wait_freed(sp, "SU", t)
            for h in range(HG):
                r, f = DK * (h % 2), h // 2
                sp.dma_start(Sp_d[h], S_bd[r:r + DK, f, h % 2, :]).then_inc(tail_out, 16)
            sp.wait_ge(kT_in, 16)
            after(sp, "dve_kT")
            sp.dma_start(ksT_d, s_kT).then_inc(tail_out, 16)
            pj.wait_freed(sp, "kv3", s)
            sp.dma_start(Ss_d, s_state).then_inc(tail_out, 16)
            dve_o.wait(sp, "y", t)
            sp.dma_start(y_d[bass.ds(t.n, 1)].rearrange("a p c -> (a p) c"), xres).then_inc(y_out, 16)
            after(sp, "dve_out")
            sp.dma_start(ys_d, s_y).then_inc(tail_out, 16)
            sp.wait_ge(y_out, 16 * NT)
            sp.wait_ge(tail_out, 16 * (HG + KVH + 1 + 3 + 1))

        @block.tensor
        def _(pe):
            def split_product(out, terms, start=True, stop=True):
                last = len(terms) - 1
                for i, (a_hi, a_lo, b_hi, b_lo) in enumerate(terms):
                    nc.tensor.matmul(out, a_hi, b_hi, start=start and i == 0, stop=False)
                    nc.tensor.matmul(out, a_hi, b_lo, start=False, stop=False)
                    mm = nc.tensor.matmul(out, a_lo, b_hi, start=False, stop=stop and i == last)
                return mm

            def bc(t):
                n = t.tokens
                pj.wait_free(pe, "bc", t)
                dve_u.wait(pe, "diag", t)
                nc.tensor.matmul(pj.bank("bc", t)[:, 0:n], ones[0:n, :].broadcast_to([n, P]), diag[0:n, 0:n],
                                 start=True, stop=True).then_inc(pj.full, 1)

            def features(t, bank, at_, c0, ntile, step=P):
                n = t.tokens
                for f in range(ntile):
                    c = c0 + f * P
                    mm = split_product(bank[:, at_ + f * step:at_ + f * step + n],
                                       [(w_hi[:, d, c:c + P], w_lo[:, d, c:c + P],
                                         u_hi[:, t.p, d, 0:n], u_lo[:, t.p, d, 0:n]) for d in range(DT)])
                return mm

            def rows(t, bank, at_, c0, width, d0=0, d1=DT):
                n = t.tokens
                return split_product(bank[0:n, at_:at_ + width],
                                     [(u_hi[:, t.p, d, 0:n], u_lo[:, t.p, d, 0:n],
                                       w_hi[:, d, c0:c0 + width], w_lo[:, d, c0:c0 + width]) for d in range(d0, d1)],
                                     start=d0 == 0, stop=d1 == DT)

            def proj_rest(t, name, d0, d1=DT):
                mm = rows(t, pj.bank(name, t), 0, COL[name], 512, d0, d1)
                if d1 == DT:
                    mm.then_inc(pj.full, 1)

            def proj(t, name, d1=DT):
                if t.static and t.off <= 1:
                    g = [g for g, _ in GROUPS].index(name)
                    pe.wait_ge(w_lo_done, g + 1)
                    pe.wait_ge(w_lo_pool, g + 1)
                pj.wait_free(pe, name, t)
                dve_u.wait(pe, "lo", t)
                bank = pj.bank(name, t)
                if name == "gqk":
                    mm = features(t, bank, 0, COL[name], 4)
                elif name == "sq":
                    mm = features(t, bank, 0, COL[name], 4)
                elif name == "gates":
                    mm = features(t, bank, 0, COL["gg"], DT, step=NS)
                elif name == "sklow":
                    features(t, bank, 0, COL[name], 1)
                    mm = rows(t, bank, P, COL[name] + P, P + RANK)
                else:
                    mm = rows(t, bank, 0, COL[name], 512, 0, d1)
                if d1 == DT:
                    mm.then_inc(pj.full, 1)

            def scores(t, pair):
                units = [f"s{2 * pair + h}" for h in range(KVH)]
                for name in units:
                    at_ring.wait_free(pe, name, t)
                if pair == 0:
                    pj.wait_freed(pe, "sq", t)
                    pj.wait_freed(pe, "sklow", t)
                    if not (t.static and t.off == 0):
                        win_kept.wait(pe, "win", t + -1)
                for i in range(2):
                    for h, name in enumerate(units):
                        r = h * HD
                        mm = nc.tensor.matmul(at_ring.bank(name, t)[:, i * 2 * P:(i + 1) * 2 * P],
                                              sq[r:r + HD, t.p, 2 * pair + i, :], kwin[r:r + HD, t.p, :],
                                              start=True, stop=True)
                        if i == 1:
                            mm.then_inc(at_ring.full, 1)

            def turn_probs(t, u):
                name = f"pt{u}"
                tr.wait_free(pe, name, t)
                act_w.wait(pe, f"p{u}", t)
                bank = tr.bank(name, t)
                for i in range(2):
                    tp = nc.tensor.transpose(bank[:, i * P:i * P + P], PR[:, u % 2, i, :], ident[:, :])
                tp.then_inc(tr.full, 1)

            def values(t, u):
                if u == 0 and not (t.static and t.off == 0):
                    dve_o.wait(pe, "sg", t + -1)
                tr.wait_freed(pe, f"pt{u}", t)
                h = u % 2
                for i in range(2):
                    c = (u // 2 * 2 + i) * P + h * HD
                    for kb in range(2):
                        mm = nc.tensor.matmul(accS[:, c:c + HD], PT[:, u % 2, i, kb, :],
                                              vwin[:, t.p, kb, h * HD:h * HD + HD], start=kb == 0, stop=kb == 1)
                mm.then_inc(pe_pv.sem, 1)

            def turn_low(t):
                tr.wait_free(pe, "glT", t)
                pj.wait_freed(pe, "sklow", t)
                nc.tensor.transpose(tr.bank("glT", t)[0:RANK, 0:P], glow[:, t.p, :], ident[:, :]).then_inc(tr.full, 1)

            def gate_up(t):
                tr.wait_free(pe, "z", t)
                tr.wait_freed(pe, "glT", t)
                bank = tr.bank("z", t)
                for f in range(FT):
                    mm = nc.tensor.matmul(bank[:, f * P:f * P + P], wgu[:, f * P:f * P + P], glT[:, :],
                                          start=True, stop=True)
                mm.then_inc(tr.full, 1)

            def leaf_scores(t):
                for h in range(2):
                    at_ring.wait_free(pe, f"leaf{h}", t)
                dve_g.wait(pe, "leaf", t)
                for f in range(FT):
                    for h in range(2):
                        r = h * DK
                        mm = nc.tensor.matmul(at_ring.bank(f"leaf{h}", t)[:, f * P:f * P + P],
                                              EX[r:r + DK, S_LEAFK, f, :], QL[r:r + DK, f, :], start=True, stop=True)
                        if f == FT - 1:
                            mm.then_inc(at_ring.full, 1)

            def level_scores(t, name, l0):
                at_ring.wait_free(pe, name, t)
                dve_g.wait(pe, "QF", t)
                bank = at_ring.bank(name, t)
                for l in range(2):
                    for f in range(FT):
                        c = (l * FT + f) * P
                        mm = nc.tensor.matmul(bank[:, c:c + P], EX[:, l0 + l, f, :],
                                              QE[:, l0 + l, f].rearrange("p h c -> p (h c)"), start=True, stop=True)
                mm.then_inc(at_ring.full, 1)

            def turn_keys(t):
                tr.wait_free(pe, "KST", t)
                dve_g.wait(pe, "QF", t)
                for f in range(FT):
                    tp = nc.tensor.transpose(tr.bank("KST", t)[:, f * P:f * P + P], EX[:, S_STATE, f, :], ident[:, :])
                tp.then_inc(tr.full, 1)

            def gla_out(t):
                if not (t.static and t.off == 0):
                    dve_o.wait(pe, "gg", t + -1)
                    tr.wait_freed(pe, "SU", t + -1)
                at_ring.wait_freed(pe, "L2", t)
                pj.wait_freed(pe, "gv", t)
                for f in range(FT):
                    nc.tensor.matmul(accG[:, f * 2 * DV:(f + 1) * 2 * DV], EX[:, S_INTER, f, :],
                                     S_bd[:, f].rearrange("p h c -> p (h c)"), start=f == 0, stop=False,
                                     skip_group_check=True)
                for h in range(HG):
                    mm = nc.tensor.matmul(accG[:, h * DV:h * DV + DV], AT[:, h, :],
                                          gv[:, t.p, h * DV:h * DV + DV], start=False, stop=h == HG - 1,
                                          skip_group_check=True)
                mm.then_inc(pe_o.sem, 1)

            def state_update(t):
                tr.wait_free(pe, "SU", t)
                tr.wait_freed(pe, "KST", t)
                bank = tr.bank("SU", t)
                for h in range(HG):
                    r, f = DK * (h % 2), h // 2
                    mm = nc.tensor.matmul(bank[r:r + DK, f * DV:f * DV + DV], KST[:, h * DK:h * DK + DK],
                                          gv[:, t.p, h * DV:h * DV + DV], start=True, stop=True)
                mm.then_inc(tr.full, 1)

            def turn_out(t, g):
                n = t.tokens
                name = f"og{g}"
                tr.wait_free(pe, name, t)
                dve_o.wait(pe, f"gsc{g}", t)
                bank = tr.bank(name, t)
                for k in range(4):
                    c = (4 * g + k) * P
                    tp = nc.tensor.transpose(bank[:, k * P:k * P + n], gates[0:n, c:c + P], ident[0:n, 0:n])
                tp.then_inc(tr.full, 1)

            def out_proj(t, g):
                n = t.tokens
                name = f"y{g}"
                at_ring.wait_free(pe, name, t)
                if g == 0:
                    tr.wait_freed(pe, "og1", t)
                    if t.static and t.off == 0:
                        pe.wait_ge(w_lo_done, NG)
                        pe.wait_ge(w_lo_pool, NG)
                c = g * D // OUT_GROUPS
                split_product(at_ring.bank(name, t)[0:n, :],
                              [(ogT_hi[:, f, 0:n], ogT_lo[:, f, 0:n], wo_hi[:, f, c:c + 512], wo_lo[:, f, c:c + 512])
                               for f in range(DT)]).then_inc(at_ring.full, 1)

            S = Tile(NT)

            def s_begin(name):
                pj.wait_free(pe, name, S)
                return pj.bank(name, S)

            def s_turn_low():
                bank = s_begin("low")
                pj.wait_freed(pe, "sklow", S)
                nc.tensor.transpose(bank[0:RANK, 0:NS], glow[0:NS, S.p, :], ident[0:NS, 0:NS]).then_inc(pj.full, 1)

            def s_gate_up():
                bank = s_begin("z")
                pj.wait_freed(pe, "low", S)
                for f in range(FT):
                    mm = nc.tensor.matmul(bank[:, f * NS:f * NS + NS], wgu[:, f * P:f * P + P], glT[:, 0:NS],
                                          start=True, stop=True)
                mm.then_inc(pj.full, 1)

            def s_turn_keys():
                bank = s_begin("kt")
                for f in range(FT):
                    tp = nc.tensor.transpose(bank[0:NS, f * P:f * P + P], gk[:, S.p, f, 0:NS], ident[:, :])
                tp.then_inc(pj.full, 1)

            def s_scores(i):
                bank = s_begin(f"sc{i}")
                after(pe, "dve_qs")
                for b in range(4):
                    mm = nc.tensor.matmul(bank[0:8, b * P:b * P + P], s_qs[:, 4 * i + b, :], s_kT[:, 4 * i + b, :],
                                          start=True, stop=True)
                mm.then_inc(pj.full, 1)

            def s_outer(r):
                bank = s_begin(f"kv{r}")
                after(pe, "dve_km")
                for b in range(2):
                    for h in range(HG):
                        c, o = (2 * b + h // 2) * DV, DK * (h % 2)
                        mm = nc.tensor.matmul(bank[o:o + DK, c:c + DV], s_km[:, 2 * r + b, h * DK:h * DK + DK],
                                              gv[0:NS, S.p, h * DV:h * DV + DV], start=True, stop=True)
                mm.then_inc(pj.full, 1)

            def s_turn_probs():
                bank = s_begin("pT")
                after(pe, "dve_pn")
                for b in range(NS):
                    tp = nc.tensor.transpose(bank[:, 8 * b:8 * b + 8], s_p[:, b, :], ident[0:8, 0:8])
                tp.then_inc(pj.full, 1)

            def s_values():
                bank = s_begin("pv")
                pj.wait_freed(pe, "pT", S)
                pe.wait_ge(v_in, 32)
                for b in range(NS):
                    mm = nc.tensor.matmul(bank[:, 8 * b:8 * b + 8], s_v[:, b, :], s_pT[:, b, :], start=True, stop=True)
                mm.then_inc(pj.full, 1)

            def s_gla_out():
                bank = s_begin("o")
                pj.wait_freed(pe, "kv3", S)
                after(pe, "dve_q2")
                for b in range(NS):
                    for f in range(FT):
                        c = b * HG + f * 2
                        mm = nc.tensor.matmul(bank[:, c:c + 2], s_state[:, b, f, :], s_q2[:, f, b, :],
                                              start=True, stop=True)
                mm.then_inc(pj.full, 1)

            def s_sum(name, step, src):
                bank = s_begin(name)
                after(pe, step)
                nc.tensor.matmul(bank[:, 0:src.shape[1]], ones[:, :].broadcast_to([P, P]), src, start=True, stop=True
                                 ).then_inc(pj.full, 1)

            def s_out_proj():
                bank = s_begin("y")
                after(pe, "dve_lo")
                for k in range(DT):
                    c = k * P
                    mm = split_product(bank[:, k * NS:k * NS + NS],
                                       [(wo_hi[:, f, c:c + P], wo_lo[:, f, c:c + P], s_ogh[:, f, :], s_ogl[:, f, :])
                                        for f in range(DT)])
                mm.then_inc(pj.full, 1)

            pe.wait_ge(ones_set, 1)
            for name, n in pj.head[:-4]:
                if name == "bc":
                    bc(Tile(n))
                else:
                    proj(Tile(n), name)
            pe.wait_ge(init, 1)

            def body(t):
                nxt = t + 1
                early = t.static and t.off == 0
                turn_low(t)
                if early:
                    proj(t, "gg")
                    scores(t, 0)
                    gate_up(t)
                else:
                    proj(nxt, "gqk")
                    gate_up(t)
                    scores(t, 0)
                if early:
                    proj(t, "sg")
                else:
                    proj(nxt, "sq")
                turn_probs(t, 0)
                turn_probs(t, 1)
                scores(t, 1)
                values(t, 0)
                values(t, 1)
                if not early:
                    proj(nxt, "sklow")
                turn_probs(t, 2)
                turn_probs(t, 3)
                leaf_scores(t)
                if not early:
                    proj(nxt, "gv")
                values(t, 2)
                level_scores(t, "L1", 0)
                values(t, 3)
                level_scores(t, "L2", 2)
                turn_keys(t)
                proj(nxt, "gg", 3)
                gla_out(t)
                state_update(t)
                proj_rest(nxt, "gg", 3)
                proj(nxt, "sg", 5)
                turn_out(t, 0)
                turn_out(t, 1)
                proj_rest(nxt, "sg", 5)
                out_proj(t, 0)
                if not (t.static and t.off + 2 > NT):
                    bc(t + 2)
                out_proj(t, 1)

            iterations(pe, body)
            t = Tile(NT - 1)
            turn_low(t)
            proj(S, "gqk")
            gate_up(t)
            scores(t, 0)
            proj(S, "sq")
            proj(S, "sklow")
            turn_probs(t, 0)
            turn_probs(t, 1)
            scores(t, 1)
            proj(S, "gv")
            s_turn_low()
            values(t, 0)
            proj(S, "gates")
            values(t, 1)
            turn_probs(t, 2)
            turn_probs(t, 3)
            s_gate_up()
            leaf_scores(t)
            values(t, 2)
            level_scores(t, "L1", 0)
            values(t, 3)
            level_scores(t, "L2", 2)
            s_turn_keys()
            turn_keys(t)
            gla_out(t)
            state_update(t)
            s_outer(0)
            s_outer(1)
            turn_out(t, 0)
            turn_out(t, 1)
            s_scores(0)
            s_scores(1)
            out_proj(t, 0)
            s_outer(2)
            s_outer(3)
            s_turn_probs()
            s_values()
            s_gla_out()
            s_sum("ss", "dve_sq", s_on[:, 0, :])
            out_proj(t, 1)
            s_out_proj()
            s_sum("hs", "dve_hsum", s_hn[:, 0, :])

        @block.scalar
        def _(act):
            def square_rows(t):
                n, s = t.tokens, xst[0:t.tokens, t.p]
                act.wait_ge(xq_in, (t.n + 1) * 16)
                nc.scalar.activation(xq[0:n, :], xq[0:n, :], ACT.Square, accum_out=s[:, 0:1]).then_inc(act_u.sem, 1)

            def norm_rows(t):
                s = xst[0:t.tokens, t.p]
                dve_u.wait(act, "ms", t)
                nc.scalar.activation(s[:, 2:3], s[:, 1:2], ACT.Ln).then_inc(act_u.sem, 1)
                act_u.wait(act, "ln", t)
                nc.scalar.activation(s[:, 3:4], s[:, 2:3], ACT.Exp, scale=-0.5).then_inc(act_u.sem, 1)

            def split_u(t):
                n = t.tokens
                pj.wait_freed(act, "bc", t)
                if not (t.static and t.off < 2):
                    pj.wait_full(act, "sg", t + -2)
                nc.scalar.copy(u_hi[:, t.p, :, 0:n], xT[:, :, 0:n]).then_inc(act_u.sem, 1)

            def take_qk(t):
                n = t.tokens
                pj.wait_full(act, "gqk", t)
                bank = pj.bank("gqk", t)[:, :].rearrange("p (f c) -> p f c", f=4)
                nc.scalar.activation(gq[:, t.p, :, 0:n], bank[:, 0:2, 0:n], ACT.Identity, scale=invq[:, 0:1])
                nc.scalar.activation(gk[:, t.p, :, 0:n], bank[:, 2:4, 0:n], ACT.Identity,
                                     scale=inv[:, 0:1]).then_inc(pj.freed["act"], 1)

            def take_sq(t):
                n = t.tokens
                pj.wait_full(act, "sq", t)
                bank = pj.bank("sq", t)[:, :].rearrange("p (f c) -> p f c", f=4)
                nc.scalar.activation(sq[:, t.p, :, 0:n], bank[:, :, 0:n], ACT.Identity,
                                     scale=invq[:, 1:2]).then_inc(pj.freed["act"], 1)

            def take_gate(t, g):
                n, name = t.tokens, ("gg", "sg")[g]
                pj.wait_full(act, name, t)
                if g == 0 and not (t.static and t.off == 0):
                    tr.wait_full(act, "og1", t + -1)
                nc.scalar.activation(gates[0:n, g * 512:g * 512 + 512], pj.bank(name, t)[0:n, :], ACT.Silu,
                                     scale=inv[0:n, 4 + g:5 + g]).then_inc(pj.freed["act"], 1)

            def take_low(t):
                tr.wait_full(act, "glT", t)
                nc.scalar.copy(glT[:, :], tr.bank("glT", t)[0:RANK, 0:P]).then_inc(tr.freed["act"], 1)

            def log_gate(t):
                tr.wait_freed(act, "z", t)
                nc.scalar.activation(EX[:, 1], EX[:, 0], ACT.Abs).then_inc(act_g.sem, 1)
                act_g.wait(act, "az", t)
                nc.scalar.activation(EX[:, 1], EX[:, 1], ACT.Exp, scale=-1.0).then_inc(act_g.sem, 1)
                act_g.wait(act, "ez", t)
                nc.scalar.activation(EX[:, 1], EX[:, 1], ACT.Ln, bias=1.0).then_inc(act_g.sem, 1)

            def decays(t):
                dve_g.wait(act, "scan", t)
                nc.scalar.activation(EX[:, S_INTER], bsum[:, :, :], ACT.Exp, scale=1 / TAU)
                nc.scalar.activation(dec[:, :].unsqueeze(2), bsum[:, :, P - 1:P], ACT.Exp, scale=1 / TAU)
                pool_g.wait(act, "leaf", t)
                nc.scalar.activation(EX[:, S_LEAFK], EX[:, S_LEAFQ], ACT.Exp, scale=-1 / TAU)
                nc.scalar.activation(EX[:, S_LEAFQ], EX[:, S_LEAFQ], ACT.Exp, scale=1 / TAU).then_inc(act_g.sem, 1)
                pool_g.wait(act, "D", t)
                dve_g.wait(act, "D", t)
                nc.scalar.activation(EX[:, 0:5], EX[:, 0:5], ACT.Exp, scale=1 / TAU).then_inc(act_g.sem, 1)

            def probs(t, u):
                at_ring.wait_freed(act, f"s{u}", t)
                for i in range(2):
                    k = head(u, i)
                    e = nc.scalar.activation(PR[:, u % 2, i, :], PR[:, u % 2, i, :], ACT.Exp, scale=-1.0,
                                             bias=wst[:, 0, k:k + 1], accum_out=wst[:, 1, k:k + 1])
                e.then_inc(act_w.sem, 1)

            def sink_term(t):
                dve_w.wait(act, "esi", t)
                nc.scalar.activation(wst[:, 2, :], wst[:, 2, :], ACT.Exp).then_inc(act_w.sem, 1)

            def take_kst(t):
                tr.wait_full(act, "KST", t)
                nc.scalar.copy(KST[:, :], tr.bank("KST", t)[:, 0:2 * P]).then_inc(tr.freed["act"], 1)

            def head_norm(t):
                n = t.tokens
                pe_o.wait(act, "o", t)
                for h in range(HG):
                    sq_ = nc.scalar.activation(junk[0:n, h * DV:h * DV + DV], accG[0:n, h * DV:h * DV + DV], ACT.Square,
                                               accum_out=ost[0:n, 0, h:h + 1])
                sq_.then_inc(act_o.sem, 1)
                dve_o.wait(act, "oms", t)
                nc.scalar.activation(ost[0:n, 2, :], ost[0:n, 1, :], ACT.Ln).then_inc(act_o.sem, 1)
                act_o.wait(act, "oln", t)
                nc.scalar.activation(ost[0:n, 3, :], ost[0:n, 2, :], ACT.Exp, scale=-0.5).then_inc(act_o.sem, 1)

            def take_out(t, g):
                n = t.tokens
                tr.wait_full(act, f"og{g}", t)
                bank = tr.bank(f"og{g}", t)[:, :].rearrange("p (f c) -> p f c", f=4)
                nc.scalar.copy(ogT_hi[:, 4 * g:4 * g + 4, 0:n], bank[:, :, 0:n]).then_inc(act_o.sem, 1)

            def final_norm(t):
                n = t.tokens
                at_ring.wait_freed(act, "y1", t)
                nc.scalar.activation(junk[0:n, :], xres[0:n, :], ACT.Square, accum_out=hst[0:n, 0:1]
                                     ).then_inc(act_o.sem, 1)
                dve_o.wait(act, "hms", t)
                nc.scalar.activation(hst[0:n, 2:3], hst[0:n, 1:2], ACT.Ln).then_inc(act_o.sem, 1)
                act_o.wait(act, "hln", t)
                nc.scalar.activation(hst[0:n, 3:4], hst[0:n, 2:3], ACT.Exp, scale=-0.5).then_inc(act_o.sem, 1)

            def split_w(g):
                act.wait_ge(w_scaled, g + 1)
                if g == len(GROUPS):
                    act.wait_ge(w_lo_done, g)
                    act.wait_ge(w_lo_pool, g)
                src, hi = staged(g), w_slice(g, w_hi, wo_hi)
                for d in range(DVE_TILES[g]):
                    h = nc.scalar.activation(hi[:, d], src[:, d], ACT.Identity, scale=gs[:, g % 2, d:d + 1])
                h.then_inc(w_hi_done, 1)
                for d in range(DVE_TILES[g], DT):
                    h = nc.scalar.activation(src[:, d], src[:, d], ACT.Identity, scale=gs[:, g % 2, d:d + 1])
                h.then_inc(w_in_place, 1)
                act.wait_ge(w_in_place, g + 1)
                nc.scalar.copy(hi[:, DVE_TILES[g]:DT], src[:, DVE_TILES[g]:DT]).then_inc(w_hi_pool, 1)

            S = Tile(NT)

            def s_step(out, x, fn, **kw):
                nc.scalar.activation(out, x, fn, **kw).then_inc(smp["act"].sem, 1)

            def s_low():
                pj.wait_full(act, "low", S)
                nc.scalar.copy(glT[:, 0:NS], pj.bank("low", S)[0:RANK, 0:NS]).then_inc(pj.freed["act"], 1)

            def s_take_gates():
                pj.wait_full(act, "gates", S)
                bank = pj.bank("gates", S)[:, 0:DT * NS].rearrange("p (d b) -> p d b", d=DT)
                nc.scalar.activation(s_gates[:, 0:4], bank[:, 0:4], ACT.Silu, scale=inv[:, 4:5])
                nc.scalar.activation(s_gates[:, 4:8], bank[:, 4:8], ACT.Silu, scale=inv[:, 5:6]
                                     ).then_inc(pj.freed["act"], 1)
                nc.scalar.preload_act_table_set(LOG_EXP_SET)

            def s_log_gate():
                pj.wait_freed(act, "z", S)
                s_step(s_z[:, 1], s_z[:, 0], ACT.Abs)
                after(act, "act_az")
                s_step(s_z[:, 1], s_z[:, 1], ACT.Exp, scale=-1.0)
                after(act, "act_ez")
                s_step(s_z[:, 1], s_z[:, 1], ACT.Ln, bias=1.0)

            def s_decay():
                after(act, "dve_la")
                s_step(s_z[:, 4], s_z[:, 3], ACT.Exp, scale=1 / TAU)

            def s_probs():
                after(act, "dve_esi")
                pj.wait_freed(act, "sc1", S)
                nc.scalar.activation(s_p, s_p, ACT.Exp)
                s_step(s_st[:, 3, :], s_st[:, 2, :], ACT.Exp)

            def s_rsqrt(x, ln, out, ready, names):
                pj.wait_freed(act, ready, S)
                s_step(ln, x, ACT.Ln)
                after(act, f"act_{names[0]}")
                s_step(out, ln, ACT.Exp, scale=-0.5)

            for dst, src in ((ident[:, :], ident_d), (gin[:, :], gin_d)):
                act.dma_start(dst, src).then_inc(first_in, 16)
            nc.scalar.preload_act_table_set(LOG_EXP_SET)
            square_rows(Tile(0))
            norm_rows(Tile(0))
            split_u(Tile(0))
            for g in range(NG):
                if g == NG - 1:
                    take_low(Tile(0))
                    act.wait_ge(w_lo_pool, g)
                    log_gate(Tile(0))
                    probs(Tile(0), 0)
                    probs(Tile(0), 1)
                split_w(g)
                if g == 0:
                    square_rows(Tile(1))
                if g == 1:
                    norm_rows(Tile(1))
                    take_qk(Tile(0))
                if g == 2:
                    split_u(Tile(1))
                    take_sq(Tile(0))
                if g == 3:
                    take_qk(Tile(1))
                if g == 4:
                    take_sq(Tile(1))

            def body(t):
                nxt = t + 1
                early = t.static and t.off == 0
                if not early:
                    take_low(t)
                    take_qk(nxt)
                    log_gate(t)
                    probs(t, 0)
                    probs(t, 1)
                    take_sq(nxt)
                decays(t)
                if early:
                    act.wait_ge(w_lo_done, NG)
                    act.wait_ge(w_lo_pool, NG)
                probs(t, 2)
                probs(t, 3)
                sink_term(t)
                if early:
                    take_gate(t, 0)
                    take_gate(t, 1)
                    nc.scalar.preload_act_table_set(LOG_EXP_SET)
                take_kst(t)
                if not (t.static and t.off + 2 > NT):
                    square_rows(t + 2)
                head_norm(t)
                take_out(t, 0)
                take_out(t, 1)
                if not (t.static and t.off + 2 > NT):
                    norm_rows(t + 2)
                take_gate(nxt, 0)
                take_gate(nxt, 1)
                nc.scalar.preload_act_table_set(LOG_EXP_SET)
                if not (t.static and t.off + 2 > NT):
                    split_u(t + 2)
                final_norm(t)

            iterations(act, body)
            t = Tile(NT - 1)
            take_low(t)
            take_qk(S)
            log_gate(t)
            probs(t, 0)
            probs(t, 1)
            take_sq(S)
            decays(t)
            probs(t, 2)
            probs(t, 3)
            s_low()
            sink_term(t)
            s_take_gates()
            take_kst(t)
            s_log_gate()
            head_norm(t)
            s_decay()
            take_out(t, 0)
            take_out(t, 1)
            s_probs()
            s_rsqrt(s_on[:, 1, :], s_on[:, 2, :], s_on[:, 3, :], "ss", ["oln"])
            final_norm(t)
            s_rsqrt(s_hn[:, 1, :], s_hn[:, 2, :], s_hn[:, 3, :], "hs", ["hln"])

        @block.vector
        def _(dve):
            V = nc.vector

            def rsqrt_step(ev, names, a, y0, tmp, y, t, gain=1.0):
                V.tensor_tensor(tmp, y0, y0, ALU.mult).then_inc(ev.sem, 1)
                ev.wait(dve, names[0], t)
                V.scalar_tensor_tensor(out=tmp, in0=tmp, scalar=-0.5 * gain, in1=a, op0=ALU.mult,
                                       op1=ALU.mult).then_inc(ev.sem, 1)
                ev.wait(dve, names[1], t)
                V.scalar_tensor_tensor(out=y, in0=tmp, scalar=1.5 * gain, in1=y0, op0=ALU.add,
                                       op1=ALU.mult).then_inc(ev.sem, 1)
                ev.wait(dve, names[2], t)

            def mean_square(t):
                s = xst[0:t.tokens, t.p]
                act_u.wait(dve, "ssq", t)
                V.tensor_scalar(s[:, 1:2], s[:, 0:1], 1.0 / D, EPS, ALU.mult, ALU.add).then_inc(dve_u.sem, 1)

            def norm_x(t):
                n, s = t.tokens, xst[0:t.tokens, t.p]
                act_u.wait(dve, "exp", t)
                rsqrt_step(dve_u, ["n0", "n1", "rstd"], s[:, 1:2], s[:, 3:4], s[:, 4:5], s[:, 5:6], t, U_SCALE)
                if not (t.static and t.off == 0):
                    pj.wait_full(dve, "bc", t + -1)
                V.tensor_scalar(diag[0:n, 0:n], ident[0:n, 0:n], s[:, 5:6], None, ALU.mult).then_inc(dve_u.sem, 1)

            def scale_u(t):
                n = t.tokens
                dve.wait_ge(xT_in, (t.n + 1) * 16)
                pj.wait_full(dve, "bc", t)
                V.tensor_tensor(xT[:, :, 0:n], xT[:, :, 0:n], bcast(pj.bank("bc", t)[:, 0:n], 1, DT),
                                ALU.mult).then_inc(pj.freed["dve"], 1)

            def split_u(t):
                n = t.tokens
                act_u.wait(dve, "hi", t)
                V.tensor_tensor(u_lo[:, t.p, :, 0:n], xT[:, :, 0:n], u_hi[:, t.p, :, 0:n],
                                ALU.subtract).then_inc(dve_u.sem, 1)

            def take_kv(t):
                n = t.tokens
                pj.wait_full(dve, "sklow", t)
                bank = pj.bank("sklow", t)
                if t.sample:
                    V.tensor_scalar(s_knew[:, :], bank[:, 0:n], inv[:, 2:3], None, ALU.mult)
                    V.tensor_scalar(s_vnew, bank[0:n, P:2 * P], inv[0:n, 2:3], None, ALU.mult)
                else:
                    V.tensor_scalar(kwin[:, t.p, P:2 * P], bank[:, 0:P], inv[:, 2:3], None, ALU.mult)
                    V.tensor_scalar(vwin[:, t.p, 1, :], bank[:, P:2 * P], inv[:, 2:3], None, ALU.mult)
                V.tensor_scalar(glow[0:n, t.p, :], bank[0:n, 2 * P:2 * P + RANK], inv[0:n, 2:3], None,
                                ALU.mult).then_inc(pj.freed["dve"], 1)

            def take_gv(t):
                n = t.tokens
                pj.wait_full(dve, "gv", t)
                V.tensor_scalar(gv[0:n, t.p, :], pj.bank("gv", t)[0:n, :], inv[0:n, 3:4], None,
                                ALU.mult).then_inc(pj.freed["dve"], 1)

            def take_z(t):
                tr.wait_full(dve, "z", t)
                bank = tr.bank("z", t)
                for f in range(FT):
                    z = V.tensor_scalar(EX[:, 0, f, :], bank[:, f * P:f * P + P], bg[:, f:f + 1], None, ALU.add)
                z.then_inc(tr.freed["dve"], 1)
                tr.wait_freed(dve, "z", t)
                V.tensor_scalar(EX[:, 2], EX[:, 0], 0.0, None, ALU.min).then_inc(dve_g.sem, 1)

            def sums(t):
                act_g.wait(dve, "l1", t)
                dve_g.wait(dve, "mz", t)
                V.tensor_tensor(EX[:, 2], EX[:, 2], EX[:, 1], ALU.subtract).then_inc(dve_g.sem, 1)
                dve_g.wait(dve, "la", t)
                V.tensor_scalar(EX[:, 3], EX[:, 2], LEAF_FLOOR * TAU, None, ALU.max).then_inc(dve_g.sem, 1)
                dve_g.wait(dve, "lc", t)
                for f in range(FT):
                    V.tensor_tensor_scan(bsum[:, f, :], leafscan[:, 0, :], EX[:, 2, f, :], 0.0, ALU.mult, ALU.add)
                    sc = V.tensor_tensor_scan(lsum[:, f, :], leafscan[:, 1, :], EX[:, 3, f, :], 0.0, ALU.mult, ALU.add)
                sc.then_inc(dve_g.sem, 1)
                dve_g.wait(dve, "scan", t)
                for l in range(DVE_LEVELS):
                    level_differences(V, l)
                V.tensor_tensor(EX[:, S_STATE], bsum[:, :, P - 1:P].broadcast_to([P, FT, P]), bsum[:, :, :],
                                ALU.subtract).then_inc(dve_g.sem, 1)

            def factors(t):
                act_g.wait(dve, "leaf", t)
                V.tensor_tensor(QL, gq[:, t.p], EX[:, S_LEAFQ], ALU.mult)
                V.tensor_tensor(EX[:, S_LEAFK], EX[:, S_LEAFK], gk[:, t.p], ALU.mult).then_inc(dve_g.sem, 1)
                act_g.wait(dve, "E", t)
                for l, s in enumerate(LEVELS):
                    for h in range(2):
                        r = h * DK
                        late = lambda ap: ap.rearrange("p f (b c) -> p f b c", c=2 * s)[:, :, :, s:2 * s]
                        V.tensor_tensor(QE[r:r + DK, l, :, h, :].rearrange("p f (b c) -> p f b c", c=s),
                                        late(gq[r:r + DK, t.p]), late(EX[r:r + DK, l]), ALU.mult)
                V.tensor_tensor(EX[:, S_INTER], EX[:, S_INTER], gq[:, t.p], ALU.mult).then_inc(dve_g.sem, 1)
                dve_g.wait(dve, "Q", t)
                V.tensor_tensor(EX[:, 0:5], EX[:, 0:5], bcast(gk[:, t.p], 1, 5), ALU.mult).then_inc(dve_g.sem, 1)

            def assemble_leaves(t):
                for h in range(2):
                    at_ring.wait_full(dve, f"leaf{h}", t)
                    V.tensor_tensor(heads_of(h), at_ring.bank(f"leaf{h}", t)[:, 0:FT * P].rearrange(
                        "p (f c) -> p f c", f=FT), bcast(leafmask[:, :], 1, FT), ALU.mult
                                    ).then_inc(at_ring.freed["dve"], 1)

            def assemble_levels(t):
                at_ring.wait_freed(dve, "leaf1", t)
                at_ring.wait_full(dve, "L1", t)
                lv = at_ring.bank("L1", t)[:, :].rearrange("p (l h c) -> p l h c", l=2, h=HG)
                V.tensor_copy(AT[0:64, :, 64:128], lv[0:64, 0])
                V.tensor_copy(AT[0:32, :, 32:64], lv[0:32, 1, :, 0:32])
                V.tensor_copy(AT[64:96, :, 96:128], lv[64:96, 1, :, 32:64]).then_inc(at_ring.freed["dve"], 1)
                at_ring.wait_freed(dve, "L1", t)
                at_ring.wait_full(dve, "L2", t)
                if not (t.static and t.off == 0):
                    pe_pv.wait(dve, "pv3", t + -1)
                V.tensor_copy(kwin[:, 1 - t.p, 0:P], kwin[:, t.p, P:2 * P])
                masked_copy(t, 2).then_inc(dve_g.sem, 1)
                dve_g.wait(dve, "L16", t)
                V.tensor_copy(vwin[:, 1 - t.p, 0, :], vwin[:, t.p, 1, :]).then_inc(win_kept.sem, 1)
                masked_copy(t, 3).then_inc(at_ring.freed["dve"], 1)

            def heads_of(h):
                return AT.rearrange("p (f h) c -> p f h c", h=2)[:, :, h, :]

            def masked_copy(t, l):
                s = LEVELS[l]
                return V.copy_predicated(
                    AT.rearrange("p h (b c) -> p h b c", c=2 * s)[:, :, :, s:2 * s],
                    bcast(lvlmask[:, l, :].bitcast(I32).rearrange("p (b c) -> p b c", c=s), 1, HG),
                    at_ring.bank("L2", t)[:, (l - 2) * 256:(l - 1) * 256].rearrange(
                        "p (h b c) -> p h b c", h=HG, c=s))

            def update_state(t):
                tr.wait_full(dve, "SU", t)
                bank = tr.bank("SU", t)
                for h in range(HG):
                    r, f = DK * (h % 2), h // 2
                    s = S_bd[r:r + DK, f, h % 2, :]
                    up = V.scalar_tensor_tensor(out=s, in0=s, scalar=dec[r:r + DK, f:f + 1],
                                                in1=bank[r:r + DK, f * DV:f * DV + DV], op0=ALU.mult, op1=ALU.add)
                up.then_inc(tr.freed["dve"], 1)

            def row_max(t, u):
                at_ring.wait_full(dve, f"s{u}", t)
                if u >= 2:
                    tr.wait_full(dve, f"pt{u - 2}", t)
                elif not (t.static and t.off == 0):
                    tr.wait_full(dve, f"pt{u + 2}", t + -1)
                first = 1 if t.static and t.off == 0 else 0
                bank = at_ring.bank(f"s{u}", t)[:, :].rearrange("p (h c) -> p h c", h=2)
                V.tensor_copy(wst[:, 3, u:u + 1], nsink[:, u:u + 1])
                V.copy_predicated(bank[:, :, P:2 * P], bcast(older[:, :].bitcast(I32), 1, 2), bank[:, :, 0:P]
                                  ).then_inc(dve_w.sem, 1)
                dve_w.wait(dve, f"m{u}", t)
                V.tensor_copy(wst[:, 3, u:u + 1], nsink[:, u:u + 1])
                for i in range(2):
                    k = head(u, i)
                    m = V.tensor_tensor_reduce(PR[:, u % 2, i, :], bank[:, i, P:2 * P], band[:, first], -1.0,
                                               nsink[:, k:k + 1], ALU.add, ALU.min, wst[:, 0, k:k + 1])
                m.then_inc(at_ring.freed["dve"], 1)

            def take_pt(t, u):
                tr.wait_full(dve, f"pt{u}", t)
                if u >= 2:
                    pe_pv.wait(dve, f"pv{u - 2}", t)
                elif not (t.static and t.off == 0):
                    pe_pv.wait(dve, f"pv{u + 2}", t + -1)
                V.tensor_tensor(PT[:, u % 2], bcast(tr.bank(f"pt{u}", t)[:, 0:2 * P].rearrange(
                    "p (h c) -> p h c", h=2), 2, 2), bcast(window[:, :, :], 1, 2), ALU.mult
                                ).then_inc(tr.freed["dve"], 1)

            def denominators(t):
                at_ring.wait_freed(dve, "s3", t)
                V.tensor_tensor(wst[:, 2, :], wst[:, 0, :], sink[:, :], ALU.add).then_inc(dve_w.sem, 1)
                act_w.wait(dve, "es", t)
                V.tensor_tensor(wst[:, 4, :], wst[:, 1, :], wst[:, 2, :], ALU.add).then_inc(dve_w.sem, 1)
                dve_w.wait(dve, "den", t)
                V.reciprocal(wst[:, 5, :], wst[:, 4, :]).then_inc(dve_w.sem, 1)

            def gate_window(t):
                n = t.tokens
                pool_w.wait(dve, "gs", t)
                pe_pv.wait(dve, "pv3", t)
                V.tensor_tensor(gates[0:n, 512:1024], gates[0:n, 512:1024], accS[0:n, :], ALU.mult
                                ).then_inc(dve_o.sem, 1)
                dve_o.wait(dve, "sg", t)
                V.tensor_reduce(amax[0:n, 0:1], gates[0:n, 512:1024], AX.X, ALU.max, apply_absolute_value=True
                                ).then_inc(dve_o.sem, 1)

            def mean_heads(t):
                o = ost[0:t.tokens]
                act_o.wait(dve, "oss", t)
                V.tensor_scalar(o[:, 1, :], o[:, 0, :], 1.0 / DV, EPS, ALU.mult, ALU.add).then_inc(dve_o.sem, 1)

            def gate_gla(t):
                n = t.tokens
                o = ost[0:n]
                act_o.wait(dve, "oexp", t)
                rsqrt_step(dve_o, ["on0", "on1", "orstd"], o[:, 1, :], o[:, 3, :], o[:, 4, :], o[:, 5, :], t)
                pj.wait_freed(dve, "gg", t)
                for h in range(HG):
                    g = gates[0:n, h * DV:h * DV + DV]
                    gg = V.scalar_tensor_tensor(out=g, in0=accG[0:n, h * DV:h * DV + DV], scalar=o[:, 5, h:h + 1],
                                                in1=g, op0=ALU.mult, op1=ALU.mult)
                gg.then_inc(dve_o.sem, 1)

            def scale_rows(t):
                n = t.tokens
                a = amax[0:n]
                dve_o.wait(dve, "gg", t)
                V.tensor_reduce(a[:, 1:2], gates[0:n, 0:512], AX.X, ALU.max, apply_absolute_value=True
                                ).then_inc(dve_o.sem, 1)
                dve_o.wait(dve, "am", t)
                V.tensor_scalar(a[:, 2:3], a[:, 0:1], a[:, 1:2], 1e-30, ALU.max, ALU.max).then_inc(dve_o.sem, 1)
                dve_o.wait(dve, "amc", t)
                V.reciprocal(a[:, 3:4], a[:, 2:3]).then_inc(dve_o.sem, 1)
                dve_o.wait(dve, "rsc", t)
                for g in range(2):
                    c = g * 512
                    V.tensor_scalar(gates[0:n, c:c + 512], gates[0:n, c:c + 512], a[:, 3:4], O_TOP, ALU.mult,
                                    ALU.mult).then_inc(dve_o.sem, 1)
                V.tensor_scalar(isc[0:n, :], inv[0:n, NG - 2:NG], a[:, 2:3], 1.0 / O_TOP, ALU.mult, ALU.mult
                                ).then_inc(dve_o.sem, 1)

            def take_out(t, g):
                n = t.tokens
                act_o.wait(dve, f"hi{g}", t)
                bank = tr.bank(f"og{g}", t)[:, :].rearrange("p (f c) -> p f c", f=4)
                V.tensor_tensor(ogT_lo[:, 4 * g:4 * g + 4, 0:n], bank[:, :, 0:n], ogT_hi[:, 4 * g:4 * g + 4, 0:n],
                                ALU.subtract).then_inc(tr.freed["dve"], 1)

            def residual(t, groups=range(OUT_GROUPS)):
                n = t.tokens
                dve.wait_ge(xres_in, (t.n + 1) * 16)
                dve_o.wait(dve, "isc", t)
                for g in groups:
                    at_ring.wait_full(dve, f"y{g}", t)
                    x = xres[0:n, g * 512:g * 512 + 512]
                    V.scalar_tensor_tensor(out=x, in0=at_ring.bank(f"y{g}", t)[0:n, :], scalar=isc[0:n, g:g + 1],
                                           in1=x, op0=ALU.mult, op1=ALU.add).then_inc(at_ring.freed["dve"], 1)

            def final_norm(t):
                n = t.tokens
                h = hst[0:n]
                act_o.wait(dve, "hss", t)
                V.tensor_scalar(h[:, 1:2], h[:, 0:1], 1.0 / D, EPS, ALU.mult, ALU.add).then_inc(dve_o.sem, 1)
                act_o.wait(dve, "hexp", t)
                rsqrt_step(dve_o, ["hn0", "hn1", "hr"], h[:, 1:2], h[:, 3:4], h[:, 4:5], h[:, 5:6], t)
                V.scalar_tensor_tensor(out=xres[0:n, :], in0=xres[0:n, :], scalar=h[:, 5:6], in1=normf[0:n, :],
                                       op0=ALU.mult, op1=ALU.mult).then_inc(dve_o.sem, 1)

            def w_gain(g):
                return (gin if g < len(GROUPS) else gout)[:, :]

            def max_w(g):
                s = g % 2
                if g >= 1:
                    dve.wait_ge(w_scaled, g)
                wait_staged(dve, g)
                V.tensor_reduce(wabs[:, s, :], staged(g), AX.X, ALU.max, apply_absolute_value=True).then_inc(w_dve, 1)
                dve.wait_ge(w_dve, 4 * g + 1)
                V.tensor_tensor(wabs[:, s, :], wabs[:, s, :], w_gain(g), ALU.mult).then_inc(w_dve, 1)
                dve.wait_ge(w_dve, 4 * g + 2)
                V.tensor_reduce(wcol[:, 0:1], wabs[:, s, :], AX.X, ALU.max, apply_absolute_value=True
                                ).then_inc(w_row, 1)

            def scale_w(g):
                dve.wait_ge(w_max, g + 1)
                V.tensor_scalar(wcol[:, 2:3], wcol[:, 1:2], 1.0 / W_TOP, 1e-30, ALU.mult, ALU.max).then_inc(w_dve, 1)
                dve.wait_ge(w_dve, 4 * g + 3)
                V.reciprocal(wcol[:, 3:4], wcol[:, 2:3]).then_inc(w_dve, 1)
                c = 1.0 / U_SCALE if g < len(GROUPS) else 1.0
                V.tensor_scalar(inv[:, g:g + 1], wcol[:, 2:3], c, None, ALU.mult)
                if g < 2:
                    V.tensor_scalar(invq[:, g:g + 1], wcol[:, 2:3], c * DK ** -0.5, None, ALU.mult)
                dve.wait_ge(w_dve, 4 * g + 4)
                V.tensor_scalar(gs[:, g % 2, :], w_gain(g), wcol[:, 3:4], None, ALU.mult).then_inc(w_scaled, 1)

            def lo_w(g, d0, d1):
                dve.wait_ge(w_hi_done, g + 1)
                for d in range(d0, d1):
                    lo = V.scalar_tensor_tensor(out=w_slice(g, w_lo, wo_lo)[:, d], in0=staged(g)[:, d],
                                                scalar=gs[:, g % 2, d:d + 1], in1=w_slice(g, w_hi, wo_hi)[:, d],
                                                op0=ALU.mult, op1=ALU.subtract)
                if d1 == DVE_TILES[g]:
                    lo.then_inc(w_lo_done, 1)

            S = Tile(NT)

            def s_done(ins):
                ins.then_inc(smp["dve"].sem, 1)

            def s_freed(ins):
                ins.then_inc(pj.freed["dve"], 1)

            def s_take_z():
                pj.wait_full(dve, "z", S)
                for f in range(FT):
                    z = V.tensor_scalar(s_z[:, 0, f, :], pj.bank("z", S)[:, f * NS:f * NS + NS], bg[:, f:f + 1], None,
                                        ALU.add)
                s_freed(z)
                pj.wait_freed(dve, "z", S)
                s_done(V.tensor_scalar(s_z[:, 2], s_z[:, 0], 0.0, None, ALU.min))

            def s_take_keys():
                pj.wait_full(dve, "kt", S)
                s_freed(V.tensor_copy(s_kt, pj.bank("kt", S)[0:NS, 0:HG * DK]))
                pj.wait_freed(dve, "kt", S)
                s_done(V.tensor_tensor(s_km, bcast(s_kt, 1, NS), bcast(ident[0:NS, 0:NS], 2, HG * DK), ALU.mult))

            def s_queries():
                s_done(V.memset(s_q2, 0.0))
                after(dve, "dve_qz")
                for h in range(2):
                    r = h * DK
                    q = V.tensor_copy(s_q2[r:r + DK, :, :, h], gq[r:r + DK, S.p, :, 0:NS])
                s_done(q)

            def s_log_decay():
                after(dve, "act_l1")
                s_done(V.tensor_tensor(s_z[:, 3], s_z[:, 2], s_z[:, 1], ALU.subtract))

            def s_window():
                dve.wait_ge(kT_in, 16)
                s_done(V.tensor_copy(s_kT[:, :, P - 1:P], s_knew[:, :].unsqueeze(2)))
                s_done(V.memset(s_qs, 0.0))
                after(dve, "dve_qsz")
                for h in range(KVH):
                    r = h * HD
                    q = V.tensor_copy(s_qs[r:r + HD, :, GRP * h:GRP * h + GRP],
                                      sq[r:r + HD, S.p, :, 0:NS].rearrange("p f b -> p b f"))
                s_done(q)

            def s_row_max():
                for i in range(2):
                    pj.wait_full(dve, f"sc{i}", S)
                    s_done(V.tensor_reduce(s_st[:, 0, 4 * i:4 * i + 4], pj.bank(f"sc{i}", S)[0:8, :].rearrange(
                        "p (b c) -> p b c", b=4), AX.X, ALU.max, negate=True))
                after(dve, "dve_mx")
                s_done(V.tensor_scalar(s_st[:, 1, :], s_st[:, 0, :], s_sink[:, 1:2], None, ALU.min))
                after(dve, "dve_nm")
                for i in range(2):
                    s_freed(V.tensor_tensor(s_p[:, 4 * i:4 * i + 4, :], pj.bank(f"sc{i}", S)[0:8, :].rearrange(
                        "p (b c) -> p b c", b=4), bcast(s_st[:, 1, 4 * i:4 * i + 4], 2, P), ALU.add))
                s_done(V.tensor_scalar(s_st[:, 2, :], s_st[:, 1, :], s_sink[:, 0:1], None, ALU.add))

            def s_normalise():
                after(dve, "act_exp")
                s_done(V.tensor_reduce(s_st[:, 4, :], s_p, AX.X, ALU.add))
                after(dve, "dve_sum")
                s_done(V.tensor_tensor(s_st[:, 5, :], s_st[:, 4, :], s_st[:, 3, :], ALU.add))
                after(dve, "dve_den")
                s_done(V.reciprocal(s_st[:, 6, :], s_st[:, 5, :]))
                after(dve, "dve_rden")
                s_done(V.tensor_tensor(s_p, s_p, bcast(s_st[:, 6, :], 2, P), ALU.mult))

            def s_states(r):
                if r == 0:
                    dve.wait_ge(state_in, 16)
                    after(dve, "act_a")
                pj.wait_full(dve, f"kv{r}", S)
                for b in range(2):
                    for f in range(FT):
                        s = s_state[:, 2 * r + b, f, :]
                        c = (2 * b + f) * DV
                        up = V.scalar_tensor_tensor(out=s, in0=s, scalar=s_z[:, 4, f, 2 * r + b:2 * r + b + 1],
                                                    in1=pj.bank(f"kv{r}", S)[:, c:c + DV], op0=ALU.mult, op1=ALU.add)
                s_freed(up)

            def s_take_probs():
                pj.wait_full(dve, "pT", S)
                s_freed(V.tensor_copy(s_pT, pj.bank("pT", S)[:, 0:8 * NS].rearrange("p (b h) -> p b h", b=NS)))

            def s_gate_window():
                pj.wait_freed(dve, "gates", S)
                pj.wait_full(dve, "pv", S)
                for h in range(KVH):
                    r = h * HD
                    g = V.tensor_tensor(s_og[r:r + HD, 4:8, :], pj.bank("pv", S)[r:r + HD, 0:8 * NS].rearrange(
                        "p (b h) -> p h b", b=NS)[:, GRP * h:GRP * h + GRP, :], s_gates[r:r + HD, 4:8, :], ALU.mult)
                s_freed(g)

            def s_squares():
                pj.wait_full(dve, "o", S)
                o = pj.bank("o", S)[:, 0:NS * HG]
                s_freed(V.tensor_copy(s_on[:, 6, :], o))
                pj.wait_freed(dve, "o", S)
                s_done(V.tensor_tensor(s_on[:, 0, :], s_on[:, 6, :], s_on[:, 6, :], ALU.mult))
                pj.wait_full(dve, "ss", S)
                s_freed(V.tensor_scalar(s_on[:, 1, :], pj.bank("ss", S)[:, 0:NS * HG], 1.0 / DV, EPS, ALU.mult,
                                        ALU.add))

            def s_gate_gla():
                after(dve, "act_oexp")
                rsqrt_step(smp["dve"], ["n0", "n1", "rstd"], s_on[:, 1, :], s_on[:, 3, :], s_on[:, 4, :],
                           s_on[:, 5, :], Tile(0))
                s_done(V.tensor_tensor(s_on[:, 6, :], s_on[:, 6, :], s_on[:, 5, :], ALU.mult))
                after(dve, "dve_on")
                s_done(V.tensor_tensor(s_og[:, 0:4, :], s_on[:, 6, :].rearrange("p (b h) -> p h b", b=NS),
                                       s_gates[:, 0:4, :], ALU.mult))

            def s_split_out():
                after(dve, "dve_gg")
                pj.wait_freed(dve, "pv", S)
                s_done(V.tensor_reduce(s_am[:, 0, :], s_og.rearrange("p d b -> p b d"), AX.X, ALU.max,
                                       apply_absolute_value=True))
                after(dve, "pool_am")
                s_done(V.tensor_scalar(s_am[:, 2, :], s_am[:, 1, :], 1e-30, None, ALU.max))
                after(dve, "dve_amc")
                s_done(V.reciprocal(s_am[:, 3, :], s_am[:, 2, :]))
                after(dve, "dve_rsc")
                s_done(V.tensor_scalar(s_am[:, 4, :], s_am[:, 3, :], O_TOP, None, ALU.mult))
                after(dve, "dve_rscs")
                s_done(V.tensor_tensor(s_og, s_og, bcast(s_am[:, 4, :], 1, DT), ALU.mult))
                after(dve, "dve_og")
                s_done(V.tensor_copy(s_ogh, s_og))
                after(dve, "dve_hi")
                s_done(V.tensor_tensor(s_ogl, s_og, s_ogh, ALU.subtract))
                s_done(V.tensor_scalar(s_am[:, 5, :], s_am[:, 2, :], 1.0 / O_TOP, None, ALU.mult))

            def s_residual():
                pj.wait_full(dve, "y", S)
                dve.wait_ge(sx_in, 16)
                after(dve, "dve_isc")
                s_freed(V.tensor_tensor(s_y, pj.bank("y", S)[:, 0:DT * NS].rearrange("p (d b) -> p d b", d=DT),
                                        bcast(s_am[:, 5, :], 1, DT), ALU.mult))
                pj.wait_freed(dve, "y", S)
                half = DT // OUT_GROUPS
                for g in range(OUT_GROUPS):
                    k = slice(g * half, g * half + half)
                    s_done(V.scalar_tensor_tensor(out=s_y[:, k], in0=s_y[:, k],
                                                  scalar=inv[:, len(GROUPS) + g:len(GROUPS) + g + 1], in1=s_x[:, k],
                                                  op0=ALU.mult, op1=ALU.add))
                after(dve, "dve_h1")
                s_done(V.tensor_tensor(s_h2, s_y, s_y, ALU.mult))
                after(dve, "dve_hsq")
                s_done(V.tensor_reduce(s_hn[:, 0, :], s_h2.rearrange("p d b -> p b d"), AX.X, ALU.add))
                pj.wait_full(dve, "hs", S)
                s_freed(V.tensor_scalar(s_hn[:, 1, :], pj.bank("hs", S)[:, 0:NS], 1.0 / D, EPS, ALU.mult, ALU.add))

            def s_final_norm():
                after(dve, "act_hexp")
                rsqrt_step(smp["dve"], ["hn0", "hn1", "hr"], s_hn[:, 1, :], s_hn[:, 3, :], s_hn[:, 4, :],
                           s_hn[:, 5, :], Tile(0))
                s_done(V.tensor_tensor(s_y, s_y, bcast(s_hn[:, 5, :], 1, DT), ALU.mult))
                after(dve, "dve_hn")
                s_done(V.tensor_tensor(s_y, s_y, bcast(normfT[:, :], 2, NS), ALU.mult))

            V.memset(ones[:, :], 1.0).then_inc(ones_set, 1)
            dve.wait_ge(first_in, 16 * 2)
            mean_square(Tile(0))
            norm_x(Tile(0))
            scale_u(Tile(0))
            max_w(0)
            scale_w(0)
            split_u(Tile(0))
            max_w(1)
            for g in range(NG):
                if g == NG - 1:
                    dve.wait_ge(w_lo_done, g)
                    dve.wait_ge(w_lo_pool, g)
                    take_z(Tile(0))
                    row_max(Tile(0), 0)
                    row_max(Tile(0), 1)
                    sums(Tile(0))
                lo_w(g, 0, 2)
                if g + 1 < NG:
                    scale_w(g + 1)
                lo_w(g, 2, DVE_TILES[g])
                if g == 2:
                    split_u(Tile(1))
                if g + 2 < NG:
                    max_w(g + 2)
                if g == 0:
                    mean_square(Tile(1))
                if g == 1:
                    dve.wait_ge(const_in, 16 * 13)
                    V.tensor_scalar(s_sink[:, 1:2], s_sink[:, 0:1], -1.0, None, ALU.mult)
                    V.tensor_scalar(nsink[:, :], sink[:, :], -1.0, None, ALU.mult)
                    V.memset(kwin[:, 0, 0:P], 0.0)
                    V.memset(vwin[:, 0, 0, :], 0.0)
                    V.memset(S_bd[:, :, :, :], 0.0).then_inc(init, 1)
                    norm_x(Tile(1))
                    scale_u(Tile(1))
                if g == 2:
                    take_kv(Tile(0))
                if g == 4:
                    take_gv(Tile(0))
                    take_kv(Tile(1))
                if g == 5:
                    take_gv(Tile(1))
            dve.wait_ge(w_lo_done, NG)
            dve.wait_ge(w_lo_pool, NG)
            V.memset(QE, 0.0).then_inc(init, 1)

            def body(t):
                nxt = t + 1
                early = t.static and t.off == 0
                if not early:
                    take_z(t)
                    row_max(t, 0)
                    row_max(t, 1)
                    sums(t)
                take_pt(t, 0)
                take_pt(t, 1)
                row_max(t, 2)
                row_max(t, 3)
                if early:
                    dve.wait_ge(init, 2)
                factors(t)
                take_pt(t, 2)
                if not early:
                    take_kv(nxt)
                take_pt(t, 3)
                assemble_leaves(t)
                denominators(t)
                assemble_levels(t)
                if not early:
                    take_gv(nxt)
                if not (t.static and t.off + 2 > NT):
                    mean_square(t + 2)
                gate_window(t)
                mean_heads(t)
                update_state(t)
                gate_gla(t)
                scale_rows(t)
                take_out(t, 0)
                take_out(t, 1)
                if not (t.static and t.off + 2 > NT):
                    norm_x(t + 2)
                if not (t.static and t.off + 2 > NT):
                    scale_u(t + 2)
                    split_u(t + 2)
                residual(t)
                final_norm(t)

            iterations(dve, body)
            t = Tile(NT - 1)
            take_z(t)
            row_max(t, 0)
            row_max(t, 1)
            sums(t)
            take_pt(t, 0)
            take_pt(t, 1)
            take_kv(S)
            row_max(t, 2)
            row_max(t, 3)
            take_gv(S)
            factors(t)
            take_pt(t, 2)
            take_pt(t, 3)
            s_take_z()
            assemble_leaves(t)
            denominators(t)
            assemble_levels(t)
            s_take_keys()
            s_queries()
            s_log_decay()
            s_window()
            gate_window(t)
            mean_heads(t)
            update_state(t)
            gate_gla(t)
            scale_rows(t)
            s_states(0)
            s_states(1)
            take_out(t, 0)
            take_out(t, 1)
            s_row_max()
            s_normalise()
            s_states(2)
            s_states(3)
            s_take_probs()
            s_gate_window()
            s_squares()
            residual(t, [0])
            s_gate_gla()
            s_split_out()
            residual(t, [1])
            final_norm(t)
            s_residual()
            s_final_norm()

        @block.gpsimd
        def _(pool):
            G = nc.gpsimd

            def lo_w(g):
                d = DVE_TILES[g]
                pool.wait_ge(w_hi_pool, g + 1)
                G.tensor_tensor(w_slice(g, w_lo, wo_lo)[:, d:DT], staged(g)[:, d:DT],
                                w_slice(g, w_hi, wo_hi)[:, d:DT], ALU.subtract).then_inc(w_lo_pool, 1)

            def differences(t):
                dve_g.wait(pool, "scan", t)
                b = lsum[:, :, :].rearrange("p f (b c) -> p (f b) c", c=LEAF)
                G.tensor_tensor(EX[:, S_LEAFQ].rearrange("p f (b c) -> p (f b) c", c=LEAF), b,
                                b[:, :, LEAF // 2 - 1:LEAF // 2].broadcast_to([P, FT * P // LEAF, LEAF]),
                                ALU.subtract).then_inc(pool_g.sem, 1)
                for l in range(DVE_LEVELS, len(LEVELS)):
                    late = level_differences(G, l)
                late.then_inc(pool_g.sem, 1)

            def gates_over_sums(t):
                dve_w.wait(pool, "rden", t)
                pj.wait_freed(pool, "sg", t)
                g = gates[:, 512:1024].rearrange("p (h c) -> p h c", h=8)
                G.tensor_tensor(g, g, bcast(wst[:, 5, :], 2, HD), ALU.mult).then_inc(pool_w.sem, 1)

            for g in range(NG):
                pool.wait_ge(w_row, g + 1)
                G.partition_all_reduce(wcol[:, 1:2], wcol[:, 0:1], P, bass.bass_isa.ReduceOp.max
                                       ).then_inc(w_max, 1)
                if g >= 1:
                    lo_w(g - 1)
            differences(Tile(0))
            lo_w(NG - 1)

            def body(t):
                if not (t.static and t.off == 0):
                    differences(t)
                gates_over_sums(t)

            iterations(pool, body)
            body(Tile(NT - 1))
            after(pool, "dve_am")
            G.partition_all_reduce(s_am[:, 1, :], s_am[:, 0, :], P, bass.bass_isa.ReduceOp.max
                                   ).then_inc(smp["pool"].sem, 1)


def _columns():
    import numpy as np
    heads = np.concatenate([np.arange(HD) + HD * (GRP * kv + f) for f in range(GRP) for kv in range(KVH)])
    gq, gk, gv, gg, low, sq, sk, sv, sg = np.split(
        np.arange(IN_W), np.cumsum([256, 256, 512, 512, 16, 512, 128, 128]))
    return [np.concatenate([gq, gk]), sq[heads], np.concatenate([sk, sv, low]), gv, gg, sg[heads]], heads


def kernel(**inputs):
    import numpy as np
    import ml_dtypes
    import concourse.bacc as _bacc
    from concourse.bass_utils import run_bass_kernel_spmd as _run

    a = {k: np.asarray(v) for k, v in inputs.items()}
    cols, heads = _columns()
    x, xs = a["x_prompt"][0], a["x_sample"][:, 0]
    w_in, w_out = a["w_in"][0], a["w_out"][0]
    w_out = np.concatenate([w_out[:512], w_out[512 + heads]])
    rows = lambda w: w.reshape(DT, P, -1).transpose(1, 0, 2).reshape(P, -1)
    half = D // OUT_GROUPS
    w_all = np.concatenate([rows(w_in[:, c]) for c in cols]
                           + [rows(w_out[:, g * half:g * half + half]) for g in range(OUT_GROUPS)], axis=1)
    head_of = np.array([GRP * kv + f for f in range(GRP) for kv in range(KVH)])
    tok = np.arange(P)
    same = tok[:, None] // LEAF == tok[None, :] // LEAF
    leaf = (same & (tok[:, None] <= tok[None, :])).astype(np.float32)
    lvl = np.zeros((P, len(LEVELS), P // 2), np.float32)
    for i, s in enumerate(LEVELS):
        pair = np.arange(P // 2) // s
        lvl[:, i] = (tok[:, None] // (2 * s) == pair[None, :]) & (tok[:, None] % (2 * s) < s)
    scan = np.ones((P, 2, P), np.float32)
    scan[:, 1, ::LEAF] = 0.0
    newer = tok[None, :] <= tok[:, None]
    band = np.stack([np.zeros((P, P)), np.where(newer, 0.0, -1e30)], 1)
    window = np.stack([~newer.T, newer.T], 1).astype(np.float32)
    arrays = {
        "xT": x.reshape(NT, P, DT, P).transpose(0, 3, 2, 1),
        "xq": x.reshape(NT, P, D),
        "xsT": xs.reshape(NS, DT, P).transpose(2, 1, 0),
        "xs": xs,
        "w": w_all,
        "gin": a["norm_in"][0].reshape(DT, P).T,
        "gout": np.concatenate([np.repeat(a["gla_norm"][0][:, None], HG, 1), np.ones((P, HG), np.float32)], 1),
        "wgu": a["w_gate_up"][0],
        "bg": a["b_gate"][0].reshape(FT, P).T,
        "sink": np.broadcast_to(a["attn_sinks"][0][head_of], (P, 8)),
        "normf": np.broadcast_to(a["norm_f"], (P, D)),
        "normfT": a["norm_f"].reshape(DT, P).T,
        "state": a["state_gla"][0].reshape(NS, FT, 2, DK, DV).transpose(2, 3, 0, 1, 4).reshape(P, NS, FT, DV),
        "kcT": np.roll(a["cache_win_k"][0], -1, axis=1).transpose(2, 3, 0, 1).reshape(P, NS, P),
        "vc": a["cache_win_v"][0].transpose(1, 0, 2, 3).reshape(P, NS, P)[1:],
        "sinks_s": a["attn_sinks"][0][:, None],
        "ident": np.eye(P, dtype=np.float32),
        "tri": leaf,
        "lvl": lvl,
        "leafscan": scan,
        "band": band.astype(ml_dtypes.bfloat16),
        "older": (~newer).astype(np.float32),
        "window": window,
    }
    outs = [("y", (NT, P, D)), ("ys", (P, DT, NS)), ("Sp", (HG, DK, DV)), ("kp", (KVH, HD, P)), ("vp", (P, P)),
            ("Ss", (P, NS, FT, DV)), ("ksT", (P, NS, P)), ("vs", (P, NS, P))]
    nc = _bacc.Bacc("TRN2", target_bir_lowering=False, num_devices=1)
    maps, args = {}, []
    for name, v in arrays.items():
        v = np.ascontiguousarray(v)
        maps[f"in_{name}"] = v
        args.append(nc.dram_tensor(f"in_{name}", v.shape, mybir.dt.from_np(v.dtype), kind="ExternalInput").ap())
    for name, shape in outs:
        args.append(nc.dram_tensor(f"out_{name}", shape, F32, kind="ExternalOutput").ap())
    hymba_step_kernel(nc, *args)
    res = _run(nc, [maps], core_ids=[0]).results[0]
    y, ys, Sp, kp, vp, Ss, ksT, vs = (np.asarray(res[f"out_{name}"]) for name, _ in outs)
    return (y.reshape(1, SEQ, D),
            ys.transpose(2, 1, 0).reshape(NS, 1, D),
            Sp.reshape(1, 1, HG, DK, DV),
            kp.transpose(2, 0, 1).reshape(1, 1, P, KVH, HD),
            vp.reshape(1, 1, P, KVH, HD),
            Ss.reshape(2, DK, NS, FT, DV).transpose(2, 3, 0, 1, 4).reshape(1, NS, HG, DK, DV),
            ksT.reshape(KVH, HD, NS, P).transpose(2, 3, 0, 1)[None],
            vs.reshape(P, NS, KVH, HD).transpose(1, 0, 2, 3)[None])
```
